# Optimizing a Trainium2 kernel written in Bass

```python
import math
import jax
import jax.numpy as jnp
from jax import lax
import numpy as np

D_MODEL = 1024
BATCH = 1
SEQ = 512
DEPTH = 2

CHUNK = 64
MEM_LEN = 256
EPS = 1e-6

SC_DIM = 512
SC_WIDTH = 3
SSM_HEADS = 16
SSM_HEAD_DIM = 64
SSM_INNER = SSM_HEADS * SSM_HEAD_DIM
SSM_GROUPS = 2
SSM_STATE = 128
SSM_CONV = 4
SSM_CONV_DIM = SSM_INNER + 2 * SSM_GROUPS * SSM_STATE
GDN_HEADS = 8
GDN_DK = 128
GDN_DV = 128
GDN_CONV = 4
GDN_QK = GDN_HEADS * GDN_DK
GDN_V = GDN_HEADS * GDN_DV
SB_HEADS = 8
SB_HEAD_DIM = 64
SB_DIM = SB_HEADS * SB_HEAD_DIM
SB_BLOCK = 128
XA_HEADS = 4
XA_HEAD_DIM = D_MODEL // XA_HEADS
MOE_GROUPS = 4
MOE_EXPERTS_PER_GROUP = 8
MOE_EXPERTS = MOE_GROUPS * MOE_EXPERTS_PER_GROUP
MOE_TOPK = 2
MOE_FF = 512
MOE_BLOCK = 128

EVEN_SPLITS = (SC_DIM, 2 * SC_DIM, 3 * SC_DIM, 3 * SC_DIM + SSM_INNER, 3 * SC_DIM + SSM_INNER + SSM_CONV_DIM)
EVEN_IN = 3 * SC_DIM + SSM_INNER + SSM_CONV_DIM + SSM_HEADS
EVEN_MIX = SC_DIM + SSM_INNER
GDN_QKV = 2 * GDN_QK + GDN_V
ODD_SPLITS = (GDN_QKV, GDN_QKV + GDN_V, GDN_QKV + GDN_V + GDN_HEADS, GDN_QKV + GDN_V + 2 * GDN_HEADS, GDN_QKV + GDN_V + 2 * GDN_HEADS + SB_DIM, GDN_QKV + GDN_V + 2 * GDN_HEADS + 2 * SB_DIM)
ODD_IN = GDN_QKV + GDN_V + 2 * GDN_HEADS + 3 * SB_DIM
ODD_MIX = GDN_V + SB_DIM

kernel_name = 'hybrid_conv_ssd_deltanet_stickbreak_hmoe'

def rmsnorm(x, g):
    xf = x.astype(jnp.float32)
    y = xf * lax.rsqrt(jnp.mean(xf * xf, axis=-1, keepdims=True) + EPS)
    return (y * g.astype(jnp.float32)).astype(x.dtype)

def l2norm(x):
    return x * lax.rsqrt(jnp.sum(x * x, axis=-1, keepdims=True) + EPS)

def causal_dwconv(x, w):
    width = w.shape[0]
    length = x.shape[1]
    xp = jnp.pad(x, ((0, 0), (width - 1, 0), (0, 0)))
    return sum(xp[:, j:j + length] * w[j] for j in range(width))

def short_conv_mixer(b_gate, c_gate, x_in, w_conv):
    return b_gate * causal_dwconv(c_gate * x_in, w_conv)

def ssd_mixer(z, xbc, dt, conv_w, conv_b, dt_bias, a_log, d_skip, norm_w):
    f32 = jnp.float32
    bsz, length, _ = z.shape
    nc = length // CHUNK
    hpg = SSM_HEADS // SSM_GROUPS
    xbc = jax.nn.silu(causal_dwconv(xbc, conv_w) + conv_b).astype(f32)
    xs, bm, cm = jnp.split(xbc, (SSM_INNER, SSM_INNER + SSM_GROUPS * SSM_STATE), axis=-1)
    xs = xs.reshape(bsz, nc, CHUNK, SSM_GROUPS, hpg, SSM_HEAD_DIM)
    bm = bm.reshape(bsz, nc, CHUNK, SSM_GROUPS, SSM_STATE)
    cm = cm.reshape(bsz, nc, CHUNK, SSM_GROUPS, SSM_STATE)
    dt = jax.nn.softplus(dt.astype(f32) + dt_bias.astype(f32)).reshape(bsz, nc, CHUNK, SSM_GROUPS, hpg)
    a = -jnp.exp(a_log.astype(f32)).reshape(SSM_GROUPS, hpg)
    a_cs = jnp.cumsum(dt * a, axis=2)
    causal = jnp.tril(jnp.ones((CHUNK, CHUNK), dtype=bool))
    seg = a_cs[:, :, :, None] - a_cs[:, :, None, :]
    decay = jnp.exp(jnp.where(causal[:, :, None, None], seg, -jnp.inf))
    xdt = xs * dt[..., None]
    cb = jnp.einsum('bctgn,bcsgn->bctsg', cm, bm)
    y_diag = jnp.einsum('bctsgh,bcsghp->bctghp', cb[..., None] * decay, xdt)
    to_end = jnp.exp(a_cs[:, :, -1:] - a_cs)
    states = jnp.einsum('bcsgn,bcsghp->bcghpn', bm, xdt * to_end[..., None])
    chunk_decay = jnp.exp(a_cs[:, :, -1])

    def step(s, inp):
        st, dec = inp
        return s * dec[..., None, None] + st, s

    s0 = jnp.zeros((bsz, SSM_GROUPS, hpg, SSM_HEAD_DIM, SSM_STATE), f32)
    _, prev = lax.scan(step, s0, (jnp.moveaxis(states, 1, 0), jnp.moveaxis(chunk_decay, 1, 0)))
    prev = jnp.moveaxis(prev, 0, 1)
    y_off = jnp.einsum('bctgn,bcghpn->bctghp', cm, prev) * jnp.exp(a_cs)[..., None]
    y = y_diag + y_off + xs * d_skip.astype(f32).reshape(SSM_GROUPS, hpg, 1)
    y = y.reshape(bsz, length, SSM_INNER) * jax.nn.silu(z.astype(f32))
    yg = y.reshape(bsz, length, SSM_GROUPS, SSM_INNER // SSM_GROUPS)
    yg = yg * lax.rsqrt(jnp.mean(yg * yg, axis=-1, keepdims=True) + EPS)
    return yg.reshape(bsz, length, SSM_INNER) * norm_w.astype(f32)

def gated_deltanet_mixer(qkv, z, a, b, conv_w, dt_bias, a_log, norm_w):
    f32 = jnp.float32
    bsz, length, _ = qkv.shape
    nc = length // CHUNK
    qkv = jax.nn.silu(causal_dwconv(qkv, conv_w)).astype(f32)
    q, k, v = jnp.split(qkv, (GDN_QK, 2 * GDN_QK), axis=-1)

    def to_chunks(t, d):
        return t.reshape(bsz, nc, CHUNK, GDN_HEADS, d).transpose(0, 3, 1, 2, 4)

    q = to_chunks(l2norm(q.reshape(bsz, length, GDN_HEADS, GDN_DK)) * GDN_DK ** -0.5, GDN_DK)
    k = to_chunks(l2norm(k.reshape(bsz, length, GDN_HEADS, GDN_DK)), GDN_DK)
    v = to_chunks(v, GDN_DV)
    beta = jax.nn.sigmoid(b.astype(f32)).reshape(bsz, nc, CHUNK, GDN_HEADS).transpose(0, 3, 1, 2)
    g = -jnp.exp(a_log.astype(f32)) * jax.nn.softplus(a.astype(f32) + dt_bias.astype(f32))
    g = g.reshape(bsz, nc, CHUNK, GDN_HEADS).transpose(0, 3, 1, 2)
    gc = jnp.cumsum(g, axis=-1)
    incl = jnp.tril(jnp.ones((CHUNK, CHUNK), dtype=bool))
    strict = jnp.tril(jnp.ones((CHUNK, CHUNK), f32), -1)
    decay = jnp.exp(jnp.where(incl, gc[..., :, None] - gc[..., None, :], -jnp.inf))
    kb = k * beta[..., None]
    lower = jnp.einsum('bhctd,bhcsd->bhcts', kb, k) * decay * strict
    rhs = jnp.concatenate([v * beta[..., None], kb * jnp.exp(gc)[..., None]], axis=-1)
    sol = lax.linalg.triangular_solve(lower + jnp.eye(CHUNK, dtype=f32), rhs,
                                      left_side=True, lower=True, unit_diagonal=True)
    u, w = jnp.split(sol, (GDN_DV,), axis=-1)
    a_qk = jnp.einsum('bhctd,bhcsd->bhcts', q, k) * decay
    q_dec = q * jnp.exp(gc)[..., None]
    k_dec = k * jnp.exp(gc[..., -1:] - gc)[..., None]
    chunk_decay = jnp.exp(gc[..., -1])

    def step(s, inp):
        qd, kd, uc, wc, aqk, dec = inp
        v_new = uc - jnp.einsum('bhld,bhdv->bhlv', wc, s)
        o = jnp.einsum('bhld,bhdv->bhlv', qd, s) + jnp.einsum('bhts,bhsv->bhtv', aqk, v_new)
        s = s * dec[..., None, None] + jnp.einsum('bhld,bhlv->bhdv', kd, v_new)
        return s, o

    s0 = jnp.zeros((bsz, GDN_HEADS, GDN_DK, GDN_DV), f32)
    seq_in = (q_dec, k_dec, u, w, a_qk, chunk_decay)
    _, o = lax.scan(step, s0, (jnp.moveaxis(seq_in[0], 2, 0), jnp.moveaxis(seq_in[1], 2, 0),
                               jnp.moveaxis(seq_in[2], 2, 0), jnp.moveaxis(seq_in[3], 2, 0),
                               jnp.moveaxis(seq_in[4], 2, 0), jnp.moveaxis(seq_in[5], 2, 0)))
    o = o.transpose(1, 0, 3, 2, 4).reshape(bsz, length, GDN_HEADS, GDN_DV)
    o = o * lax.rsqrt(jnp.mean(o * o, axis=-1, keepdims=True) + EPS) * norm_w.astype(f32)
    o = o * jax.nn.silu(z.astype(f32).reshape(bsz, length, GDN_HEADS, GDN_DV))
    return o.reshape(bsz, length, GDN_V)

def stick_breaking_mixer(q, k, v):
    bsz, length, _ = q.shape
    nb = length // SB_BLOCK

    def heads(t):
        return t.reshape(bsz, length, SB_HEADS, SB_HEAD_DIM).transpose(0, 2, 1, 3)

    q, k, v = heads(q), heads(k), heads(v)
    q_blocks = q.reshape(bsz, SB_HEADS, nb, SB_BLOCK, SB_HEAD_DIM).transpose(2, 0, 1, 3, 4)
    k_pos = jnp.arange(length)
    scale = SB_HEAD_DIM ** -0.5

    def block(args):
        qb, blk = args
        logits = jnp.einsum('bhqd,bhkd->bhqk', qb, k).astype(jnp.float32) * scale
        q_pos = blk * SB_BLOCK + jnp.arange(SB_BLOCK)
        earlier = k_pos[None, :] < q_pos[:, None]
        log_keep = jnp.where(earlier, jax.nn.log_sigmoid(-logits), 0.0)
        log_between = lax.cumsum(log_keep, axis=3, reverse=True) - log_keep
        log_w = jnp.where(earlier, jax.nn.log_sigmoid(logits) + log_between, -jnp.inf)
        return jnp.einsum('bhqk,bhkd->bhqd', jnp.exp(log_w).astype(v.dtype), v)

    out = lax.map(block, (q_blocks, jnp.arange(nb)))
    return out.transpose(1, 0, 3, 2, 4).reshape(bsz, length, SB_DIM)

def memory_cross_attention(h, memn, wq, wk, wv, wo):
    bsz, length, _ = h.shape
    m = memn.shape[1]
    q = (h @ wq).reshape(bsz, length, XA_HEADS, XA_HEAD_DIM)
    k = (memn @ wk).reshape(bsz, m, XA_HEADS, XA_HEAD_DIM)
    v = (memn @ wv).reshape(bsz, m, XA_HEADS, XA_HEAD_DIM)
    s = jnp.einsum('blhd,bmhd->bhlm', q, k).astype(jnp.float32) * XA_HEAD_DIM ** -0.5
    p = jax.nn.softmax(s, axis=-1).astype(v.dtype)
    o = jnp.einsum('bhlm,bmhd->blhd', p, v).reshape(bsz, length, D_MODEL)
    return o @ wo

def hierarchical_moe(x, w_group, b_group, w_expert, b_expert, w_gate, w_up, w_down):
    f32 = jnp.float32
    bsz, length, d = x.shape
    n_tok = bsz * length
    xf = x.reshape(n_tok, d)
    g_prob = jax.nn.softmax((xf @ w_group).astype(f32) + b_group.astype(f32), axis=-1)
    g_sel = jnp.argmax(g_prob, axis=-1)
    g_w = jnp.take_along_axis(g_prob, g_sel[:, None], axis=-1)
    e_logits = ((xf @ w_expert).astype(f32) + b_expert.astype(f32)).reshape(n_tok, MOE_GROUPS, MOE_EXPERTS_PER_GROUP)
    e_logits = jnp.take_along_axis(e_logits, g_sel[:, None, None], axis=1)[:, 0]
    top_p, top_i = lax.top_k(jax.nn.softmax(e_logits, axis=-1), MOE_TOPK)
    gate = g_w * top_p / jnp.sum(top_p, axis=-1, keepdims=True)
    eid = (g_sel[:, None] * MOE_EXPERTS_PER_GROUP + top_i).reshape(-1).astype(jnp.int32)
    tok = jnp.repeat(jnp.arange(n_tok, dtype=jnp.int32), MOE_TOPK)
    gw = gate.reshape(-1)
    n_assign = n_tok * MOE_TOPK
    order = jnp.argsort(eid)
    s_eid, s_tok, s_w = eid[order], tok[order], gw[order]
    counts = jax.ops.segment_sum(jnp.ones_like(eid), eid, num_segments=MOE_EXPERTS)
    starts = jnp.cumsum(counts) - counts
    padded = (counts + MOE_BLOCK - 1) // MOE_BLOCK * MOE_BLOCK
    pad_end = jnp.cumsum(padded)
    pad_start = pad_end - padded
    dest = pad_start[s_eid] + jnp.arange(n_assign, dtype=jnp.int32) - starts[s_eid]
    n_blocks = -(-(n_assign + MOE_EXPERTS * (MOE_BLOCK - 1)) // MOE_BLOCK)
    n_slots = n_blocks * MOE_BLOCK
    slot_tok = jnp.full((n_slots,), n_tok, jnp.int32).at[dest].set(s_tok)
    slot_w = jnp.zeros((n_slots,), f32).at[dest].set(s_w)
    block_eid = jnp.minimum(jnp.searchsorted(pad_end, jnp.arange(n_blocks, dtype=jnp.int32) * MOE_BLOCK, side='right'),
                            MOE_EXPERTS - 1)
    x_pad = jnp.concatenate([xf, jnp.zeros((1, d), xf.dtype)], axis=0)
    xs = x_pad[slot_tok].reshape(n_blocks, MOE_BLOCK, d)

    def expert_block(args):
        xb, e = args
        return (jax.nn.silu(xb @ w_gate[e]) * (xb @ w_up[e])) @ w_down[e]

    ys = lax.map(expert_block, (xs, block_eid)).reshape(n_slots, d)
    y = jnp.zeros((n_tok + 1, d), f32).at[slot_tok].add(ys.astype(f32) * slot_w[:, None])[:n_tok]
    return y.reshape(bsz, length, d).astype(x.dtype)

def even_mixer(u, w_in, sc_conv, ssm_conv_w, ssm_conv_b, ssm_dt_bias, ssm_a_log, ssm_d, ssm_norm, w_out):
    sc_b, sc_c, sc_x, z, xbc, dt = jnp.split(u @ w_in, EVEN_SPLITS, axis=-1)
    y_a = short_conv_mixer(sc_b, sc_c, sc_x, sc_conv)
    y_b = ssd_mixer(z, xbc, dt, ssm_conv_w, ssm_conv_b, ssm_dt_bias, ssm_a_log, ssm_d, ssm_norm).astype(u.dtype)
    return jnp.concatenate([y_a, y_b], axis=-1) @ w_out

def odd_mixer(u, w_in, gdn_conv, gdn_dt_bias, gdn_a_log, gdn_norm, w_out):
    qkv, z, a, b, sq, sk, sv = jnp.split(u @ w_in, ODD_SPLITS, axis=-1)
    y_c = gated_deltanet_mixer(qkv, z, a, b, gdn_conv, gdn_dt_bias, gdn_a_log, gdn_norm).astype(u.dtype)
    y_d = stick_breaking_mixer(sq, sk, sv).astype(u.dtype)
    return jnp.concatenate([y_c, y_d], axis=-1) @ w_out

def setup_inputs(seed: int = 0) -> dict:
    key = jax.random.key(seed)
    keys = iter(jax.random.split(key, 48))
    f32 = jnp.float32
    n_even = (DEPTH + 1) // 2
    n_odd = DEPTH // 2

    def normal(shape, scale):
        return jax.random.normal(next(keys), shape, f32) * scale

    def gain(shape):
        return 1.0 + normal(shape, 0.05)

    def dt_bias(shape):
        dt = jnp.exp(jax.random.uniform(next(keys), shape, f32, math.log(1e-3), math.log(1e-1)))
        return dt + jnp.log(-jnp.expm1(-dt))

    def a_log(shape):
        return jnp.log(jax.random.uniform(next(keys), shape, f32, 1.0, 16.0))

    sd = D_MODEL ** -0.5
    return {
        'x': normal((BATCH, SEQ, D_MODEL), 1.0),
        'mem': normal((BATCH, MEM_LEN, D_MODEL), 1.0),
        'mem_norm': gain((D_MODEL,)),
        'final_norm': gain((D_MODEL,)),
        'norm_mix': gain((DEPTH, D_MODEL)),
        'norm_xa': gain((DEPTH, D_MODEL)),
        'norm_ffn': gain((DEPTH, D_MODEL)),
        'xa_wq': normal((DEPTH, D_MODEL, D_MODEL), sd),
        'xa_wk': normal((DEPTH, D_MODEL, D_MODEL), sd),
        'xa_wv': normal((DEPTH, D_MODEL, D_MODEL), sd),
        'xa_wo': normal((DEPTH, D_MODEL, D_MODEL), sd),
        'moe_w_group': normal((DEPTH, D_MODEL, MOE_GROUPS), sd),
        'moe_b_group': normal((DEPTH, MOE_GROUPS), 0.01),
        'moe_w_expert': normal((DEPTH, D_MODEL, MOE_EXPERTS), sd),
        'moe_b_expert': normal((DEPTH, MOE_EXPERTS), 0.01),
        'moe_w_gate': normal((DEPTH, MOE_EXPERTS, D_MODEL, MOE_FF), sd),
        'moe_w_up': normal((DEPTH, MOE_EXPERTS, D_MODEL, MOE_FF), sd),
        'moe_w_down': normal((DEPTH, MOE_EXPERTS, MOE_FF, D_MODEL), MOE_FF ** -0.5),
        'ev_w_in': normal((n_even, D_MODEL, EVEN_IN), sd),
        'ev_sc_conv': normal((n_even, SC_WIDTH, SC_DIM), SC_WIDTH ** -0.5),
        'ev_ssm_conv_w': normal((n_even, SSM_CONV, SSM_CONV_DIM), SSM_CONV ** -0.5),
        'ev_ssm_conv_b': normal((n_even, SSM_CONV_DIM), 0.02),
        'ev_ssm_dt_bias': dt_bias((n_even, SSM_HEADS)),
        'ev_ssm_a_log': a_log((n_even, SSM_HEADS)),
        'ev_ssm_d': gain((n_even, SSM_HEADS)),
        'ev_ssm_norm': gain((n_even, SSM_INNER)),
        'ev_w_out': normal((n_even, EVEN_MIX, D_MODEL), EVEN_MIX ** -0.5),
        'od_w_in': normal((n_odd, D_MODEL, ODD_IN), sd),
        'od_gdn_conv': normal((n_odd, GDN_CONV, GDN_QKV), GDN_CONV ** -0.5),
        'od_gdn_dt_bias': dt_bias((n_odd, GDN_HEADS)),
        'od_gdn_a_log': a_log((n_odd, GDN_HEADS)),
        'od_gdn_norm': gain((n_odd, GDN_DV)),
        'od_w_out': normal((n_odd, ODD_MIX, D_MODEL), ODD_MIX ** -0.5),
    }

def reference(x, mem, mem_norm, final_norm, norm_mix, norm_xa, norm_ffn,
              xa_wq, xa_wk, xa_wv, xa_wo,
              moe_w_group, moe_b_group, moe_w_expert, moe_b_expert, moe_w_gate, moe_w_up, moe_w_down,
              ev_w_in, ev_sc_conv, ev_ssm_conv_w, ev_ssm_conv_b, ev_ssm_dt_bias, ev_ssm_a_log, ev_ssm_d,
              ev_ssm_norm, ev_w_out,
              od_w_in, od_gdn_conv, od_gdn_dt_bias, od_gdn_a_log, od_gdn_norm, od_w_out):
    memn = rmsnorm(mem, mem_norm)
    h = x
    for layer in range(DEPTH):
        i = layer // 2
        u = rmsnorm(h, norm_mix[layer])
        if layer % 2 == 0:
            mix = even_mixer(u, ev_w_in[i], ev_sc_conv[i], ev_ssm_conv_w[i], ev_ssm_conv_b[i],
                             ev_ssm_dt_bias[i], ev_ssm_a_log[i], ev_ssm_d[i], ev_ssm_norm[i], ev_w_out[i])
        else:
            mix = odd_mixer(u, od_w_in[i], od_gdn_conv[i], od_gdn_dt_bias[i], od_gdn_a_log[i],
                            od_gdn_norm[i], od_w_out[i])
        h = h + mix.astype(h.dtype)
        h = h + memory_cross_attention(rmsnorm(h, norm_xa[layer]), memn, xa_wq[layer], xa_wk[layer],
                                       xa_wv[layer], xa_wo[layer]).astype(h.dtype)
        h = h + hierarchical_moe(rmsnorm(h, norm_ffn[layer]), moe_w_group[layer], moe_b_group[layer],
                                 moe_w_expert[layer], moe_b_expert[layer], moe_w_gate[layer],
                                 moe_w_up[layer], moe_w_down[layer])
    return rmsnorm(h, final_norm)


_drawn_inputs = setup_inputs


def setup_inputs(seed=0):
    import zlib

    import numpy as np

    out = dict(_drawn_inputs(seed))
    spreads = {}
    factors = {'mem_norm': 2.685,
     'norm_xa': 3.167,
     'moe_b_group': 10.314,
     'moe_b_expert': 4.017,
     'od_gdn_norm': 2.752}
    for name, (base, spread) in spreads.items():
        noise = np.random.default_rng([zlib.crc32(name.encode()), seed]).standard_normal(out[name].shape)
        drawn = base * np.exp(spread * noise) if base else spread * noise
        out[name] = jnp.asarray(drawn.astype(out[name].dtype))
    for name, factor in factors.items():
        out[name] = (out[name] * factor).astype(out[name].dtype)
    return out
```

```python
from contextlib import ExitStack

import numpy as np
import concourse.bass as bass
from concourse import mybir

F32, I32 = mybir.dt.float32, mybir.dt.int32
ALU = mybir.AluOpType
ACT = mybir.ActivationFunctionType
AX = mybir.AxisListType

P = 128
D = 1024
KD = D // P
SEQ = 512
NT = SEQ // P
MEM = 256
NM = MEM // P
EPS = 1e-6
SC = 512
SSM_H, SSM_P, SSM_G, SSM_N = 16, 64, 2, 128
SSM_INNER = SSM_H * SSM_P
XBC = SSM_INNER + 2 * SSM_G * SSM_N
GH, GDK = 8, 128
SBH, SBD = 8, 64
XH = 4
NE, NG, EPG = 32, 4, 8
FF = 512
CAP = 64
NPASS = SEQ // CAP
PAIRS = NE // 2
WSLOTS = 6
BLK = 4096
MIXT = 12
LEVELS = 7


def constant_columns():
    r = np.arange(P)
    a, b = r[:, None], r[None, :]
    cols = {
        "ident": a == b,
        "upper": a <= b,
        "lower": a >= b,
        "slower": a > b,
        "supper": a < b,
        "ones": np.ones((P, P)),
    }
    below = []
    for l in range(LEVELS):
        s = 1 << l
        m = (a // (2 * s) == b // (2 * s)) & ((a // s) % 2 == 1) & ((b // s) % 2 == 0)
        below.append(m)
    cols["below0"] = below[0]
    cols["belowT"] = np.concatenate([m.T for m in below[1:]], 1)
    cols["iota"] = np.broadcast_to(np.arange(CAP), (P, CAP))
    cols["prio"] = np.broadcast_to(EPG - np.arange(EPG), (P, EPG))
    cols["limits"] = np.broadcast_to(CAP * np.arange(1, NPASS), (P, NPASS - 1))
    return pack(cols)


def pack(cols):
    at, parts, where = 0, [], {}
    for name, c in cols.items():
        c = np.ascontiguousarray(c, dtype=np.float32)
        where[name] = (at, c.shape[1])
        at += c.shape[1]
        parts.append(c)
    return np.concatenate(parts, 1), where


def feature_major(v):
    v = np.asarray(v)
    v = v.reshape(-1, v.shape[-1] // P, P)
    return v.transpose(2, 1, 0).reshape(P, -1)


def on_every_row(v):
    v = np.asarray(v).reshape(1, -1)
    return np.broadcast_to(v, (P, v.shape[1]))


def weight_tiles(w):
    w = np.asarray(w)
    return w.reshape(KD, P, -1).transpose(1, 0, 2).reshape(P, -1)


def small_columns(i):
    cols = {"g_mem": feature_major(i["mem_norm"])}
    for l in range(2):
        cols[f"g_mix{l}"] = feature_major(i["norm_mix"][l])
        cols[f"g_xa{l}"] = feature_major(i["norm_xa"][l])
        cols[f"g_ffn{l}"] = feature_major(i["norm_ffn"][l])
        cols[f"w_route{l}"] = weight_tiles(np.concatenate([i["moe_w_group"][l], i["moe_w_expert"][l]], 1))
        cols[f"b_route{l}"] = on_every_row(np.concatenate([i["moe_b_group"][l], i["moe_b_expert"][l]]))
    dt0 = 3 * SC + SSM_INNER + XBC
    cols["w_dt"] = weight_tiles(i["ev_w_in"][0][:, dt0:dt0 + SSM_H])
    ab0 = 4 * GH * GDK
    cols["w_ab"] = weight_tiles(i["od_w_in"][0][:, ab0:ab0 + 2 * GH])
    cols["sc_conv"] = feature_major(i["ev_sc_conv"][0])
    cols["ssm_conv"] = feature_major(i["ev_ssm_conv_w"][0])
    cols["ssm_convb"] = feature_major(i["ev_ssm_conv_b"][0])
    cols["gdn_conv"] = feature_major(i["od_gdn_conv"][0])
    cols["ssm_norm"] = feature_major(i["ev_ssm_norm"][0])
    cols["gdn_norm"] = feature_major(i["od_gdn_norm"][0])
    cols["dt_bias"] = on_every_row(i["ev_ssm_dt_bias"][0])
    cols["a_log"] = on_every_row(i["ev_ssm_a_log"][0])
    cols["d_skip"] = on_every_row(i["ev_ssm_d"][0])
    cols["gdn_dtb"] = on_every_row(i["od_gdn_dt_bias"][0])
    cols["gdn_alog"] = on_every_row(i["od_gdn_a_log"][0])
    return pack(cols)


class Ring:

    def __init__(self, banks, full, free):
        self.banks, self.full, self.free = banks, full, free
        self.filled = self.emptied = 0

    def fill(self):
        n = self.filled
        self.filled += 1
        return self.banks[n % len(self.banks)], n + 1

    def empty(self):
        n = self.emptied
        self.emptied += 1
        return self.banks[n % len(self.banks)], n + 1

    def all(self):
        return self.stored(self.filled)

    def stored(self, n):
        return n + len(self.banks)


class Links:

    def __init__(self, eng, sem):
        self.eng, self.sem, self.n = eng, sem, 0

    def __call__(self, ins):
        self.n = self.n + 1
        ins.then_inc(self.sem, 1)
        self.eng.wait_ge(self.sem, self.n)
        return ins


class Weights:

    def __init__(self, slots, full, free):
        self.slots, self.full, self.free = slots, full, free
        self.loaded = self.taken = self.owed = 0

    def first(self, mm):
        if self.owed:
            mm.then_inc(self.free, self.owed)
            self.owed = 0

    def load(self):
        n = self.loaded
        self.loaded += 1
        return self.slots[n % WSLOTS], self.full[n % WSLOTS], n + 1

    def take(self):
        n = self.taken
        self.taken += 1
        return self.slots[n % WSLOTS], self.full[n % WSLOTS], 16 * (n // WSLOTS + 1)


class Core:

    def __init__(self, nc, ctx, aps, consts, small):
        self.nc, self.ctx, self.dram = nc, ctx, aps
        self.reserved, self.sems = {}, {}
        sb = lambda name, n, dt=F32: ctx.enter_context(nc.sbuf_tensor(name, [P, n], dt))
        self.wring = sb("weights", WSLOTS * BLK)
        self.h = sb("h", NT * D)[:, :].rearrange("p (i d) -> p i d", i=NT)
        self.constbuf = sb("consts", consts[0].shape[1])
        self.smallbuf = sb("small", small[0].shape[1])
        self.arena = sb("arena", 20992)
        self.cwhere, self.swhere = consts[1], small[1]
        banks = [ctx.enter_context(nc.psum_tensor(f"bank{i}", [P, 512], F32)) for i in range(8)]
        self.banks = [b[:, :] for b in banks]
        self.A = Ring(self.banks[:4], self.sem("act_bank_full"), self.sem("act_bank_free"))
        self.R = Ring(self.banks[4:], self.sem("dve_bank_full"), self.sem("dve_bank_free"))
        slots = [self.wring[:, i * BLK:(i + 1) * BLK] for i in range(WSLOTS)]
        self.W = Weights(slots, [self.sem(f"weights_full{i}") for i in range(WSLOTS)], self.sem("weights_free"))
        self.stage_ends = self.sem("stage_ends")

    def sem(self, name):
        if name not in self.sems:
            self.sems[name] = self.ctx.enter_context(self.nc.semaphore(name))
        return self.sems[name]

    def reserve(self, name, n):
        base = self.reserved.get(name, 0)
        self.reserved[name] = base + n
        return self.sem(name), base

    def c(self, name):
        at, n = self.cwhere[name]
        return self.constbuf[:, at:at + n]

    def s(self, name):
        at, n = self.swhere[name]
        return self.smallbuf[:, at:at + n]

    def at(self, off, n, **dims):
        v = self.arena[:, off:off + n]
        if dims:
            names = list(dims)
            v = v.rearrange(f"p ({' '.join(names)} x) -> p {' '.join(names)} x", **dims)
        return v


def spread(ap, n):
    return ap.unsqueeze(len(ap.shape)).broadcast_to([*ap.shape, n])


UT0 = 0
JUNK0, HN0 = 17408, 18432


class Norm:

    def __init__(self, k, src, n, gain, dst, keep=None, ready=None):
        self.k, self.src, self.n, self.gain, self.dst, self.keep, self.ready = k, src, n, gain, dst, keep, ready
        self.sq, self.sq0 = k.reserve("norm_sums", n)
        self.ms, self.ms0 = k.reserve("norm_means", 1)
        self.rt, self.rt0 = k.reserve("norm_roots", 1)
        self.hn, self.hn0 = k.reserve("norm_rows", n)
        self.junk = k.at(JUNK0, D)
        self.stat = k.stat

    def rows(self, i):
        return self.keep[:, i, :] if self.keep is not None else self.k.at(HN0, 2 * D, i=2)[:, i % 2, :]

    def act(self, act):
        k = self.k
        if self.ready:
            act.wait_ge(*self.ready)
        for i in range(self.n):
            if i:
                act.wait_ge(self.sq, self.sq0 + i)
            act.activation(self.junk, self.src(i), ACT.Square, accum_out=self.stat[:, i:i + 1]).then_inc(self.sq, 1)
        act.wait_ge(self.ms, self.ms0 + 1)
        act.activation(self.stat[:, 8:8 + self.n], self.stat[:, 4:4 + self.n], ACT.Sqrt).then_inc(self.rt, 1)

    def dve(self, dve):
        k = self.k
        n = self.n
        if self.ready:
            dve.wait_ge(*self.ready)
        dve.wait_ge(self.sq, self.sq0 + n)
        dve.tensor_scalar(self.stat[:, 4:4 + n], self.stat[:, 0:n], 1.0 / D, EPS, ALU.mult,
                          ALU.add).then_inc(self.ms, 1)
        dve.wait_ge(self.rt, self.rt0 + 1)
        k.dlink(dve.reciprocal(self.stat[:, 12:12 + n], self.stat[:, 8:8 + n]))

        def scale(i):
            dve.tensor_scalar(self.rows(i), self.src(i), self.stat[:, 12 + i:13 + i], None,
                              ALU.mult).then_inc(self.hn, 1)

        scale(0)
        scale(1)
        for i in range(n):
            for half in range(2):
                bank, full = k.R.empty()
                dve.wait_ge(k.R.full, full)
                dve.tensor_tensor(
                    self.dst[:, 4 * half:4 * half + 4, i * P:(i + 1) * P],
                    bank.rearrange("p (a t) -> p a t", a=4),
                    spread(self.gain[:, 4 * half:4 * half + 4], P), ALU.mult,
                ).then_inc(k.R.free, 1)
            if i + 2 < n:
                scale(i + 2)

    def pe(self, pe):
        k = self.k
        for i in range(self.n):
            pe.wait_ge(self.hn, self.hn0 + i + 1)
            for half in range(2):
                bank, free = k.R.fill()
                pe.wait_ge(k.R.free, free)
                for a in range(4):
                    c = 4 * half + a
                    mm = pe.transpose(bank[:, a * P:(a + 1) * P], self.rows(i)[:, c * P:(c + 1) * P], k.c("ident"))
                    k.W.first(mm)
                mm.then_inc(k.R.full, 1)


class CrossAttention:

    def __init__(self, k, l):
        self.k, self.l = k, l
        self.uT = k.at(0, 4096, k=KD)
        self.oT = k.at(0, 4096, k=KD)
        self.qT = k.at(4096, 4096, k=KD)
        self.kT = k.at(8192, 2048, k=KD)
        self.v = k.at(10240, 2048, j=NM)
        self.memT = k.at(12288, 2048, k=KD)
        self.pT = k.at(12288, 2048, r=2, j=NM)
        self.mem = k.at(14336, 2048, j=NM)
        self.prob = k.at(14336, 4096, i=NT, h=XH)
        self.mload, m0 = k.reserve("mem_loaded", 16)
        self.mload0 = m0
        self.mnorm = Norm(k, lambda i: self.mem[:, i, :], NM, k.s("g_mem"), self.memT, ready=(self.mload, m0 + 16))
        self.norm = Norm(k, lambda i: k.h[:, i, :], NT, k.s(f"g_xa{l}"), self.uT)
        self.mx, self.mx0 = k.reserve("xa_max", 8)
        self.pr, self.pr0 = k.reserve("xa_prob", 8)
        self.neg = k.stat[:, 16:32]
        self.sum = k.stat[:, 32:48]
        self.inv = k.stat[:, 48:64]

    def loads(self):
        d, l = self.k.dram, self.l
        for w in ("xa_wk", "xa_wv", "xa_wq"):
            for n in range(2):
                yield d[w][l][:, n * 512:(n + 1) * 512].rearrange("(k p) n -> p k n", p=P)
        for j in range(2):
            yield d["xa_wo"][l][j * 512:(j + 1) * 512, :].rearrange("(k p) n -> p k n", p=P)

    def sp(self, sp):
        k = self.k
        load_weights(k, sp, self.loads())

    def pool(self, pool):
        k = self.k
        pool.dma_start(self.mem, k.dram["mem"][0].rearrange("(j p) d -> p j d", p=P)).then_inc(self.mload, 16)

    def pe(self, pe):
        k = self.k
        self.mnorm.pe(pe)
        pe.wait_ge(k.R.free, k.R.all())
        for n in range(2):
            w, full, got = k.W.take()
            pe.wait_ge(full, got)
            w = w.rearrange("p (k n) -> p k n", k=KD)
            for pair in range(2):
                bank, free = k.A.fill()
                pe.wait_ge(k.A.free, free)
                for s in range(2):
                    m = 2 * pair + s
                    for c in range(KD):
                        mm = pe.matmul(bank[:, s * MEM:(s + 1) * MEM], w[:, c, m * P:(m + 1) * P],
                                       self.memT[:, c, :], start=c == 0, stop=c == KD - 1)
                        k.W.first(mm)
                mm.then_inc(k.A.full, 1)
            k.W.owed += 1
        for n in range(2):
            w, full, got = k.W.take()
            pe.wait_ge(full, got)
            w = w.rearrange("p (k n) -> p k n", k=KD)
            for j in range(NM):
                bank, free = k.A.fill()
                pe.wait_ge(k.A.free, free)
                for c in range(KD):
                    mm = pe.matmul(bank, self.memT[:, c, j * P:(j + 1) * P], w[:, c, :], start=c == 0,
                                   stop=c == KD - 1)
                    k.W.first(mm)
                mm.then_inc(k.A.full, 1)
            k.W.owed += 1
        self.norm.pe(pe)
        pe.wait_ge(k.R.free, k.R.all())
        for n in range(2):
            w, full, got = k.W.take()
            pe.wait_ge(full, got)
            w = w.rearrange("p (k n) -> p k n", k=KD)
            for m in range(4):
                bank, free = k.A.fill()
                pe.wait_ge(k.A.free, free)
                for c in range(KD):
                    mm = pe.matmul(bank, w[:, c, m * P:(m + 1) * P], self.uT[:, c, :], start=c == 0,
                                   stop=c == KD - 1)
                    k.W.first(mm)
                mm.then_inc(k.A.full, 1)
            k.W.owed += 1
        pe.wait_ge(k.A.free, k.A.all())
        for i in range(NT):
            for hp in range(2):
                bank, free = k.A.fill()
                pe.wait_ge(k.A.free, free)
                for s in range(2):
                    for c in range(2):
                        t = 2 * (2 * hp + s) + c
                        mm = pe.matmul(bank[:, s * MEM:(s + 1) * MEM], self.qT[:, t, i * P:(i + 1) * P],
                                       self.kT[:, t, :], start=c == 0, stop=c == 1)
                mm.then_inc(k.A.full, 1)
        pe.wait_ge(self.pr, self.pr0 + 8)

        pt_done = []

        def weighted(hh):
            pe.wait_ge(k.R.free, pt_done[hh])
            for c in range(2):
                bank, free = k.A.fill()
                pe.wait_ge(k.A.free, free)
                t = 2 * hh + c
                for j in range(NM):
                    mm = pe.matmul(bank, self.v[:, j, t * P:(t + 1) * P], self.pT[:, hh % 2, j, :], start=j == 0,
                                   stop=j == NM - 1)
                mm.then_inc(k.A.full, 1)

        for hh in range(XH):
            for j in range(NM):
                bank, free = k.R.fill()
                pe.wait_ge(k.R.free, free)
                for i in range(NT):
                    mm = pe.transpose(bank[:, i * P:(i + 1) * P], self.prob[:, i, hh, j * P:(j + 1) * P],
                                      k.c("ident"))
                mm.then_inc(k.R.full, 1)
            pt_done.append(k.R.all())
            if hh:
                weighted(hh - 1)
        weighted(XH - 1)
        pe.wait_ge(k.A.free, k.A.all())
        project_rows(k, pe, [self.oT[:, c, :] for c in range(KD)])

    def act(self, act):
        k = self.k
        self.mnorm.act(act)
        for n in range(2):
            for pair in range(2):
                bank, full = k.A.empty()
                act.wait_ge(k.A.full, full)
                m = 4 * n + 2 * pair
                act.activation(self.kT[:, m:m + 2, :], bank.rearrange("p (a t) -> p a t", a=2),
                               ACT.Copy).then_inc(k.A.free, 1)
        for n in range(2):
            for j in range(NM):
                bank, full = k.A.empty()
                act.wait_ge(k.A.full, full)
                act.activation(self.v[:, j, n * 512:(n + 1) * 512], bank,
                               ACT.Copy).then_inc(k.A.free, 1)
        self.norm.act(act)
        for m in range(KD):
            bank, full = k.A.empty()
            act.wait_ge(k.A.full, full)
            act.activation(self.qT[:, m, :], bank, ACT.Copy,
                           scale=(D // XH) ** -0.5).then_inc(k.A.free, 1)
        for i in range(NT):
            for hp in range(2):
                bank, full = k.A.empty()
                act.wait_ge(self.mx, self.mx0 + 2 * i + hp + 1)
                for s in range(2):
                    hh = 2 * hp + s
                    ins = act.activation(self.prob[:, i, hh, :], bank[:, s * MEM:(s + 1) * MEM], ACT.Exp,
                                         bias=self.neg[:, 4 * i + hh:4 * i + hh + 1],
                                         accum_out=self.sum[:, 4 * i + hh:4 * i + hh + 1])
                ins.then_inc(k.A.free, 1)
        for t in range(KD):
            bank, full = k.A.empty()
            act.wait_ge(k.A.full, full)
            act.activation(self.oT[:, t, :], bank, ACT.Copy).then_inc(k.A.free, 1)

    def dve(self, dve):
        k = self.k
        self.mnorm.dve(dve)
        self.norm.dve(dve)
        first = self.a0 + 16
        for i in range(NT):
            for hp in range(2):
                n = first + 2 * i + hp
                dve.wait_ge(k.A.full, n + 1)
                dve.tensor_reduce(self.neg[:, 4 * i + 2 * hp:4 * i + 2 * hp + 2],
                                  k.A.banks[n % 4].rearrange("p (a t) -> p a t", a=2), AX.X, ALU.max,
                                  negate=True).then_inc(self.mx, 1)
            if i:
                self.normalise(dve, i - 1)
        self.normalise(dve, NT - 1)
        for hh in range(XH):
            for j in range(NM):
                bank, full = k.R.empty()
                dve.wait_ge(k.R.full, full)
                if hh >= 2:
                    dve.wait_ge(k.A.full, first + 8 + 2 * (hh - 2) + 2)
                dve.tensor_copy(self.pT[:, hh % 2, j, :], bank).then_inc(k.R.free, 1)
        add_rows(k, dve)

    def normalise(self, dve, i):
        k = self.k
        dve.wait_ge(k.A.free, k.A.stored(self.a0 + 16 + 2 * i + 2))
        k.dlink(dve.reciprocal(self.inv[:, 4 * i:4 * i + 4], self.sum[:, 4 * i:4 * i + 4]))
        for hp in range(2):
            dve.tensor_tensor(self.prob[:, i, 2 * hp:2 * hp + 2, :], self.prob[:, i, 2 * hp:2 * hp + 2, :],
                              spread(self.inv[:, 4 * i + 2 * hp:4 * i + 2 * hp + 2], MEM),
                              ALU.mult).then_inc(self.pr, 1)

    A_JOBS, R_JOBS = 4 + 4 + 8 + 8 + 8, 2 * NM + 2 * NT + 8 + 8


def load_weights(k, sp, blocks):
    for src in blocks:
        slot, full, free = k.W.load()
        sp.wait_ge(k.W.free, free)
        sp.dma_start(slot.rearrange("p (k n) -> p k n", k=src.shape[1]), src).then_inc(full, 16)


def project_rows(k, pe, tiles):
    blocks = [k.W.take() for _ in range(len(tiles) // 4)]
    for _, full, got in blocks:
        pe.wait_ge(full, got)
    for i in range(NT):
        for n in range(2):
            bank, free = k.R.fill()
            pe.wait_ge(k.R.free, free)
            for c, t in enumerate(tiles):
                w = blocks[c // 4][0].rearrange("p (k n) -> p k n", k=4)
                mm = pe.matmul(bank, t[:, i * P:(i + 1) * P], w[:, c % 4, n * 512:(n + 1) * 512], start=c == 0,
                               stop=c == len(tiles) - 1)
            mm.then_inc(k.R.full, 1)
    k.W.owed += len(blocks)


def add_rows(k, dve):
    for i in range(NT):
        for n in range(2):
            bank, full = k.R.empty()
            dve.wait_ge(k.R.full, full)
            hs = k.h[:, i, n * 512:(n + 1) * 512]
            dve.tensor_tensor(hs, hs, bank, ALU.add).then_inc(k.R.free, 1)


class PairSignals:

    def __init__(self, k, name):
        s = lambda what: k.sem(f"{name}_{what}")
        self.chosen = s("chosen")
        self.gated = s("gated")
        self.x_full = s("x_full")
        self.x_stored = s("x_stored")
        self.turn_full = s("turn_full")
        self.turn_stored = s("turn_stored")
        self.hT_full = s("hT_full")
        self.hT_stored = s("hT_stored")
        self.g_full = s("gate_full")
        self.u_full = s("up_full")
        self.silu = s("silu")
        self.hid = s("hid")
        self.y_full = s("y_full")
        self.y_stored = s("y_stored")
        self.sc_full = s("sc_full")
        self.sc_added = s("sc_added")


class Moe:

    DVE_STEPS = 1

    def __init__(self, k, l):
        self.k, self.l = k, l
        self.uT = k.at(0, 4096, k=KD)
        self.xn = k.at(4096, 4096, i=NT)
        self.norm = Norm(k, lambda i: k.h[:, i, :], NT, k.s(f"g_ffn{l}"), self.uT, keep=self.xn)
        self.S = k.at(8192, 512, i=NT)
        self.SG = k.at(8704, 512, i=NT)
        self.xsT = k.at(9216, 1024, k=KD)
        self.turned = k.at(10240, 512, i=NT)
        self.y = k.at(10752, 1024)
        self.hidden_rows = k.at(11776, 512)
        self.hT = k.at(12288, 512, m=4)
        self.rank = k.at(12800, NPASS * NT * NE, b=NPASS, i=NT)
        self.gates = k.at(13824, NT * NE, i=NT)
        self.member = k.at(13952, NT * NE, i=NT)
        self.tmp = 14080
        self.routed, self.routed0 = k.reserve("moe_routed", 1)
        self.passes, self.passes0 = k.reserve("moe_passes", 1)
        self.rexp, self.rexp0 = k.reserve("moe_exp_in", 2)
        self.rexpd, self.rexpd0 = k.reserve("moe_exp_out", 2)
        self.main = PairSignals(k, "pair")
        self.more = PairSignals(k, f"more{l}")
        self.more_done = k.sem(f"more{l}_done")
        self.more_w = k.sem(f"more{l}_weights_full")
        self.npass = k.npass

    A_JOBS, R_JOBS = 0, 2 * NT + 2

    def pair_blocks(self, pair):
        d, l = self.k.dram, self.l
        for w in ("moe_w_gate", "moe_w_up"):
            for e in range(2):
                yield d[w][l][bass.ds(2 * pair + e, 1)].rearrange("e (k p) n -> p (e k) n", p=P)
        for e in range(2):
            yield d["moe_w_down"][l][bass.ds(2 * pair + e, 1)].rearrange("e (k p) n -> p (e k) n", p=P)

    def sp(self, sp):
        k = self.k
        n0 = k.W.loaded
        with sp.Fori(0, PAIRS) as pair:
            for j, src in enumerate(self.pair_blocks(pair)):
                slot = k.W.slots[(n0 + j) % WSLOTS]
                sp.wait_ge(k.W.free, 6 * pair + (n0 + j + 1))
                sp.dma_start(slot.rearrange("p (k n) -> p k n", k=src.shape[1]), src).then_inc(
                    k.W.full[(n0 + j) % WSLOTS], 16)
        k.W.loaded += 6 * PAIRS
        self.w0 = n0

        def again(g, pair):
            sp.wait_ge(self.more.sc_added, 8 * g + 2)
            for j, src in enumerate(self.pair_blocks(pair)):
                slot = k.W.slots[(n0 + j) % WSLOTS]
                sp.dma_start(slot.rearrange("p (k n) -> p k n", k=src.shape[1]), src).then_inc(self.more_w, 16)

        self.further(sp, again, lambda: sp.wait_ge(self.main.sc_added, self.l * 8 * PAIRS + 8 * PAIRS + 2),
                     lambda: sp.wait_ge(self.more_done, 1))

    def further(self, eng, body, before=None, after=None):
        eng.wait_ge(self.passes, self.passes0 + 1)
        n = eng.value_load(self.npass[0:1, self.l:self.l + 1], min_val=1, max_val=NPASS)
        with eng.If(n > 1):
            if before:
                before()
            with eng.Fori(1, n) as b:
                with eng.Fori(0, PAIRS) as pair:
                    g = eng.snap(b * PAIRS + pair - PAIRS, min_val=0, max_val=PAIRS * NPASS)
                    body(g, pair)
            if after:
                after()

    def choose(self, dve, sg, g, b, pair, alone=False):
        k = self.k
        if not alone:
            dve.wait_ge(sg.x_full, 2 * g)
            dve.wait_ge(sg.gated, g)
        slots = self.S.rearrange("p i (e s) -> p i e s", e=2)
        iota = k.c("iota").unsqueeze(1).unsqueeze(1).broadcast_to([P, NT, 2, CAP])
        rank = self.rank[:, b, :, :] if isinstance(b, int) else self.rank[:, bass.ds(b, 1), :, :].rearrange(
            "p b i e -> p (b i) e")
        rank = spread(rank[:, :, bass.ds(2 * pair, 2)], CAP)
        dve.tensor_tensor(slots, iota, rank, ALU.is_equal).then_inc(sg.chosen, 1)

    def weigh(self, dve, sg, g, pair, alone=False):
        if not alone:
            dve.wait_ge(sg.turn_full, g)
        dve.wait_ge(sg.chosen, g + 1)
        dve.tensor_tensor(self.SG.rearrange("p i (e s) -> p i e s", e=2),
                          self.S.rearrange("p i (e s) -> p i e s", e=2),
                          spread(self.gates[:, :, bass.ds(2 * pair, 2)], CAP), ALU.mult).then_inc(sg.gated, 1)

    def gather(self, pe, sg, g):
        k = self.k
        pe.wait_ge(sg.chosen, g + 1)
        for half in range(2):
            bank = k.banks[half]
            for a in range(4):
                c = 4 * half + a
                for i in range(NT):
                    mm = pe.matmul(bank[:, a * P:(a + 1) * P], self.xn[:, i, c * P:(c + 1) * P], self.S[:, i, :],
                                   start=i == 0, stop=i == NT - 1)
            mm.then_inc(sg.x_full, 1)

    def turn(self, pe, sg, g):
        k = self.k
        pe.wait_ge(sg.gated, g + 1)
        pe.wait_ge(sg.hid, g + 1)
        for i in range(NT):
            mm = pe.transpose(k.banks[2][:, i * P:(i + 1) * P], self.SG[:, i, :], k.c("ident"))
            if i == 0:
                self.freed(mm)
        mm.then_inc(sg.turn_full, 1)

    def turn_hidden(self, pe, sg, g):
        k = self.k
        pe.wait_ge(sg.hid, g + 1)
        for m in range(4):
            mm = pe.transpose(k.banks[3][:, m * P:(m + 1) * P], self.hidden_rows[:, m * P:(m + 1) * P],
                              k.c("ident"))
        mm.then_inc(sg.hT_full, 1)

    def gate_up(self, pe, sg, g, wait, w, alone=False, free_first=False):
        k = self.k
        pe.wait_ge(sg.x_stored, 2 * g + 2)
        for u in range(2):
            if not alone:
                pe.wait_ge(*((sg.turn_stored, g), (sg.hT_stored, g))[u])
            wait(2 * u)
            wait(2 * u + 1)
            bank = k.banks[2 + u]
            for c in range(KD):
                for e in range(2):
                    wt = w[2 * u + e].rearrange("p (k n) -> p k n", k=KD)
                    mm = pe.matmul(bank[e * CAP:(e + 1) * CAP, :], self.xsT[:, c, e * CAP:(e + 1) * CAP],
                                   wt[:, c, :], start=c == 0, stop=c == KD - 1)
                    if c == 0 and e == 0 and (u == 1 or free_first):
                        self.freed(mm)
            mm.then_inc((sg.g_full, sg.u_full)[u], 1)

    def down(self, pe, sg, g, wait, w, alone=False):
        k = self.k
        pe.wait_ge(sg.hT_stored, g + 1)
        for n in range(2):
            if not alone:
                pe.wait_ge(sg.y_stored, 2 * g + n - 1)
            if n == 0:
                wait(4)
                wait(5)
            for m in range(4):
                for e in range(2):
                    wt = w[4 + e].rearrange("p (k n) -> p k n", k=4)
                    mm = pe.matmul(k.banks[4 + n][e * CAP:(e + 1) * CAP, :], self.hT[:, m, e * CAP:(e + 1) * CAP],
                                   wt[:, m, n * 512:(n + 1) * 512], start=m == 0, stop=m == 3)
            mm.then_inc(sg.y_full, 1)

    def scatter(self, pe, sg, g):
        k = self.k
        pe.wait_ge(sg.turn_stored, g + 1)
        pe.wait_ge(sg.y_stored, 2 * g + 2)
        for j in range(8):
            i, n = j // 2, j % 2
            pe.wait_ge(sg.sc_added, 8 * g + j + 1)
            pe.matmul(k.banks[6 + n], self.turned[:, i, :], self.y[:, n * 512:(n + 1) * 512], start=True,
                      stop=True).then_inc(sg.sc_full, 1)

    def store_gathered(self, dve, sg, g):
        k = self.k
        for half in range(2):
            dve.wait_ge(sg.x_full, 2 * g + half + 1)
            dve.tensor_tensor(self.xsT[:, 4 * half:4 * half + 4, :],
                              k.banks[half].rearrange("p (a t) -> p a t", a=4),
                              spread(k.s(f"g_ffn{self.l}")[:, 4 * half:4 * half + 4], P),
                              ALU.mult).then_inc(sg.x_stored, 1)

    def hidden(self, dve, sg, g):
        dve.wait_ge(sg.u_full, g + 1)
        dve.wait_ge(sg.silu, g + 1)
        dve.tensor_tensor(self.hidden_rows, self.hidden_rows, self.k.banks[3], ALU.mult).then_inc(sg.hid, 1)

    def add_scattered(self, dve, sg, g):
        k = self.k
        for j in range(8):
            i, n = j // 2, j % 2
            dve.wait_ge(sg.sc_full, 8 * g + j + 1)
            if j == 0:
                dve.wait_ge(sg.sc_added, 8 * g + 2)
            hs = k.h[:, i, n * 512:(n + 1) * 512]
            dve.tensor_tensor(hs, hs, k.banks[6 + n], ALU.add).then_inc(sg.sc_added, 1)

    def silu(self, act, sg, g, alone=False):
        act.wait_ge(sg.g_full, g + 1)
        if not alone:
            act.wait_ge(sg.hT_full, g)
        act.activation(self.hidden_rows, self.k.banks[2], ACT.Silu).then_inc(sg.silu, 1)

    def store_turned(self, act, sg, g, alone=False):
        act.wait_ge(sg.turn_full, g + 1)
        if not alone:
            act.wait_ge(sg.sc_full, 8 * g)
        act.activation(self.turned, self.k.banks[2].rearrange("p (i t) -> p i t", i=NT),
                       ACT.Copy).then_inc(sg.turn_stored, 1)

    def store_hidden(self, act, sg, g, alone=False):
        act.wait_ge(sg.hT_full, g + 1)
        if not alone:
            act.wait_ge(sg.y_full, 2 * g)
        act.activation(self.hT, self.k.banks[3].rearrange("p (m s) -> p m s", m=4),
                       ACT.Copy).then_inc(sg.hT_stored, 1)

    def store_down(self, act, sg, g):
        for n in range(2):
            act.wait_ge(sg.y_full, 2 * g + n + 1)
            act.activation(self.y[:, n * 512:(n + 1) * 512], self.k.banks[4 + n],
                           ACT.Copy).then_inc(sg.y_stored, 1)

    def each(self, eng, body):
        g0 = self.l * PAIRS
        body(0, g0, True, False)
        with eng.Fori(1, PAIRS - 1) as pair:
            body(pair, pair + g0, False, False)
        body(PAIRS - 1, g0 + PAIRS - 1, False, True)

    def pe(self, pe):
        k, sg = self.k, self.main
        self.norm.pe(pe)
        bank, free = k.R.fill()
        pe.wait_ge(k.R.free, free)
        pe.wait_ge(k.R.free, k.R.stored(k.R.filled - 1))
        wr = k.s(f"w_route{self.l}").rearrange("p (k n) -> p k n", k=KD)
        for i in range(NT):
            for c in range(KD):
                mm = pe.matmul(bank[:, i * 36:(i + 1) * 36], self.uT[:, c, i * P:(i + 1) * P], wr[:, c, :],
                               start=c == 0, stop=c == KD - 1)
        mm.then_inc(k.R.full, 1)
        bank, free = k.R.fill()
        pe.wait_ge(k.R.free, free)
        pe.wait_ge(self.routed, self.routed0 + 1)
        for i in range(NT + 1):
            for j in range(min(i + 1, NT)):
                mm = pe.matmul(bank[:, i * NE:(i + 1) * NE], k.c("supper") if j == i else k.c("ones"),
                               self.member[:, j, :], start=j == 0, stop=j == min(i, NT - 1))
        mm.then_inc(k.R.full, 1)
        pe.wait_ge(k.A.free, k.A.all())
        pe.wait_ge(k.R.free, k.R.all())
        n0 = k.W.taken
        w = [k.W.slots[(n0 + j) % WSLOTS] for j in range(6)]

        def wait_main(pair):
            def wait(j):
                s = (n0 + j) % WSLOTS
                pe.wait_ge(k.W.full[s], 16 * pair + 16 * ((n0 + j) // WSLOTS + 1))
            return wait

        self.freed = lambda mm: mm.then_inc(k.W.free, 2)
        assert k.W.owed == 0
        self.gather(pe, sg, self.l * PAIRS)

        def body(pair, g, first, last):
            wait = wait_main(pair)
            alone = first and self.l == 0
            self.gate_up(pe, sg, g, wait, w, alone, free_first=not first)
            if not first:
                self.scatter(pe, sg, g - 1)
            self.turn(pe, sg, g)
            self.turn_hidden(pe, sg, g)
            if not last:
                self.gather(pe, sg, g + 1)
            self.down(pe, sg, g, wait, w, alone)

        self.each(pe, body)
        self.scatter(pe, sg, self.l * PAIRS + PAIRS - 1)
        k.W.taken += 6 * PAIRS
        k.W.owed += 2

        def again(g, pair):
            sm = self.more
            self.freed = lambda mm: None
            wait = lambda j: pe.wait_ge(self.more_w, 96 * g + 96)
            self.gather(pe, sm, g)
            self.gate_up(pe, sm, g, wait, w, alone=True)
            self.turn(pe, sm, g)
            self.turn_hidden(pe, sm, g)
            self.down(pe, sm, g, wait, w, alone=True)
            self.scatter(pe, sm, g)

        self.further(pe, again)

    def act(self, act):
        k, sg = self.k, self.main
        self.norm.act(act)
        t = self.route_tiles()
        act.wait_ge(self.rexp, self.rexp0 + 1)
        act.activation(t["gexp"], t["gdiff"], ACT.Exp).then_inc(self.rexpd, 1)
        act.wait_ge(self.rexp, self.rexp0 + 2)
        act.activation(t["eexp"], t["ediff"], ACT.Exp).then_inc(self.rexpd, 1)

        def body(pair, g, first, last):
            alone = first and self.l == 0
            self.silu(act, sg, g, alone)
            self.store_turned(act, sg, g, alone)
            self.store_hidden(act, sg, g, alone)
            self.store_down(act, sg, g)

        self.each(act, body)

        def again(g, pair):
            sm = self.more
            self.silu(act, sm, g, alone=True)
            self.store_turned(act, sm, g, alone=True)
            self.store_hidden(act, sm, g, alone=True)
            self.store_down(act, sm, g)

        self.further(act, again)

    def route_tiles(self):
        k, at, out = self.k, self.tmp, {}

        def tile(name, *shape):
            nonlocal at
            n = int(np.prod(shape))
            v = k.arena[:, at:at + n]
            at += n
            letters = "abcd"[:len(shape)]
            out[name] = v.rearrange(f"p ({' '.join(letters)}) -> p {' '.join(letters)}",
                                    **dict(zip(letters, shape))) if len(shape) > 1 else v

        tile("logits", NT, NG + NE)
        tile("gmax", NT)
        tile("gdiff", NT, NG)
        tile("gexp", NT, NG)
        tile("gsum", NT)
        tile("gw", NT)
        tile("geq", NT, NG)
        tile("gtop", NT)
        tile("group", NT, NG)
        tile("spreadl", NT, NG, EPG)
        tile("el", NT, EPG)
        tile("m1", NT)
        tile("m2", NT)
        tile("eq", NT, EPG)
        tile("top", NT)
        tile("one1", NT, EPG)
        tile("one2", NT, EPG)
        tile("el2", NT, EPG)
        tile("ediff", NT)
        tile("eexp", NT)
        tile("den", NT)
        tile("gate1", NT)
        tile("gate2", NT)
        tile("g8", NT, EPG)
        tile("m8", NT, EPG)
        tile("cmax", 1)
        tile("over", NPASS - 1)
        tile("np", 1)
        return out

    def first_of(self, link, dve, x, top, eq, cand, onehot, n):
        k = self.k
        prio = k.c("prio")[:, 0:n].unsqueeze(1).broadcast_to([P, NT, n])
        link(dve.tensor_tensor(eq, x, spread(top, n), ALU.is_equal))
        link(dve.tensor_tensor(eq, eq, prio, ALU.mult))
        link(dve.tensor_reduce(cand, eq, AX.X, ALU.max))
        link(dve.tensor_tensor(onehot, eq, spread(cand, n), ALU.is_equal))

    def route(self, dve):
        k, t, link = self.k, self.route_tiles(), self.k.dlink
        logits = t["logits"]
        bank, full = k.R.empty()
        dve.wait_ge(k.R.full, full)
        bias = k.s(f"b_route{self.l}").unsqueeze(1).broadcast_to([P, NT, NG + NE])
        dve.tensor_tensor(logits, bank[:, 0:NT * (NG + NE)].rearrange("p (a b) -> p a b", a=NT), bias,
                          ALU.add).then_inc(k.R.free, 1)
        dve.wait_ge(k.R.free, k.R.stored(k.R.emptied))
        groups, experts = logits[:, :, 0:NG], logits[:, :, NG:NG + NE]
        link(dve.tensor_reduce(t["gmax"], groups, AX.X, ALU.max))
        dve.tensor_tensor(t["gdiff"], groups, spread(t["gmax"], NG), ALU.subtract).then_inc(self.rexp, 1)
        self.first_of(link, dve, groups, t["gmax"], t["geq"], t["gtop"], t["group"], NG)
        link(dve.tensor_tensor(t["spreadl"], experts.rearrange("p a (g e) -> p a g e", g=NG),
                               spread(t["group"], EPG), ALU.mult))
        link(dve.tensor_reduce(t["el"], t["spreadl"].rearrange("p a g e -> p a e g"), AX.X, ALU.add))
        link(dve.tensor_reduce(t["m1"], t["el"], AX.X, ALU.max))
        self.first_of(link, dve, t["el"], t["m1"], t["eq"], t["top"], t["one1"], EPG)
        link(dve.scalar_tensor_tensor(t["el2"], t["one1"], -3.0e38, t["el"], ALU.mult, ALU.add))
        link(dve.tensor_reduce(t["m2"], t["el2"], AX.X, ALU.max))
        self.first_of(link, dve, t["el2"], t["m2"], t["eq"], t["top"], t["one2"], EPG)
        dve.tensor_tensor(t["ediff"], t["m2"], t["m1"], ALU.subtract).then_inc(self.rexp, 1)
        dve.wait_ge(self.rexpd, self.rexpd0 + 2)
        link(dve.tensor_reduce(t["gsum"], t["gexp"], AX.X, ALU.add))
        link(dve.tensor_scalar(t["den"], t["eexp"], 1.0, None, ALU.add))
        link(dve.tensor_tensor(t["den"], t["den"], t["gsum"], ALU.mult))
        link(dve.reciprocal(t["gate1"], t["den"]))
        link(dve.tensor_tensor(t["gate2"], t["gate1"], t["eexp"], ALU.mult))
        link(dve.tensor_tensor(t["g8"], t["one1"], spread(t["gate1"], EPG), ALU.mult))
        link(dve.tensor_tensor(t["m8"], t["one2"], spread(t["gate2"], EPG), ALU.mult))
        link(dve.tensor_tensor(t["g8"], t["g8"], t["m8"], ALU.add))
        link(dve.tensor_tensor(t["m8"], t["one1"], t["one2"], ALU.add))

        def by_group(dst, v):
            ins = None
            for g in range(NG):
                ins = dve.tensor_tensor(dst[:, :, g * EPG:(g + 1) * EPG], v,
                                        t["group"][:, :, g:g + 1].broadcast_to([P, NT, EPG]), ALU.mult)
                if g < NG - 1:
                    ins.then_inc(k.dlink.sem, 1)
                    k.dlink.n += 1
            return ins

        link(by_group(self.gates, t["g8"]))
        link(by_group(self.member, t["m8"]))
        dve.sem_inc(self.routed, 1)
        bank, full = k.R.empty()
        dve.wait_ge(k.R.full, full)
        ranks = bank[:, 0:NT * NE].rearrange("p (a e) -> p a e", a=NT)
        link(dve.scalar_tensor_tensor(self.rank[:, 0, :, :], ranks, 1.0, self.member, ALU.add, ALU.mult))
        link(dve.tensor_reduce(t["cmax"], bank[:, NT * NE:(NT + 1) * NE], AX.X, ALU.max))
        link(dve.tensor_scalar(self.rank[:, 0, :, :], self.rank[:, 0, :, :], -1.0, None, ALU.add))
        for b in range(1, NPASS):
            dve.tensor_scalar(self.rank[:, b, :, :], self.rank[:, 0, :, :], -float(CAP * b), None,
                              ALU.add).then_inc(k.dlink.sem, 1)
            k.dlink.n += 1
        link(dve.tensor_tensor(t["over"], k.c("limits"), t["cmax"].broadcast_to([P, NPASS - 1]), ALU.is_lt))
        link(dve.tensor_reduce(t["np"], t["over"], AX.X, ALU.add))
        dve.tensor_scalar(self.npass[:, self.l:self.l + 1], t["np"], 1.0, None, ALU.add).then_inc(self.passes, 1)
        dve.sem_inc(k.R.free, 1)

    def dve(self, dve):
        k, sg = self.k, self.main
        self.norm.dve(dve)
        self.route(dve)
        g0 = self.l * PAIRS
        self.choose(dve, sg, g0, 0, 0, alone=True)
        self.weigh(dve, sg, g0, 0, alone=True)
        self.store_gathered(dve, sg, g0)

        def body(pair, g, first, last):
            if not last:
                self.choose(dve, sg, g + 1, 0, pair + 1)
            self.hidden(dve, sg, g)
            if not first:
                self.add_scattered(dve, sg, g - 1)
            if not last:
                self.weigh(dve, sg, g + 1, pair + 1)
                self.store_gathered(dve, sg, g + 1)

        self.each(dve, body)
        self.add_scattered(dve, sg, g0 + PAIRS - 1)

        def again(g, pair):
            sm = self.more
            b = dve.snap((g - pair) // PAIRS + 1, min_val=1, max_val=NPASS - 1)
            self.choose(dve, sm, g, b, pair, alone=True)
            self.weigh(dve, sm, g, pair, alone=True)
            self.store_gathered(dve, sm, g)
            self.hidden(dve, sm, g)
            self.add_scattered(dve, sm, g)

        self.further(dve, again, after=lambda: dve.drain().then_inc(self.more_done, 1))

    def pool(self, pool):
        pass


class Store:

    A_JOBS = R_JOBS = 0

    def __init__(self, k):
        self.k = k
        self.sq, self.ms, self.rt = k.sem("final_sums"), k.sem("final_means"), k.sem("final_roots")
        self.rows, self.out, self.gain = k.sem("final_rows"), k.sem("out_stored"), k.sem("final_gain")
        self.g = k.at(4096, D)

    def pool(self, pool):
        k = self.k
        pool.dma_start(self.g, k.dram["final_gain"]).then_inc(self.gain, 16)

    def sp(self, sp):
        k = self.k
        for i in range(NT):
            sp.wait_ge(self.rows, i + 1)
            sp.dma_start(k.dram["out"][0][i * P:(i + 1) * P, :], k.at(8192, NT * D, i=NT)[:, i, :]).then_inc(self.out, 16)
        sp.wait_ge(self.out, 16 * NT)

    def act(self, act):
        k = self.k
        for i in range(NT):
            if i:
                act.wait_ge(self.sq, i)
            act.activation(k.at(0, D), k.h[:, i, :], ACT.Square, accum_out=k.stat[:, i:i + 1]).then_inc(self.sq, 1)
        act.wait_ge(self.ms, 1)
        act.activation(k.stat[:, 8:12], k.stat[:, 4:8], ACT.Sqrt).then_inc(self.rt, 1)

    def dve(self, dve):
        k = self.k
        dve.wait_ge(self.sq, NT)
        dve.tensor_scalar(k.stat[:, 4:8], k.stat[:, 0:4], 1.0 / D, EPS, ALU.mult, ALU.add).then_inc(self.ms, 1)
        dve.wait_ge(self.rt, 1)
        k.dlink(dve.reciprocal(k.stat[:, 12:16], k.stat[:, 8:12]))
        dve.wait_ge(self.gain, 16)
        for i in range(NT):
            dve.scalar_tensor_tensor(k.at(8192, NT * D, i=NT)[:, i, :], k.h[:, i, :], k.stat[:, 12 + i:13 + i],
                                     self.g, ALU.mult, ALU.mult).then_inc(self.rows, 1)

    def pe(self, pe):
        pass



class Even:

    A_JOBS = 4 + 12 + 16 + 8
    R_JOBS = 8 + 8 + 10 + 1 + 1 + (3 * NT + 2 * (NT - 1) + 2 * (NT - 1)) + 8 + 8

    def __init__(self, k):
        self.k = k
        self.uT = k.at(0, 4096, k=KD)
        self.mixT = k.at(4096, 6144, k=MIXT)
        self.norm = Norm(k, lambda i: k.h[:, i, :], NT, k.s("g_mix0"), self.uT)
        self.xs = k.at(10240, 4096, i=NT)
        self.bc = k.at(14336, 2048, k=4)
        self.btok = k.at(16384, 1024, i=NT, g=SSM_G)
        self.cg = k.at(17408, 1024, b=2)
        self.pad3 = k.at(18432, 2 * 514, b=2)
        self.acc3 = k.at(19460, 1024, b=2)
        self.xpad = k.at(6144, 2 * 516, b=2)
        self.acc = k.at(7176, 1024, b=2)
        self.sil = k.at(8200, 1024, b=2)
        self.state = k.at(17408, 1024, g=SSM_G)
        self.xdt = k.at(18432, 1024)
        self.xde = k.at(19456, 1024)
        self.G = k.at(6144, 1024, b=2)
        self.E = k.at(7168, 1024, b=2)
        self.cb = k.at(8192, 256, g=SSM_G)
        self.off = [k.at(8448, 512), k.at(20480, 512)]
        small = lambda j: k.at(9344 + 64 * j, 64, i=NT)
        (self.dt, self.adt, self.cum, self.ecum, self.tot, self.etot, self.toend, self.dte, self.t0,
         self.t1) = [small(j) for j in range(10)]
        self.ea = k.at(9984, 16)
        self.gsum = k.at(10000, 8)
        self.zs = k.at(18432, 2048, b=2)
        self.junk = k.at(17408, 512)
        s = lambda n: k.sem(f"ssd_{n}")
        self.pads, self.conv, self.silu = s("pads"), s("convolved"), s("silu")
        self.dte_in, self.dte_out, self.dt_ready = s("softplus_in"), s("softplus_out"), s("decay_ready")
        self.dt_first = s("exponents_ready")
        self.cexp = s("cum_exp")
        self.g_ready, self.w_ready, self.x_ready = s("segments_in"), s("weights_ready"), s("x_scaled")
        self.gated, self.sums, self.roots, self.normed = s("gated"), s("sums"), s("roots"), s("normed")
        self.state_ready = s("state_ready")
        self.sq_free = s("means")

    def loads(self):
        d = self.k.dram
        for c in (1, 2, 0, 5, 6, 7, 3, 4):
            yield d["ev_w_in"][0][:, c * 512:(c + 1) * 512].rearrange("(k p) n -> p k n", p=P)
        for j in range(3):
            yield d["ev_w_out"][0][j * 512:(j + 1) * 512, :].rearrange("(k p) n -> p k n", p=P)

    def sp(self, sp):
        load_weights(self.k, sp, self.loads())

    def pool(self, pool):
        k = self.k
        pool.wait_ge(self.dt_ready, 1)
        upper = k.c("upper").unsqueeze(1).broadcast_to([P, 4, P])
        for i in range(NT):
            if i:
                pool.wait_ge(k.R.full, self.chunk_r(i))
            xs = self.xs[:, i, :].rearrange("p (h d) -> p h d", h=SSM_H)

            def segment(hb):
                n = 4 * i + hb
                if n >= 2:
                    pool.wait_ge(k.A.full, self.a0 + 16 + n - 2 + 1)
                pool.tensor_tensor(self.G[:, n % 2, :].rearrange("p (h t) -> p h t", h=4), upper,
                                   spread(self.adt[:, i, 4 * hb:4 * hb + 4], P), ALU.mult).then_inc(self.g_ready, 1)

            segment(0)
            segment(1)
            pool.tensor_tensor(self.xdt.rearrange("p (h d) -> p h d", h=SSM_H), xs, spread(self.dt[:, i, :], SSM_P),
                               ALU.mult).then_inc(self.x_ready, 1)
            pool.tensor_tensor(self.xde.rearrange("p (h d) -> p h d", h=SSM_H), xs, spread(self.dte[:, i, :], SSM_P),
                               ALU.mult).then_inc(self.x_ready, 1)
            pool.wait_ge(self.x_ready, 3 * i + 2)
            pool.tensor_tensor(xs, xs, spread(k.s("d_skip"), SSM_P), ALU.mult).then_inc(self.x_ready, 1)
            segment(2)
            segment(3)

    def chunk_r(self, i):
        return self.r0 + 8 + 8 + 10 + 2 + 3 * i + 2 * max(i - 1, 0) + 2 * min(i, NT - 1)

    def pe(self, pe):
        k = self.k
        self.norm.pe(pe)
        pe.wait_ge(k.R.free, k.R.all())

        def project(ring, w, m):
            bank, free = ring.fill()
            pe.wait_ge(ring.free, free)
            for c in range(KD):
                mm = pe.matmul(bank, w[:, c, m * P:(m + 1) * P], self.uT[:, c, :], start=c == 0, stop=c == KD - 1)
                k.W.first(mm)
            mm.then_inc(ring.full, 1)

        def block():
            w, full, got = k.W.take()
            pe.wait_ge(full, got)
            return w.rearrange("p (k n) -> p k n", k=KD)

        wc, wx, wb = block(), block(), block()
        for m in range(4):
            project(k.A, wc, m)
            project(k.R, wx, m)
            project(k.R, wb, m)
        k.W.owed += 3

        def turned(m):
            pe.wait_ge(self.silu, m + 1)
            bank, free = k.R.fill()
            pe.wait_ge(k.R.free, free)
            src = self.sil[:, m % 2, :] if m < 8 else self.bc[:, m - 8, :]
            for i in range(NT):
                mm = pe.transpose(bank[:, i * P:(i + 1) * P], src[:, i * P:(i + 1) * P], k.c("ident"))
            mm.then_inc(k.R.full, 1)

        for m in range(12):
            if m % 4 == 0:
                w = block()
            project(k.A, w, m % 4)
            if m % 4 == 3:
                k.W.owed += 1
            if 2 <= m:
                turned(m - 2)
        bank, free = k.R.fill()
        pe.wait_ge(k.R.free, free)
        wdt = k.s("w_dt").rearrange("p (k n) -> p k n", k=KD)
        for i in range(NT):
            for c in range(KD):
                mm = pe.matmul(bank[:, i * SSM_H:(i + 1) * SSM_H], self.uT[:, c, i * P:(i + 1) * P], wdt[:, c, :],
                               start=c == 0, stop=c == KD - 1)
        mm.then_inc(k.R.full, 1)
        bank, free = k.R.fill()
        pe.wait_ge(k.R.free, free)
        pe.wait_ge(self.dt_first, 1)
        adt = self.adt.rearrange("p i h -> p (i h)")
        pe.matmul(bank[:, 0:64], k.c("upper"), adt, start=True, stop=True)
        pe.matmul(bank[:, 64:128], k.c("ones"), adt, start=True, stop=True).then_inc(k.R.full, 1)

        for i in range(NT):
            tok = slice(i * P, (i + 1) * P)
            bank, free = k.R.fill()
            pe.wait_ge(k.R.free, free)
            pe.wait_ge(self.silu, 12)
            for g in range(SSM_G):
                mm = pe.matmul(bank[:, g * P:(g + 1) * P], self.bc[:, g, tok], self.bc[:, 2 + g, tok], start=True,
                               stop=True)
            mm.then_inc(k.R.full, 1)

            def segment(hb):
                n = 4 * i + hb
                bank, free = k.A.fill()
                pe.wait_ge(k.A.free, free)
                pe.wait_ge(self.g_ready, n + 1)
                pe.matmul(bank, k.c("slower"), self.G[:, n % 2, :], start=True, stop=True).then_inc(k.A.full, 1)

            def diagonal(bank, hb):
                n = 4 * i + hb
                pe.wait_ge(self.w_ready, n + 1)
                for j in range(4):
                    h = 4 * hb + j
                    mm = pe.matmul(bank[:, (h % 8) * SSM_P:(h % 8 + 1) * SSM_P],
                                   self.E[:, n % 2, j * P:(j + 1) * P], self.xdt[:, h * SSM_P:(h + 1) * SSM_P],
                                   start=True, stop=True)
                return mm

            segment(0)
            segment(1)
            if i:
                pe.wait_ge(self.state_ready, 2 * i)
                for g in range(SSM_G):
                    bank, free = k.R.fill()
                    pe.wait_ge(k.R.free, free)
                    pe.matmul(bank, self.bc[:, 2 + g, tok], self.state[:, g, :], start=True,
                              stop=True).then_inc(k.R.full, 1)
            pe.wait_ge(self.x_ready, 3 * i + 2)
            bank, free = k.R.fill()
            pe.wait_ge(k.R.free, free)
            diagonal(bank, 0)
            segment(2)
            mm = diagonal(bank, 1)
            mm.then_inc(k.R.full, 1)
            segment(3)
            bank, free = k.R.fill()
            pe.wait_ge(k.R.free, free)
            diagonal(bank, 2)
            mm = diagonal(bank, 3)
            mm.then_inc(k.R.full, 1)
            if i < NT - 1:
                for g in range(SSM_G):
                    bank, free = k.R.fill()
                    pe.wait_ge(k.R.free, free)
                    pe.matmul(bank, self.btok[:, i, g, :], self.xde[:, g * 512:(g + 1) * 512], start=True,
                              stop=True).then_inc(k.R.full, 1)
        wz = [block(), block()]
        for i in range(NT):
            for n in range(2):
                bank, free = k.A.fill()
                pe.wait_ge(k.A.free, free)
                for c in range(KD):
                    mm = pe.matmul(bank, self.uT[:, c, i * P:(i + 1) * P], wz[n][:, c, :], start=c == 0,
                                   stop=c == KD - 1)
                    k.W.first(mm)
                mm.then_inc(k.A.full, 1)
        k.W.owed += 2
        for i in range(NT):
            pe.wait_ge(self.normed, i + 1)
            for half in range(2):
                bank, free = k.R.fill()
                pe.wait_ge(k.R.free, free)
                for a in range(4):
                    c = 4 * half + a
                    mm = pe.transpose(bank[:, a * P:(a + 1) * P], self.xs[:, i, c * P:(c + 1) * P], k.c("ident"))
                    k.W.first(mm)
                mm.then_inc(k.R.full, 1)
        pe.wait_ge(k.R.free, k.R.all())
        project_rows(k, pe, [self.mixT[:, c, :] for c in range(MIXT)])

    def act(self, act):
        k = self.k
        self.norm.act(act)
        for m in range(4):
            bank, full = k.A.empty()
            act.wait_ge(k.A.full, full)
            if m >= 2:
                act.wait_ge(k.R.free, k.R.stored(self.r0 + 8 + 2 * (m - 2) + 1))
            act.activation(self.cg[:, m % 2, :], bank, ACT.Copy).then_inc(k.A.free, 1)
        w, b = k.s("ssm_conv"), k.s("ssm_convb")

        def silu(m):
            act.wait_ge(self.conv, m + 1)
            if 2 <= m < 10:
                act.wait_ge(k.R.full, self.r0 + 16 + m - 2 + 1)
            dst = self.sil[:, m % 2, :] if m < 8 else self.bc[:, m - 8, :]
            act.activation(dst, self.acc[:, m % 2, :], ACT.Silu).then_inc(self.silu, 1)

        act.wait_ge(self.pads, 2)
        for m in range(12):
            bank, full = k.A.empty()
            act.wait_ge(k.A.full, full)
            if m >= 2:
                act.wait_ge(self.silu, m - 1)
            act.activation(self.xpad[:, m % 2, 3:3 + SEQ], bank, ACT.Copy)
            act.activation(self.acc[:, m % 2, :], bank, ACT.Identity, bias=b[:, m:m + 1],
                           scale=w[:, 4 * m + 3:4 * m + 4]).then_inc(k.A.free, 1)
            if m:
                silu(m - 1)
        silu(11)
        act.activation(self.ea, k.s("a_log"), ACT.Exp).then_inc(self.dte_out, 1)
        act.wait_ge(self.dte_in, 1)
        softplus_tail(act, self.t0, self.dt, self.dte_out, 1)
        act.wait_ge(self.cexp, 1)
        act.activation(self.ecum, self.cum, ACT.Exp).then_inc(self.dte_out, 1)
        act.activation(self.etot, self.tot, ACT.Exp).then_inc(self.dte_out, 1)
        act.wait_ge(self.cexp, 2)
        act.activation(self.toend, self.t1, ACT.Exp).then_inc(self.dte_out, 1)
        for n in range(4 * NT):
            bank, full = k.A.empty()
            act.wait_ge(k.A.full, full)
            act.activation(self.E[:, n % 2, :], bank, ACT.Exp).then_inc(k.A.free, 1)
        for i in range(NT):
            for n in range(2):
                bank, full = k.A.empty()
                act.wait_ge(k.A.full, full)
                if n == 0:
                    act.wait_ge(self.gated, max(i - 1, 0) + 1)
                act.activation(self.zs[:, i % 2, n * 512:(n + 1) * 512], bank, ACT.Silu).then_inc(k.A.free, 1)
            if i:
                self.square(act, i - 1)
        self.square(act, NT - 1)
        act.wait_ge(self.sq_free, 1)
        act.activation(k.stat[:, 24:32], k.stat[:, 16:24], ACT.Sqrt).then_inc(self.roots, 1)

    def square(self, act, i):
        k = self.k
        act.wait_ge(self.gated, i + 2)
        for g in range(SSM_G):
            if 2 * i + g:
                act.wait_ge(self.sums, 2 * i + g)
            act.activation(self.junk, self.xs[:, i, g * 512:(g + 1) * 512], ACT.Square,
                           accum_out=self.gsum[:, 2 * i + g:2 * i + g + 1]).then_inc(self.sums, 1)

    def dve(self, dve):
        k = self.k
        link = k.dlink
        self.norm.dve(dve)
        w = k.s("sc_conv")
        dve.memset(self.pad3[:, :, 0:2], 0.0).then_inc(self.pads, 1)
        dve.memset(self.xpad[:, :, 0:3], 0.0).then_inc(self.pads, 1)
        dve.wait_ge(self.pads, 2)
        for m in range(4):
            b = m % 2
            bank, full = k.R.empty()
            dve.wait_ge(k.R.full, full)
            dve.wait_ge(k.A.free, k.A.stored(self.a0 + m + 1))
            dve.tensor_tensor(self.pad3[:, b, 2:2 + SEQ], self.cg[:, b, :], bank, ALU.mult).then_inc(k.R.free, 1)
            dve.wait_ge(k.R.free, k.R.stored(k.R.emptied))
            link(dve.tensor_scalar(self.acc3[:, b, :], self.pad3[:, b, 0:SEQ], w[:, 3 * m:3 * m + 1], None, ALU.mult))
            for j in (1, 2):
                link(dve.scalar_tensor_tensor(self.acc3[:, b, :], self.pad3[:, b, j:j + SEQ],
                                              w[:, 3 * m + j:3 * m + j + 1], self.acc3[:, b, :], ALU.mult, ALU.add))
            bank, full = k.R.empty()
            dve.wait_ge(k.R.full, full)
            dve.tensor_tensor(self.mixT[:, m, :], self.acc3[:, b, :], bank, ALU.mult).then_inc(k.R.free, 1)
        w = k.s("ssm_conv")

        def store(m):
            bank, full = k.R.empty()
            dve.wait_ge(k.R.full, full)
            dst = self.xs[:, :, m * P:(m + 1) * P] if m < 8 else self.btok[:, :, m - 8, :]
            dve.tensor_copy(dst, bank.rearrange("p (i f) -> p i f", i=NT)).then_inc(k.R.free, 1)

        for m in range(12):
            dve.wait_ge(k.A.free, k.A.stored(self.a0 + 4 + m + 1))
            for j in range(3):
                ins = dve.scalar_tensor_tensor(self.acc[:, m % 2, :], self.xpad[:, m % 2, j:j + SEQ],
                                               w[:, 4 * m + j:4 * m + j + 1], self.acc[:, m % 2, :], ALU.mult, ALU.add)
                if j < 2:
                    link(ins)
                else:
                    ins.then_inc(self.conv, 1)
            if m >= 2:
                store(m - 2)
        bank, full = k.R.empty()
        dve.wait_ge(k.R.full, full)
        bias = k.s("dt_bias").unsqueeze(1).broadcast_to([P, NT, SSM_H])
        dve.tensor_tensor(self.dt, bank[:, 0:64].rearrange("p (i h) -> p i h", i=NT), bias,
                          ALU.add).then_inc(k.R.free, 1)
        dve.wait_ge(k.R.free, k.R.stored(k.R.emptied))
        dve.sem_inc(self.dte_in, 1)
        dve.wait_ge(self.dte_out, 4)
        link(dve.scalar_tensor_tensor(self.dt, self.dt, 0.0, self.t0, ALU.max, ALU.add))
        ea = self.ea.unsqueeze(1).broadcast_to([P, NT, SSM_H])
        dve.scalar_tensor_tensor(self.adt, self.dt, -1.0, ea, ALU.mult, ALU.mult).then_inc(self.dt_first, 1)
        bank, full = k.R.empty()
        dve.wait_ge(k.R.full, full)
        link(dve.tensor_copy(self.cum, bank[:, 0:64].rearrange("p (i h) -> p i h", i=NT)))
        dve.tensor_copy(self.tot, bank[:, 64:128].rearrange("p (i h) -> p i h", i=NT)).then_inc(k.R.free, 1)
        dve.wait_ge(k.R.free, k.R.stored(k.R.emptied))
        link(dve.tensor_tensor(self.t1, self.tot, self.cum, ALU.subtract))
        dve.sem_inc(self.cexp, 2)
        dve.wait_ge(self.dte_out, 7)
        dve.tensor_tensor(self.dte, self.dt, self.toend, ALU.mult).then_inc(self.dt_ready, 1)
        upper = k.c("upper").unsqueeze(1).broadcast_to([P, SSM_G, P])
        for i in range(NT):
            bank, full = k.R.empty()
            dve.wait_ge(k.R.full, full)
            dve.tensor_tensor(self.cb, bank[:, 0:256].rearrange("p (g t) -> p g t", g=2), upper,
                              ALU.mult).then_inc(k.R.free, 1)
            dve.wait_ge(k.R.free, k.R.stored(k.R.emptied))

            def weigh(hb):
                n = 4 * i + hb
                dve.wait_ge(k.A.free, k.A.stored(self.a0 + 16 + n + 1))
                e = self.E[:, n % 2, :].rearrange("p (h t) -> p h t", h=4)
                cb = self.cb[:, hb // 2, :].unsqueeze(1).broadcast_to([P, 4, P])
                dve.tensor_tensor(e, e, cb, ALU.mult).then_inc(self.w_ready, 1)

            weigh(0)
            weigh(1)
            if i:
                for g in range(SSM_G):
                    bank, full = k.R.empty()
                    dve.wait_ge(k.R.full, full)
                    dve.tensor_tensor(self.off[g].rearrange("p (h d) -> p h d", h=8),
                                      bank.rearrange("p (h d) -> p h d", h=8),
                                      spread(self.ecum[:, i, 8 * g:8 * g + 8], SSM_P), ALU.mult).then_inc(k.R.free, 1)
                dve.wait_ge(k.R.free, k.R.stored(k.R.emptied))
            weigh(2)
            weigh(3)
            dve.wait_ge(self.x_ready, 3 * i + 3)
            for g in range(SSM_G):
                xs = self.xs[:, i, g * 512:(g + 1) * 512]
                if i:
                    link(dve.tensor_tensor(xs, xs, self.off[g], ALU.add))
                bank, full = k.R.empty()
                dve.wait_ge(k.R.full, full)
                dve.tensor_tensor(xs, xs, bank, ALU.add).then_inc(k.R.free, 1)
            if i < NT - 1:
                for g in range(SSM_G):
                    st = self.state[:, g, :]
                    if i:
                        s3 = st.rearrange("p (h d) -> p h d", h=8)
                        link(dve.tensor_tensor(s3, s3, spread(self.etot[:, i, 8 * g:8 * g + 8], SSM_P), ALU.mult))
                    bank, full = k.R.empty()
                    dve.wait_ge(k.R.full, full)
                    if i:
                        dve.tensor_tensor(st, st, bank, ALU.add).then_inc(k.R.free, 1)
                    else:
                        dve.tensor_copy(st, bank).then_inc(k.R.free, 1)
                dve.wait_ge(k.R.free, k.R.stored(k.R.emptied))
                dve.sem_inc(self.state_ready, 2)
        dve.wait_ge(k.R.free, k.R.stored(k.R.emptied))
        dve.sem_inc(self.gated, 1)
        for i in range(NT):
            dve.wait_ge(k.A.free, k.A.stored(self.a0 + 32 + 2 * i + 2))
            dve.tensor_tensor(self.xs[:, i, :], self.xs[:, i, :], self.zs[:, i % 2, :], ALU.mult).then_inc(self.gated, 1)
        dve.wait_ge(self.sums, 2 * NT)
        dve.tensor_scalar(k.stat[:, 16:24], self.gsum, SSM_G / SSM_INNER, EPS, ALU.mult,
                          ALU.add).then_inc(self.sq_free, 1)
        dve.wait_ge(self.roots, 1)
        link(dve.reciprocal(k.stat[:, 32:40], k.stat[:, 24:32]))
        for i in range(NT):
            y = self.xs[:, i, :].rearrange("p (g d) -> p g d", g=2)
            dve.tensor_tensor(y, y, spread(k.stat[:, 32 + 2 * i:34 + 2 * i], 512), ALU.mult).then_inc(self.normed, 1)
        for i in range(NT):
            for half in range(2):
                bank, full = k.R.empty()
                dve.wait_ge(k.R.full, full)
                dve.tensor_tensor(self.mixT[:, 4 + 4 * half:8 + 4 * half, i * P:(i + 1) * P],
                                  bank.rearrange("p (a t) -> p a t", a=4),
                                  spread(k.s("ssm_norm")[:, 4 * half:4 * half + 4], P), ALU.mult).then_inc(k.R.free, 1)
        add_rows(k, dve)


def softplus_tail(act, x, src, done, base):
    act.activation(x, src, ACT.Abs).then_inc(done, 1)
    act.wait_ge(done, base + 1)
    act.activation(x, x, ACT.Exp, scale=-1.0).then_inc(done, 1)
    act.wait_ge(done, base + 2)
    act.activation(x, x, ACT.Ln, bias=1.0).then_inc(done, 1)



def over_heads(m, n=4):
    return m.unsqueeze(1).broadcast_to([P, n, m.shape[1]])


class Odd:

    A_HALF = 12 + 8 + 4 * 18 + 4
    R_HALF = 12 + 4 * 9 + 3 + 3 + 4
    A_JOBS = 2 * A_HALF + 12 + 8 * 5
    R_JOBS = 8 + 2 + 2 * R_HALF + 32 + 8

    def __init__(self, k):
        self.k = k
        self.uT = k.at(0, 4096, k=KD)
        self.mixT = k.at(4096, 6144, k=MIXT)
        self.norm = Norm(k, lambda i: k.h[:, i, :], NT, k.s("g_mix1"), self.uT)
        self.qT = k.at(10240, 2048, h=4)
        self.kT = k.at(12288, 2048, h=4)
        self.ktok = k.at(14336, 2048, i=NT)
        self.vtok = k.at(16384, 2048, i=NT)
        self.qtok = k.at(6144, 2048, i=NT)
        self.xpad = k.at(18432, 2 * 516, b=2)
        self.acc = k.at(19464, 1024, b=2)
        self.sil = k.at(8192, 1024, b=2)
        self.sqr = k.at(9216, 1024, b=2)
        self.b = [k.at(8192 + 512 * j, 512, h=4) for j in range(4)] + [k.at(18432 + 512 * j, 512, h=4) for j in range(5)]
        per = lambda j: k.decays[:, 32 * j:32 * j + 32].rearrange("p (i h) -> p i h", i=NT)
        self.g, self.beta, self.egl, self.etot = per(0), per(1), per(2), per(3)
        tmp = lambda j: k.at(8192 + 32 * j, 32, i=NT)
        self.araw, self.braw, self.t0, self.cum, self.ebeta, self.den = [tmp(j) for j in range(6)]
        self.ea = k.at(8192 + 32 * 6, GH)
        self.sq = k.at(10240, 2048, m=4)
        self.sk = k.at(12288, 2048, m=4)
        self.sv = k.at(14336, 2048, i=NT)
        self.sp_ = k.at(16384, 1280)
        self.lg = k.at(17664, 2560, b=2)
        s = lambda n: k.sem(f"gdn_{n}")
        self.pads, self.conv, self.silu = s("pads"), s("convolved"), s("silu")
        self.gin, self.gout, self.gready, self.cin = s("gates_in"), s("gates_out"), s("decays_ready"), s("cum_in")
        self.squares, self.ssum, self.means, self.roots, self.recip, self.scaled = (
            s("squares"), s("square_sums"), s("means"), s("roots"), s("reciprocals"), s("scaled"))
        self.seg, self.edec, self.dmask, self.tinit, self.lmask, self.kd, self.rhs, self.done = (
            s("segments_in"), s("decayed_qk"), s("decay_masked"), s("inverse_begun"), s("level_masked"), s("k_decayed"),
            s("rhs_ready"), s("chunk_done"))
        self.gatedz = s("gated")
        t = lambda n: k.sem(f"stick_{n}")
        self.sa, self.ssp, self.sw, self.swm = t("softplus"), t("softplus_masked"), t("weights"), t("weights_masked")

    def loads(self):
        w = self.k.dram["od_w_in"][0]
        cols = []
        for hf in range(2):
            cols += [512 * hf, 1024 + 512 * hf, 2048 + 512 * hf, 3072 + 512 * hf]
        base = 4 * GH * GDK + 2 * GH
        cols += [base, base + 512, base + 1024]
        for c in cols:
            yield w[:, c:c + 512].rearrange("(k p) n -> p k n", p=P)
        for j in range(3):
            yield self.k.dram["od_w_out"][0][j * 512:(j + 1) * 512, :].rearrange("(k p) n -> p k n", p=P)

    def sp(self, sp):
        load_weights(self.k, sp, self.loads())

    def half_a(self, hf):
        return self.a0 + hf * self.A_HALF

    def half_r(self, hf):
        return self.r0 + 10 + hf * self.R_HALF

    def chunk_a(self, hf, c):
        return self.half_a(hf) + 20 + 18 * c

    def chunk_r(self, hf, c):
        return self.half_r(hf) + 12 + 9 * c + max(c - 1, 0) + c

    def pe(self, pe):
        k = self.k
        self.norm.pe(pe)
        pe.wait_ge(k.R.free, k.R.all())
        bank, free = k.R.fill()
        pe.wait_ge(k.R.free, free)
        wab = k.s("w_ab").rearrange("p (k n) -> p k n", k=KD)
        for i in range(NT):
            for c in range(KD):
                mm = pe.matmul(bank[:, i * 16:(i + 1) * 16], self.uT[:, c, i * P:(i + 1) * P], wab[:, c, :],
                               start=c == 0, stop=c == KD - 1)
        mm.then_inc(k.R.full, 1)
        bank, free = k.R.fill()
        pe.wait_ge(k.R.free, free)
        pe.wait_ge(self.cin, 1)
        g = self.g.rearrange("p i h -> p (i h)")
        pe.matmul(bank[:, 0:32], k.c("upper"), g, start=True, stop=True)
        pe.matmul(bank[:, 32:64], k.c("ones"), g, start=True, stop=True).then_inc(k.R.full, 1)
        for hf in range(2):
            self.pe_project(pe, hf)
            for c in range(NT):
                self.pe_chunk(pe, hf, c)
            self.pe_gate(pe, hf)
        self.pe_stick(pe)
        project_rows(k, pe, [self.mixT[:, c, :] for c in range(MIXT)])

    def block(self, pe):
        w, full, got = self.k.W.take()
        pe.wait_ge(full, got)
        return w.rearrange("p (k n) -> p k n", k=KD)

    def columns(self, pe, w, m):
        k = self.k
        bank, free = k.A.fill()
        pe.wait_ge(k.A.free, free)
        for c in range(KD):
            mm = pe.matmul(bank, w[:, c, m * P:(m + 1) * P], self.uT[:, c, :], start=c == 0, stop=c == KD - 1)
            k.W.first(mm)
        mm.then_inc(k.A.full, 1)

    def rows(self, pe, w, i):
        k = self.k
        bank, free = k.A.fill()
        pe.wait_ge(k.A.free, free)
        for c in range(KD):
            mm = pe.matmul(bank, self.uT[:, c, i * P:(i + 1) * P], w[:, c, :], start=c == 0, stop=c == KD - 1)
            k.W.first(mm)
        mm.then_inc(k.A.full, 1)

    def four(self, pe, ring, f):
        k = self.k
        bank, free = ring.fill()
        pe.wait_ge(ring.free, free)
        for h in range(4):
            mm = f(bank[:, h * P:(h + 1) * P], h)
        mm.then_inc(ring.full, 1)

    def pe_project(self, pe, hf):
        k = self.k

        def turned(t):
            pe.wait_ge(self.silu, 12 * hf + t + 1)
            self.four(pe, k.R, lambda out, i: pe.transpose(out, self.sil[:, t % 2, i * P:(i + 1) * P], k.c("ident")))

        for t in range(12):
            if t % 4 == 0:
                w = self.block(pe)
            self.columns(pe, w, t % 4)
            if t % 4 == 3:
                k.W.owed += 1
            if t >= 2:
                turned(t - 2)
        turned(10)
        turned(11)
        for kind, x in enumerate((self.qtok, self.ktok)):
            pe.wait_ge(self.scaled, 8 * hf + 4 * kind + 4)
            for h in range(4):
                self.four(pe, k.A, lambda out, i: pe.transpose(out, x[:, i, h * P:(h + 1) * P], k.c("ident")))

    def pe_chunk(self, pe, hf, c):
        k, n, b = self.k, 4 * hf + c, self.b
        tok = slice(c * P, (c + 1) * P)
        flat = lambda x: x.rearrange("p h t -> p (h t)")
        pe.wait_ge(k.A.free, k.A.all())
        for lhs, rhs in ((k.c("upper"), b[1]), (k.c("ones"), b[0])):
            bank, free = k.A.fill()
            pe.wait_ge(k.A.free, free)
            pe.wait_ge(self.seg, 2 * n + 2)
            pe.matmul(bank, lhs, flat(rhs), start=True, stop=True).then_inc(k.A.full, 1)
        self.four(pe, k.R, lambda out, h: pe.matmul(out, self.kT[:, h, tok], self.kT[:, h, tok], start=True, stop=True))
        self.four(pe, k.R, lambda out, h: pe.matmul(out, self.qT[:, h, tok], self.kT[:, h, tok], start=True, stop=True))
        pe.wait_ge(k.R.free, k.R.all())
        self.four(pe, k.A, lambda out, h: pe.transpose(out, b[0][:, h, :], k.c("ident")))
        self.four(pe, k.A, lambda out, h: pe.transpose(out, b[2][:, h, :], k.c("ident")))
        pe.wait_ge(self.tinit, n + 1)
        self.four(pe, k.A, lambda out, h: pe.transpose(out, b[6][:, h, :], k.c("ident")))
        for l in range(1, LEVELS):
            pe.wait_ge(self.lmask, 6 * n + l)
            self.four(pe, k.A, lambda out, h: pe.matmul(out, b[2][:, h, :], b[6][:, h, :], start=True, stop=True))
            pe.wait_ge(k.A.free, k.A.all())
            self.four(pe, k.R, lambda out, h: pe.matmul(out, b[7][:, h, :], b[0][:, h, :], start=True, stop=True))
            pe.wait_ge(k.R.free, k.R.all())
            self.four(pe, k.A, lambda out, h: pe.transpose(out, b[6][:, h, :], k.c("ident")))
        if c:
            pe.wait_ge(self.edec, 2 * n + 2)
            pe.wait_ge(self.done, n)
            self.four(pe, k.R, lambda out, h: pe.matmul(out, b[5][:, h, :], b[8][:, h, :], start=True, stop=True))
        pe.wait_ge(k.A.free, k.A.all())
        pe.wait_ge(self.rhs, n + 1)
        self.four(pe, k.A, lambda out, h: pe.matmul(out, b[7][:, h, :], b[6][:, h, :], start=True, stop=True))
        pe.wait_ge(k.A.free, k.A.all())

        def out_rows(out, h):
            if c:
                pe.matmul(out, b[4][:, h, :], b[8][:, h, :], start=True, stop=False)
            return pe.matmul(out, b[3][:, h, :], b[0][:, h, :], start=c == 0, stop=True)

        self.four(pe, k.R, out_rows)
        if c < NT - 1:
            pe.wait_ge(self.kd, n + 1)
            self.four(pe, k.R, lambda out, h: pe.matmul(out, b[1][:, h, :], b[0][:, h, :], start=True, stop=True))

    def pe_gate(self, pe, hf):
        k = self.k
        w = self.block(pe)
        for i in range(NT):
            self.rows(pe, w, i)
        k.W.owed += 1
        for i in range(NT):
            pe.wait_ge(self.gatedz, 4 * hf + i + 1)
            bank, free = k.R.fill()
            pe.wait_ge(k.R.free, free)
            for j in range(4):
                mm = pe.transpose(bank[:, j * P:(j + 1) * P], self.vtok[:, i, j * P:(j + 1) * P], k.c("ident"))
                k.W.first(mm)
            mm.then_inc(k.R.full, 1)

    def width(self, kt):
        return SEQ - kt * P

    def span(self, x, kt):
        at = sum(self.width(j) for j in range(kt))
        return x[:, at:at + self.width(kt)]

    def pe_stick(self, pe):
        k = self.k
        pe.wait_ge(k.R.free, k.R.all())
        for _ in range(2):
            w = self.block(pe)
            for m in range(4):
                self.columns(pe, w, m)
            k.W.owed += 1
        w = self.block(pe)
        for i in range(NT):
            self.rows(pe, w, i)
        k.W.owed += 1
        pe.wait_ge(k.A.free, k.A.all())

        def values(hh):
            pe.wait_ge(self.swm, 4 * hh + 4)
            at = SBD * (hh % 2)
            bank, free = k.A.fill()
            pe.wait_ge(k.A.free, free)
            for kt in range(NT):
                mm = pe.matmul(bank[at:at + SBD, kt * P:SEQ], self.sv[:, kt, hh * SBD:(hh + 1) * SBD],
                               self.span(self.lg[:, hh % 2, :], kt), start=kt == 0, stop=kt == NT - 1)
            mm.then_inc(k.A.full, 1)

        for hh in range(SBH):
            m, at = hh // 2, SBD * (hh % 2)
            for kt in reversed(range(NT)):
                bank, free = k.A.fill()
                pe.wait_ge(k.A.free, free)
                mm = pe.matmul(bank[:, 0:self.width(kt)], self.sk[at:at + SBD, m, kt * P:(kt + 1) * P],
                               self.sq[at:at + SBD, m, kt * P:SEQ], start=True, stop=True)
                mm.then_inc(k.A.full, 1)
            if hh:
                values(hh - 1)
            for j, kt in enumerate(reversed(range(NT))):
                pe.wait_ge(self.ssp, 4 * hh + j + 1)
                bank, free = k.R.fill()
                pe.wait_ge(k.R.free, free)
                for later in range(kt, NT):
                    mm = pe.matmul(bank[:, (later - kt) * P:self.width(kt)],
                                   k.c("lower") if later == kt else k.c("ones"), self.span(self.sp_, later),
                                   start=later == kt, stop=later == NT - 1)
                mm.then_inc(k.R.full, 1)
        values(SBH - 1)
        pe.wait_ge(k.A.free, k.A.all())
        pe.wait_ge(k.R.free, k.R.all())

    def act(self, act):
        k = self.k
        self.norm.act(act)
        act.activation(self.ea, k.s("gdn_alog"), ACT.Exp).then_inc(self.gout, 1)
        act.wait_ge(self.gin, 1)
        softplus_tail(act, self.t0, self.araw, self.gout, 1)
        act.activation(self.ebeta, self.braw, ACT.Exp, scale=-1.0).then_inc(self.gout, 1)
        act.wait_ge(self.gin, 2)
        act.activation(self.egl, self.egl, ACT.Exp).then_inc(self.gout, 1)
        act.activation(self.etot, self.etot, ACT.Exp).then_inc(self.gout, 1)
        for hf in range(2):
            self.act_project(act, hf)
            for c in range(NT):
                self.act_chunk(act, hf, c)
            self.act_gate(act, hf)
        self.act_stick(act)

    def act_project(self, act, hf):
        k = self.k
        w = k.s("gdn_conv")
        act.wait_ge(self.pads, hf + 1)

        def silu(t):
            n = 12 * hf + t
            act.wait_ge(self.conv, n + 1)
            if t >= 2:
                act.wait_ge(k.R.full, self.half_r(hf) + t - 2 + 1)
            act.activation(self.sil[:, t % 2, :], self.acc[:, t % 2, :], ACT.Silu).then_inc(self.silu, 1)

        for t in range(12):
            bank, full = k.A.empty()
            act.wait_ge(k.A.full, full)
            if t >= 2:
                act.wait_ge(self.silu, 12 * hf + t - 1)
            tile = 8 * (t // 4) + 4 * hf + t % 4
            act.activation(self.xpad[:, t % 2, 3:3 + SEQ], bank, ACT.Copy)
            act.activation(self.acc[:, t % 2, :], bank, ACT.Copy,
                           scale=w[:, 4 * tile + 3:4 * tile + 4]).then_inc(k.A.free, 1)
            if t:
                silu(t - 1)
        silu(11)
        act.wait_ge(self.means, 2 * hf + 1)
        act.activation(k.stat[:, 16:48], k.stat[:, 16:48], ACT.Sqrt).then_inc(self.roots, 1)
        for x in (self.qT, self.kT):
            for h in range(4):
                bank, full = k.A.empty()
                act.wait_ge(k.A.full, full)
                act.activation(x[:, h, :], bank, ACT.Copy).then_inc(k.A.free, 1)

    def act_chunk(self, act, hf, c):
        k, n, b = self.k, 4 * hf + c, self.b

        def store(dst, func=ACT.Copy):
            bank, full = k.A.empty()
            act.wait_ge(k.A.full, full)
            act.activation(dst, bank.rearrange("p (h t) -> p h t", h=4), func).then_inc(k.A.free, 1)

        if c:
            act.wait_ge(self.done, n)
        store(b[2], ACT.Exp)
        store(b[3], ACT.Exp)
        store(b[1])
        act.wait_ge(self.edec, 2 * n + 2)
        store(b[3])
        store(b[7])
        for l in range(1, LEVELS):
            store(b[0])
            store(b[7])
        store(b[0])

    def act_gate(self, act, hf):
        k = self.k
        act.wait_ge(self.done, 4 * hf + 4)
        for i in range(NT):
            bank, full = k.A.empty()
            act.wait_ge(k.A.full, full)
            if i >= 2:
                act.wait_ge(self.gatedz, 4 * hf + i - 1)
            act.activation(self.b[4 + i % 2], bank.rearrange("p (h t) -> p h t", h=4), ACT.Silu).then_inc(k.A.free, 1)
            if i == 1:
                act.wait_ge(self.means, 2 * hf + 2)
                act.activation(k.stat[:, 16:32], k.stat[:, 16:32], ACT.Sqrt).then_inc(self.roots, 1)

    def act_stick(self, act):
        k = self.k
        for x, scale in ((self.sq, SBD ** -0.5), (self.sk, 1.0)):
            for m in range(4):
                bank, full = k.A.empty()
                act.wait_ge(k.A.full, full)
                act.activation(x[:, m, :], bank, ACT.Copy, scale=scale).then_inc(k.A.free, 1)
        for i in range(NT):
            bank, full = k.A.empty()
            act.wait_ge(k.A.full, full)
            act.activation(self.sv[:, i, :], bank, ACT.Copy).then_inc(k.A.free, 1)

        def store_values(hh):
            at = SBD * (hh % 2)
            bank, full = k.A.empty()
            act.wait_ge(k.A.full, full)
            act.activation(self.mixT[at:at + SBD, 8 + hh // 2, :], bank[at:at + SBD, :], ACT.Copy).then_inc(k.A.free, 1)

        r0 = self.r0 + 10 + 2 * self.R_HALF
        for hh in range(SBH):
            lg = self.lg[:, hh % 2, :]
            if hh:
                act.wait_ge(k.R.full, r0 + 4 * hh)
            if hh >= 2:
                act.wait_ge(self.swm, 4 * hh - 4)
            for kt in reversed(range(NT)):
                bank, full = k.A.empty()
                act.wait_ge(k.A.full, full)
                act.activation(self.span(self.sp_, kt), bank[:, 0:self.width(kt)], ACT.Abs).then_inc(self.sa, 1)
                act.activation(self.span(lg, kt), bank[:, 0:self.width(kt)], ACT.Copy).then_inc(k.A.free, 1)
            for step in range(2):
                for j, kt in enumerate(reversed(range(NT))):
                    act.wait_ge(self.sa, 12 * hh + 4 * step + j + 1)
                    sp = self.span(self.sp_, kt)
                    if step == 0:
                        act.activation(sp, sp, ACT.Exp, scale=-1.0).then_inc(self.sa, 1)
                    else:
                        act.activation(sp, sp, ACT.Ln, bias=1.0).then_inc(self.sa, 1)
            if hh:
                store_values(hh - 1)
            for j, kt in enumerate(reversed(range(NT))):
                act.wait_ge(k.R.free, k.R.stored(r0 + 4 * hh + j + 1))
                lt = self.span(lg, kt)
                act.activation(lt, lt, ACT.Exp).then_inc(self.sw, 1)
        store_values(SBH - 1)

    def dve(self, dve):
        k, link = self.k, self.k.dlink
        self.norm.dve(dve)
        bank, full = k.R.empty()
        dve.wait_ge(k.R.full, full)
        raw = bank[:, 0:64].rearrange("p (i n) -> p i n", i=NT)
        bias = k.s("gdn_dtb").unsqueeze(1).broadcast_to([P, NT, GH])
        link(dve.tensor_tensor(self.araw, raw[:, :, 0:GH], bias, ALU.add))
        dve.tensor_copy(self.braw, raw[:, :, GH:2 * GH]).then_inc(k.R.free, 1)
        dve.wait_ge(k.R.free, k.R.stored(k.R.emptied))
        dve.sem_inc(self.gin, 1)
        dve.wait_ge(self.gout, 5)
        link(dve.scalar_tensor_tensor(self.t0, self.araw, 0.0, self.t0, ALU.max, ALU.add))
        ea = self.ea.unsqueeze(1).broadcast_to([P, NT, GH])
        dve.scalar_tensor_tensor(self.g, self.t0, -1.0, ea, ALU.mult, ALU.mult).then_inc(self.cin, 1)
        link(dve.tensor_scalar(self.den, self.ebeta, 1.0, None, ALU.add))
        link(dve.reciprocal(self.beta, self.den))
        bank, full = k.R.empty()
        dve.wait_ge(k.R.full, full)
        link(dve.tensor_copy(self.cum, bank[:, 0:32].rearrange("p (i h) -> p i h", i=NT)))
        dve.tensor_copy(self.etot, bank[:, 32:64].rearrange("p (i h) -> p i h", i=NT)).then_inc(k.R.free, 1)
        dve.wait_ge(k.R.free, k.R.stored(k.R.emptied))
        dve.tensor_tensor(self.egl, self.etot, self.cum, ALU.subtract).then_inc(self.gin, 1)
        dve.wait_ge(self.gout, 7)
        dve.sem_inc(self.gready, 1)
        for hf in range(2):
            self.dve_project(dve, hf)
            for c in range(NT):
                self.dve_chunk(dve, hf, c)
            self.dve_gate(dve, hf)
        self.dve_stick(dve)
        add_rows(k, dve)

    def dve_project(self, dve, hf):
        k, link = self.k, self.k.dlink
        w = k.s("gdn_conv")
        dve.memset(self.xpad[:, :, 0:3], 0.0).then_inc(self.pads, 1)
        dve.wait_ge(self.pads, hf + 1)

        def store(t):
            bank, full = k.R.empty()
            dve.wait_ge(k.R.full, full)
            dst = (self.qtok, self.ktok, self.vtok)[t // 4]
            dve.tensor_copy(dst[:, :, (t % 4) * P:(t % 4 + 1) * P],
                            bank.rearrange("p (i f) -> p i f", i=NT)).then_inc(k.R.free, 1)

        for t in range(12):
            dve.wait_ge(k.A.free, k.A.stored(self.half_a(hf) + t + 1))
            tile = 8 * (t // 4) + 4 * hf + t % 4
            for j in range(3):
                ins = dve.scalar_tensor_tensor(self.acc[:, t % 2, :], self.xpad[:, t % 2, j:j + SEQ],
                                               w[:, 4 * tile + j:4 * tile + j + 1], self.acc[:, t % 2, :], ALU.mult,
                                               ALU.add)
                if j < 2:
                    link(ins)
                else:
                    ins.then_inc(self.conv, 1)
            if t >= 2:
                store(t - 2)
        store(10)
        store(11)
        for n in range(8):
            self.reduce_square(dve, 12 * hf + n, k.stat[:, 16 + 4 * n:20 + 4 * n])
        dve.wait_ge(self.ssum, 12 * hf + 8)
        dve.tensor_scalar(k.stat[:, 16:48], k.stat[:, 16:48], EPS, None, ALU.add).then_inc(self.means, 1)
        dve.wait_ge(self.roots, 2 * hf + 1)
        link(dve.reciprocal(k.stat[:, 16:48], k.stat[:, 16:48]))
        dve.tensor_scalar(k.stat[:, 16:32], k.stat[:, 16:32], GDK ** -0.5, None, ALU.mult).then_inc(self.recip, 1)

    def reduce_square(self, dve, n, dst):
        dve.wait_ge(self.squares, n + 1)
        dve.tensor_reduce(dst, self.sqr[:, n % 2, :].rearrange("p (h d) -> p h d", h=4), AX.X,
                          ALU.add).then_inc(self.ssum, 1)

    def dve_chunk(self, dve, hf, c):
        k, n, b, link = self.k, 4 * hf + c, self.b, self.k.dlink
        four = lambda bank: bank.rearrange("p (h t) -> p h t", h=4)
        heads = slice(4 * hf, 4 * hf + 4)
        bank, full = k.R.empty()
        dve.wait_ge(k.R.full, full)
        dve.wait_ge(self.dmask, 2 * n + 2)
        dve.scalar_tensor_tensor(b[0].rearrange("p h t -> p (h t)"), bank, -1.0, b[0].rearrange("p h t -> p (h t)"),
                                 ALU.mult, ALU.mult).then_inc(k.R.free, 1)
        bank, full = k.R.empty()
        dve.wait_ge(k.R.full, full)
        dve.tensor_tensor(b[2], four(bank), b[2], ALU.mult).then_inc(k.R.free, 1)
        for l in range(1, LEVELS):
            bank, full = k.R.empty()
            dve.wait_ge(k.R.full, full)
            if l == 1:
                dve.wait_ge(self.tinit, n + 1)
            dve.tensor_tensor(b[6], b[6], four(bank), ALU.add).then_inc(k.R.free, 1)
            dve.wait_ge(k.R.free, k.R.stored(k.R.emptied))
        dve.wait_ge(k.A.full, self.chunk_a(hf, c) + 17)
        v = self.vtok[:, c, :].rearrange("p (h d) -> p h d", h=4)
        if c:
            bank, full = k.R.empty()
            dve.wait_ge(k.R.full, full)
            dve.tensor_tensor(b[6], v, four(bank), ALU.subtract).then_inc(k.R.free, 1)
            dve.wait_ge(k.R.free, k.R.stored(k.R.emptied))
            v = b[6]
        dve.tensor_tensor(b[6], v, spread(self.beta[:, c, heads], P), ALU.mult).then_inc(self.rhs, 1)
        bank, full = k.R.empty()
        dve.wait_ge(k.R.full, full)
        dve.tensor_copy(self.vtok[:, c, :], bank).then_inc(k.R.free, 1)
        if c < NT - 1:
            if c:
                link(dve.tensor_tensor(b[8], b[8], spread(self.etot[:, c, heads], P), ALU.mult))
            bank, full = k.R.empty()
            dve.wait_ge(k.R.full, full)
            if c:
                dve.tensor_tensor(b[8], b[8], four(bank), ALU.add).then_inc(k.R.free, 1)
            else:
                dve.tensor_copy(b[8], four(bank)).then_inc(k.R.free, 1)
        dve.wait_ge(k.R.free, k.R.stored(k.R.emptied))
        dve.sem_inc(self.done, 1)

    def dve_gate(self, dve, hf):
        k, link = self.k, self.k.dlink
        for i in range(NT):
            self.reduce_square(dve, 12 * hf + 8 + i, k.stat[:, 16 + 4 * i:20 + 4 * i])
        dve.wait_ge(self.ssum, 12 * hf + 12)
        dve.tensor_scalar(k.stat[:, 16:32], k.stat[:, 16:32], 1.0 / GDK, EPS, ALU.mult, ALU.add).then_inc(self.means, 1)
        dve.wait_ge(self.roots, 2 * hf + 2)
        dve.reciprocal(k.stat[:, 16:32], k.stat[:, 16:32]).then_inc(self.recip, 1)
        for i in range(NT):
            bank, full = k.R.empty()
            dve.wait_ge(k.R.full, full)
            dve.tensor_scalar(self.mixT[:, 4 * hf:4 * hf + 4, i * P:(i + 1) * P],
                              bank.rearrange("p (h t) -> p h t", h=4), k.s("gdn_norm"), None,
                              ALU.mult).then_inc(k.R.free, 1)

    def dve_stick(self, dve):
        k, link = self.k, self.k.dlink
        mask = k.c("supper")
        for hh in range(SBH):
            lg = self.lg[:, hh % 2, :]
            for j, kt in enumerate(reversed(range(NT))):
                dve.wait_ge(self.sa, 12 * hh + 8 + j + 1)
                sp, lt = self.span(self.sp_, kt), self.span(lg, kt)
                link(dve.scalar_tensor_tensor(sp, lt, 0.0, sp, ALU.max, ALU.add))
                dve.tensor_tensor(sp[:, 0:P], sp[:, 0:P], mask, ALU.mult).then_inc(self.ssp, 1)
            for kt in reversed(range(NT)):
                lt = self.span(lg, kt)
                bank, full = k.R.empty()
                dve.wait_ge(k.R.full, full)
                dve.tensor_tensor(lt, lt, bank[:, 0:self.width(kt)], ALU.subtract).then_inc(k.R.free, 1)
            for j, kt in enumerate(reversed(range(NT))):
                dve.wait_ge(self.sw, 4 * hh + j + 1)
                lt = self.span(lg, kt)
                dve.scalar_tensor_tensor(lt[:, 0:P], lt[:, 0:P], 1.0, mask, ALU.min, ALU.mult).then_inc(self.swm, 1)

    def pool(self, pool):
        k = self.k
        for hf in range(2):
            xs = ((self.qtok, k.stat[:, 16:32]), (self.ktok, k.stat[:, 32:48]))
            for kind, (x, _) in enumerate(xs):
                for i in range(NT):
                    n = 12 * hf + 4 * kind + i
                    if i == 0:
                        pool.wait_ge(k.R.free, k.R.stored(self.half_r(hf) + 4 * kind + 4))
                    self.square(pool, n, x[:, i, :])
            pool.wait_ge(self.recip, 2 * hf + 1)
            for kind, (x, r) in enumerate(xs):
                for i in range(NT):
                    xi = x[:, i, :].rearrange("p (h d) -> p h d", h=4)
                    pool.tensor_tensor(xi, xi, spread(r[:, 4 * i:4 * i + 4], P), ALU.mult).then_inc(self.scaled, 1)
            pool.wait_ge(self.gready, 1)
            for c in range(NT):
                self.pool_chunk(pool, hf, c)
            pool.wait_ge(self.done, 4 * hf + 4)
            for i in range(NT):
                self.square(pool, 12 * hf + 8 + i, self.vtok[:, i, :])
            pool.wait_ge(self.recip, 2 * hf + 2)
            for i in range(NT):
                o = self.vtok[:, i, :].rearrange("p (h d) -> p h d", h=4)
                k.plink(pool.tensor_tensor(o, o, spread(k.stat[:, 16 + 4 * i:20 + 4 * i], P), ALU.mult))
                pool.wait_ge(k.A.free, k.A.stored(self.half_a(hf) + 92 + i + 1))
                pool.tensor_tensor(o, o, self.b[4 + i % 2], ALU.mult).then_inc(self.gatedz, 1)

    def square(self, pool, n, x):
        if n >= 2:
            pool.wait_ge(self.ssum, n - 1)
        pool.tensor_tensor(self.sqr[:, n % 2, :], x, x, ALU.mult).then_inc(self.squares, 1)

    def pool_chunk(self, pool, hf, c):
        k, n, b = self.k, 4 * hf + c, self.b
        tok = slice(c * P, (c + 1) * P)
        heads = slice(4 * hf, 4 * hf + 4)
        g = spread(self.g[:, c, heads], P)
        a0 = self.chunk_a(hf, c)
        if c:
            pool.wait_ge(self.done, n)
        else:
            pool.wait_ge(self.ssum, 12 * hf + 8)
            pool.wait_ge(k.A.free, k.A.stored(a0))
        pool.tensor_tensor(b[0], over_heads(k.c("upper")), g, ALU.mult).then_inc(self.seg, 1)
        pool.tensor_tensor(b[1], over_heads(k.c("slower")), g, ALU.mult).then_inc(self.seg, 1)
        pool.wait_ge(k.A.free, k.A.stored(a0 + 2))
        link = k.plink
        link(pool.tensor_tensor(b[0], b[2], over_heads(k.c("slower")), ALU.mult))
        pool.tensor_tensor(b[0], b[0], spread(self.beta[:, c, heads], P), ALU.mult).then_inc(self.dmask, 1)
        pool.tensor_tensor(b[2], b[2], over_heads(k.c("lower")), ALU.mult).then_inc(self.dmask, 1)
        pool.tensor_tensor(b[4], self.qT[:, :, tok], b[3], ALU.mult).then_inc(self.edec, 1)
        pool.tensor_tensor(b[5], self.kT[:, :, tok], b[3], ALU.mult).then_inc(self.edec, 1)
        pool.wait_ge(k.R.free, k.R.stored(self.chunk_r(hf, c) + 1))
        link(pool.tensor_tensor(b[6], b[0], over_heads(k.c("below0")), ALU.mult))
        pool.tensor_tensor(b[6], b[6], over_heads(k.c("ident")), ALU.add).then_inc(self.tinit, 1)
        for l in range(1, LEVELS):
            if l == 1:
                pool.wait_ge(k.A.free, k.A.stored(a0 + 4))
            else:
                pool.wait_ge(k.A.full, a0 + 5 + 2 * (l - 2) + 1)
            m = k.c("belowT")[:, (l - 1) * P:l * P]
            pool.tensor_tensor(b[2], b[1], over_heads(m), ALU.mult).then_inc(self.lmask, 1)
        pool.wait_ge(self.lmask, 6 * n + 6)
        kt = self.ktok[:, c, :].rearrange("p (h d) -> p h d", h=4)
        pool.tensor_tensor(b[1], kt, spread(self.egl[:, c, heads], P), ALU.mult).then_inc(self.kd, 1)


def stages(k, which):
    out = []
    for name in which:
        if name == "xa0" or name == "xa1":
            st = CrossAttention(k, int(name[-1]))
        elif name == "moe0" or name == "moe1":
            st = Moe(k, int(name[-1]))
        elif name == "even":
            st = Even(k)
        elif name == "odd":
            st = Odd(k)
        else:
            st = Store(k)
        out.append(st)
    return out


STAGES = ("even", "xa0", "moe0", "odd", "xa1", "moe1", "store")


def build_program(nc, dram, consts, small, which=STAGES):
    with ExitStack() as ctx:
        k = Core(nc, ctx, dram, consts, small)
        k.stat = ctx.enter_context(nc.sbuf_tensor("stat", [P, 64], F32))[:, :]
        k.npass = ctx.enter_context(nc.sbuf_tensor("npass", [P, 2], I32))[:, :]
        k.decays = ctx.enter_context(nc.sbuf_tensor("decays", [P, 128], F32))[:, :]
        k.dlink = k.alink = k.plink = None
        plan = stages(k, which)
        a = r = 0
        for st in plan:
            st.a0, st.r0 = a, r
            a, r = a + st.A_JOBS, r + st.R_JOBS
        ready = k.sem("inputs_ready")
        primed = k.sem("zeroed")
        dchain, achain, pchain = k.sem("dve_chain"), k.sem("act_chain"), k.sem("pool_chain")
        block = ctx.enter_context(nc.Block())

        def between(eng, n):
            eng.drain().then_inc(k.stage_ends, 1)
            eng.wait_ge(k.stage_ends, 4 * n)

        @block.sync
        def _(sp):
            sp.dma_start(k.h, dram["x"][0].rearrange("(i p) d -> p i d", p=P)).then_inc(ready, 16)
            sp.dma_start(k.smallbuf[:, :], dram["small"]).then_inc(ready, 16)
            sp.dma_start(k.constbuf[:, :], dram["consts"]).then_inc(ready, 16)
            for st in plan:
                st.sp(sp)

        @block.gpsimd
        def _(pool):
            k.plink = Links(pool, pchain)
            pool.wait_ge(ready, 48)
            for n, st in enumerate(plan):
                if n:
                    between(pool, n)
                st.pool(pool)

        @block.tensor
        def _(pe):
            pe.sem_inc(k.W.free, WSLOTS)
            pe.wait_ge(ready, 48)
            for n, st in enumerate(plan):
                if n:
                    between(pe, n)
                assert (k.A.filled, k.R.filled) == (st.a0, st.r0), (n, k.A.filled, st.a0, k.R.filled, st.r0)
                st.pe(pe)

        @block.scalar
        def _(act):
            k.alink = Links(act, achain)
            act.sem_inc(k.A.free, len(k.A.banks))
            act.wait_ge(ready, 48)
            for n, st in enumerate(plan):
                if n:
                    between(act, n)
                assert k.A.emptied == st.a0, (n, k.A.emptied, st.a0)
                st.act(act)

        @block.vector
        def _(dve):
            k.dlink = Links(dve, dchain)
            dve.sem_inc(k.R.free, len(k.R.banks))
            for name in ("pair", "more0", "more1"):
                if f"{name}_sc_added" in k.sems:
                    dve.sem_inc(k.sem(f"{name}_sc_added"), 2)
            dve.wait_ge(ready, 48)
            for n, st in enumerate(plan):
                if n:
                    between(dve, n)
                assert k.R.emptied == st.r0, (n, k.R.emptied, st.r0)
                st.dve(dve)


WHICH = STAGES
BIG = ("x", "mem", "xa_wq", "xa_wk", "xa_wv", "xa_wo", "moe_w_gate", "moe_w_up", "moe_w_down", "ev_w_in",
       "ev_w_out", "od_w_in", "od_w_out")


def kernel(**inputs):
    import concourse.bacc as bacc
    from concourse.bass_utils import run_bass_kernel_spmd as run

    nc = bacc.Bacc("TRN2", target_bir_lowering=False, num_devices=1)
    consts, small = constant_columns(), small_columns(inputs)
    arrays = {name: np.ascontiguousarray(inputs[name]) for name in BIG}
    arrays["consts"], arrays["small"] = consts[0], small[0]
    arrays["final_gain"] = np.ascontiguousarray(on_every_row(inputs["final_norm"]))
    dram = {name: nc.dram_tensor(f"in_{name}", a.shape, mybir.dt.from_np(a.dtype), kind="ExternalInput").ap()
            for name, a in arrays.items()}
    dram["out"] = nc.dram_tensor("out", (1, SEQ, D), F32, kind="ExternalOutput").ap()
    build_program(nc, dram, consts, small, WHICH)
    r = run(nc, [{f"in_{name}": a for name, a in arrays.items()}], core_ids=[0])
    return r.results[0]["out"]
```

```python
from contextlib import ExitStack

import numpy as np
import concourse.bass as bass
from concourse import mybir

F32, I32, BF16 = mybir.dt.float32, mybir.dt.int32, mybir.dt.bfloat16
ALU = mybir.AluOpType
ACT = mybir.ActivationFunctionType
AX = mybir.AxisListType

P = 128
D = 1024
KD = D // P
SEQ = 512
NT = SEQ // P
MEM = 256
NM = MEM // P
EPS = 1e-6
SC = 512
SSM_H, SSM_P, SSM_G, SSM_N = 16, 64, 2, 128
SSM_INNER = SSM_H * SSM_P
XBC = SSM_INNER + 2 * SSM_G * SSM_N
GH, GDK = 8, 128
SBH, SBD = 8, 64
XH = 4
NE, NG, EPG = 32, 4, 8
FF = 512
CAP = 64
NPASS = SEQ // CAP
PAIRS = NE // 2
WSLOTS = 6
BLK = 4096
MIXT = 12
LEVELS = 7


def constant_columns():
    r = np.arange(P)
    a, b = r[:, None], r[None, :]
    cols = {
        "ident": a == b,
        "upper": a <= b,
        "lower": a >= b,
        "slower": a > b,
        "supper": a < b,
        "ones": np.ones((P, P)),
    }
    below = []
    for l in range(LEVELS):
        s = 1 << l
        m = (a // (2 * s) == b // (2 * s)) & ((a // s) % 2 == 1) & ((b // s) % 2 == 0)
        below.append(m)
    cols["below0"] = below[0]
    cols["belowT"] = np.concatenate([m.T for m in below[1:]], 1)
    cols["iota"] = np.broadcast_to(np.arange(CAP), (P, CAP))
    cols["prio"] = np.broadcast_to(EPG - np.arange(EPG), (P, EPG))
    cols["limits"] = np.broadcast_to(CAP * np.arange(1, NPASS), (P, NPASS - 1))
    return pack(cols)


def pack(cols):
    at, parts, where = 0, [], {}
    for name, c in cols.items():
        c = np.ascontiguousarray(c, dtype=np.float32)
        where[name] = (at, c.shape[1])
        at += c.shape[1]
        parts.append(c)
    return np.concatenate(parts, 1), where


def feature_major(v):
    v = np.asarray(v)
    v = v.reshape(-1, v.shape[-1] // P, P)
    return v.transpose(2, 1, 0).reshape(P, -1)


def on_every_row(v):
    v = np.asarray(v).reshape(1, -1)
    return np.broadcast_to(v, (P, v.shape[1]))


def weight_tiles(w):
    w = np.asarray(w)
    return w.reshape(KD, P, -1).transpose(1, 0, 2).reshape(P, -1)


def small_columns(i):
    cols = {"g_mem": feature_major(i["mem_norm"])}
    for l in range(2):
        cols[f"g_mix{l}"] = feature_major(i["norm_mix"][l])
        cols[f"g_xa{l}"] = feature_major(i["norm_xa"][l])
        cols[f"g_ffn{l}"] = feature_major(i["norm_ffn"][l])
        cols[f"w_route{l}"] = weight_tiles(np.concatenate([i["moe_w_group"][l], i["moe_w_expert"][l]], 1))
        cols[f"b_route{l}"] = on_every_row(np.concatenate([i["moe_b_group"][l], i["moe_b_expert"][l]]))
    dt0 = 3 * SC + SSM_INNER + XBC
    cols["w_dt"] = weight_tiles(i["ev_w_in"][0][:, dt0:dt0 + SSM_H])
    ab0 = 4 * GH * GDK
    cols["w_ab"] = weight_tiles(i["od_w_in"][0][:, ab0:ab0 + 2 * GH])
    cols["sc_conv"] = feature_major(i["ev_sc_conv"][0])
    cols["ssm_conv"] = feature_major(i["ev_ssm_conv_w"][0])
    cols["ssm_convb"] = feature_major(i["ev_ssm_conv_b"][0])
    cols["gdn_conv"] = feature_major(i["od_gdn_conv"][0])
    cols["ssm_norm"] = feature_major(i["ev_ssm_norm"][0])
    cols["gdn_norm"] = feature_major(i["od_gdn_norm"][0])
    cols["dt_bias"] = on_every_row(i["ev_ssm_dt_bias"][0])
    cols["a_log"] = on_every_row(i["ev_ssm_a_log"][0])
    cols["d_skip"] = on_every_row(i["ev_ssm_d"][0])
    cols["gdn_dtb"] = on_every_row(i["od_gdn_dt_bias"][0])
    cols["gdn_alog"] = on_every_row(i["od_gdn_a_log"][0])
    return pack(cols)


class Ring:

    def __init__(self, banks, full, free):
        self.banks, self.full, self.free = banks, full, free
        self.filled = self.emptied = 0

    def fill(self):
        n = self.filled
        self.filled += 1
        return self.banks[n % len(self.banks)], n + 1

    def empty(self):
        n = self.emptied
        self.emptied += 1
        return self.banks[n % len(self.banks)], n + 1

    def all(self):
        return self.stored(self.filled)

    def stored(self, n):
        return n + len(self.banks)


class Links:

    def __init__(self, eng, sem):
        self.eng, self.sem, self.n = eng, sem, 0

    def __call__(self, ins):
        self.n = self.n + 1
        ins.then_inc(self.sem, 1)
        self.eng.wait_ge(self.sem, self.n)
        return ins


class Weights:

    def __init__(self, slots, full, free):
        self.slots, self.full, self.free = slots, full, free
        self.loaded = self.taken = self.owed = 0

    def first(self, mm):
        if self.owed:
            mm.then_inc(self.free, self.owed)
            self.owed = 0

    def load(self):
        n = self.loaded
        self.loaded += 1
        return self.slots[n % len(self.slots)], self.full[n % len(self.slots)], n + 1

    def take(self):
        n = self.taken
        self.taken += 1
        return self.slots[n % len(self.slots)], self.full[n % len(self.slots)], 16 * (n // len(self.slots) + 1)


class Core:

    def __init__(self, nc, ctx, aps, consts, small):
        self.nc, self.ctx, self.dram = nc, ctx, aps
        self.reserved, self.sems = {}, {}
        sb = lambda name, n, dt=F32: ctx.enter_context(nc.sbuf_tensor(name, [P, n], dt))
        self.wring = sb("weights", WSLOTS * BLK)
        self.h = sb("h", NT * D)[:, :].rearrange("p (i d) -> p i d", i=NT)
        self.constbuf = sb("consts", consts[0].shape[1])
        self.smallbuf = sb("small", small[0].shape[1])
        self.arena = sb("arena", 20992)
        self.cwhere, self.swhere = consts[1], small[1]
        banks = [ctx.enter_context(nc.psum_tensor(f"bank{i}", [P, 512], F32)) for i in range(8)]
        self.banks = [b[:, :] for b in banks]
        self.A = Ring(self.banks[:4], self.sem("act_bank_full"), self.sem("act_bank_free"))
        self.R = Ring(self.banks[4:], self.sem("dve_bank_full"), self.sem("dve_bank_free"))
        slots = [self.wring[:, i * BLK:(i + 1) * BLK] for i in range(WSLOTS)]
        self.W = self.W6 = Weights(slots, [self.sem(f"weights_full{i}") for i in range(WSLOTS)],
                                   self.sem("weights_free"))
        self.handed_back = []
        self.stage_ends = self.sem("stage_ends")

    def sem(self, name):
        if name not in self.sems:
            self.sems[name] = self.ctx.enter_context(self.nc.semaphore(name))
        return self.sems[name]

    def reserve(self, name, n):
        base = self.reserved.get(name, 0)
        self.reserved[name] = base + n
        return self.sem(name), base

    def c(self, name):
        at, n = self.cwhere[name]
        return self.constbuf[:, at:at + n]

    def s(self, name):
        at, n = self.swhere[name]
        return self.smallbuf[:, at:at + n]

    def at(self, off, n, **dims):
        v = self.arena[:, off:off + n]
        if dims:
            names = list(dims)
            v = v.rearrange(f"p ({' '.join(names)} x) -> p {' '.join(names)} x", **dims)
        return v


def spread(ap, n):
    return ap.unsqueeze(len(ap.shape)).broadcast_to([*ap.shape, n])


UT0 = 0
JUNK0, HN0 = 17408, 18432
SPLIT0 = 14848


class Norm:

    def __init__(self, k, src, n, gain, dst, keep=None, ready=None):
        self.k, self.src, self.n, self.gain, self.dst, self.keep, self.ready = k, src, n, gain, dst, keep, ready
        self.sq, self.sq0 = k.reserve("norm_sums", n)
        self.ms, self.ms0 = k.reserve("norm_means", 1)
        self.rt, self.rt0 = k.reserve("norm_roots", 1)
        self.hn, self.hn0 = k.reserve("norm_rows", n)
        self.junk = k.at(JUNK0, D)
        self.stat = k.stat
        self.squared = 0

    def rows(self, i):
        return self.keep[:, i, :] if self.keep is not None else self.k.at(HN0, 2 * D, i=2)[:, i % 2, :]

    def square(self, act, i):
        if i:
            act.wait_ge(self.sq, self.sq0 + i)
        act.activation(self.junk, self.src(i), ACT.Square, accum_out=self.stat[:, i:i + 1]).then_inc(self.sq, 1)

    def early(self, act, added):
        for i in range(self.n - 1):
            act.wait_ge(self.k.R.free, added(i))
            self.square(act, i)
        self.squared = self.n - 1

    def act(self, act):
        k = self.k
        if self.ready:
            act.wait_ge(*self.ready)
        for i in range(self.squared, self.n):
            self.square(act, i)
        act.wait_ge(self.ms, self.ms0 + 1)
        act.activation(self.stat[:, 8:8 + self.n], self.stat[:, 4:4 + self.n], ACT.Sqrt).then_inc(self.rt, 1)

    def dve(self, dve):
        k = self.k
        n = self.n
        if self.ready:
            dve.wait_ge(*self.ready)
        dve.wait_ge(self.sq, self.sq0 + n)
        dve.tensor_scalar(self.stat[:, 4:4 + n], self.stat[:, 0:n], 1.0 / D, EPS, ALU.mult,
                          ALU.add).then_inc(self.ms, 1)
        dve.wait_ge(self.rt, self.rt0 + 1)
        k.dlink(dve.reciprocal(self.stat[:, 12:12 + n], self.stat[:, 8:8 + n]))

        def scale(i):
            dve.tensor_scalar(self.rows(i), self.src(i), self.stat[:, 12 + i:13 + i], None,
                              ALU.mult).then_inc(self.hn, 1)

        scale(0)
        scale(1)
        for i in range(n):
            for half in range(2):
                bank, full = k.R.empty()
                dve.wait_ge(k.R.full, full)
                dve.tensor_tensor(
                    self.dst[:, 4 * half:4 * half + 4, i * P:(i + 1) * P],
                    bank.rearrange("p (a t) -> p a t", a=4),
                    spread(self.gain[:, 4 * half:4 * half + 4], P), ALU.mult,
                ).then_inc(k.R.free, 1)
            if i + 2 < n:
                scale(i + 2)

    def pe(self, pe):
        k = self.k
        for i in range(self.n):
            pe.wait_ge(self.hn, self.hn0 + i + 1)
            for half in range(2):
                bank, free = k.R.fill()
                pe.wait_ge(k.R.free, free)
                for a in range(4):
                    c = 4 * half + a
                    mm = pe.transpose(bank[:, a * P:(a + 1) * P], self.rows(i)[:, c * P:(c + 1) * P], k.c("ident"))
                    k.W.first(mm)
                mm.then_inc(k.R.full, 1)


class MemoryRows:

    R_JOBS = 2 * NM

    def __init__(self, k):
        self.k = k
        self.memT = k.at(12288, 2048, k=KD)
        self.mem = k.at(14336, 2048, j=NM)
        self.loaded, m0 = k.reserve("mem_loaded", 16)
        self.norm = Norm(k, lambda i: self.mem[:, i, :], NM, k.s("g_mem"), self.memT, ready=(self.loaded, m0 + 16))

    def load(self, pool, *free):
        pool.wait_ge(*free)
        pool.dma_start(self.mem, self.k.dram["mem"][0].rearrange("(j p) d -> p j d", p=P)).then_inc(self.loaded, 16)


class CrossAttention:

    def __init__(self, k, l):
        self.k, self.l = k, l
        self.uT = k.at(0, 4096, k=KD)
        self.oT = k.at(0, 4096, k=KD)
        self.qT = k.at(4096, 4096, k=KD)
        self.kT = k.at(8192, 2048, k=KD)
        self.v = k.at(10240, 2048, j=NM)
        self.memT = k.at(12288, 2048, k=KD)
        self.pT = k.at(12288, 2048, r=2, j=NM)
        self.prob = k.at(14336, 4096, i=NT, h=XH)
        self.norm = Norm(k, lambda i: k.h[:, i, :], NT, k.s(f"g_xa{l}"), self.uT)
        self.mx, self.mx0 = k.reserve("xa_max", 8)
        self.pr, self.pr0 = k.reserve("xa_prob", 8)
        self.neg = k.stat[:, 16:32]
        self.sum = k.stat[:, 32:48]
        self.inv = k.stat[:, 48:64]

    def loads(self):
        d, l = self.k.dram, self.l
        for w in ("xa_wk", "xa_wq", "xa_wv"):
            for n in range(2):
                yield d[w][l][:, n * 512:(n + 1) * 512].rearrange("(k p) n -> p k n", p=P)
        for j in range(2):
            yield d["xa_wo"][l][j * 512:(j + 1) * 512, :].rearrange("(k p) n -> p k n", p=P)

    def sp(self, sp):
        k = self.k
        load_weights(k, sp, self.loads())

    def pool(self, pool):
        pass

    def pe(self, pe):
        k = self.k
        pe.wait_ge(k.R.free, k.R.all())
        for n in range(2):
            w, full, got = k.W.take()
            pe.wait_ge(full, got)
            w = w.rearrange("p (k n) -> p k n", k=KD)
            for pair in range(2):
                bank, free = k.A.fill()
                pe.wait_ge(k.A.free, free)
                for s in range(2):
                    m = 2 * pair + s
                    for c in range(KD):
                        mm = pe.matmul(bank[:, s * MEM:(s + 1) * MEM], w[:, c, m * P:(m + 1) * P],
                                       self.memT[:, c, :], start=c == 0, stop=c == KD - 1)
                        k.W.first(mm)
                mm.then_inc(k.A.full, 1)
            k.W.owed += 1
        self.norm.pe(pe)
        pe.wait_ge(k.R.free, k.R.all())
        for n in range(2):
            w, full, got = k.W.take()
            pe.wait_ge(full, got)
            w = w.rearrange("p (k n) -> p k n", k=KD)
            for m in range(4):
                bank, free = k.A.fill()
                pe.wait_ge(k.A.free, free)
                for c in range(KD):
                    mm = pe.matmul(bank, w[:, c, m * P:(m + 1) * P], self.uT[:, c, :], start=c == 0,
                                   stop=c == KD - 1)
                    k.W.first(mm)
                mm.then_inc(k.A.full, 1)
            k.W.owed += 1
        pe.wait_ge(k.A.free, k.A.all())
        for i in range(NT):
            for hp in range(2):
                bank, free = k.A.fill()
                pe.wait_ge(k.A.free, free)
                for s in range(2):
                    for c in range(2):
                        t = 2 * (2 * hp + s) + c
                        mm = pe.matmul(bank[:, s * MEM:(s + 1) * MEM], self.qT[:, t, i * P:(i + 1) * P],
                                       self.kT[:, t, :], start=c == 0, stop=c == 1)
                mm.then_inc(k.A.full, 1)
        for n in range(2):
            w, full, got = k.W.take()
            pe.wait_ge(full, got)
            w = w.rearrange("p (k n) -> p k n", k=KD)
            for j in range(NM):
                bank, free = k.A.fill()
                pe.wait_ge(k.A.free, free)
                for c in range(KD):
                    mm = pe.matmul(bank, self.memT[:, c, j * P:(j + 1) * P], w[:, c, :], start=c == 0,
                                   stop=c == KD - 1)
                    k.W.first(mm)
                mm.then_inc(k.A.full, 1)
            k.W.owed += 1
        v_stored = k.A.all()
        pe.wait_ge(self.pr, self.pr0 + 8)

        pt_done = []

        def weighted(hh):
            pe.wait_ge(k.R.free, pt_done[hh])
            pe.wait_ge(k.A.free, v_stored)
            for c in range(2):
                bank, free = k.A.fill()
                pe.wait_ge(k.A.free, free)
                t = 2 * hh + c
                for j in range(NM):
                    mm = pe.matmul(bank, self.v[:, j, t * P:(t + 1) * P], self.pT[:, hh % 2, j, :], start=j == 0,
                                   stop=j == NM - 1)
                mm.then_inc(k.A.full, 1)

        for hh in range(XH):
            for j in range(NM):
                bank, free = k.R.fill()
                pe.wait_ge(k.R.free, free)
                for i in range(NT):
                    mm = pe.transpose(bank[:, i * P:(i + 1) * P], self.prob[:, i, hh, j * P:(j + 1) * P],
                                      k.c("ident"))
                mm.then_inc(k.R.full, 1)
            pt_done.append(k.R.all())
            if hh:
                weighted(hh - 1)
        weighted(XH - 1)
        pe.wait_ge(k.A.free, k.A.all())
        project_rows(k, pe, [self.oT[:, c, :] for c in range(KD)])

    def act(self, act):
        k = self.k
        self.norm.act(act)
        for n in range(2):
            for pair in range(2):
                bank, full = k.A.empty()
                act.wait_ge(k.A.full, full)
                m = 4 * n + 2 * pair
                act.activation(self.kT[:, m:m + 2, :], bank.rearrange("p (a t) -> p a t", a=2),
                               ACT.Copy).then_inc(k.A.free, 1)
        for m in range(KD):
            bank, full = k.A.empty()
            act.wait_ge(k.A.full, full)
            act.activation(self.qT[:, m, :], bank, ACT.Copy,
                           scale=(D // XH) ** -0.5).then_inc(k.A.free, 1)
        for i in range(NT):
            for hp in range(2):
                bank, full = k.A.empty()
                act.wait_ge(self.mx, self.mx0 + 2 * i + hp + 1)
                for s in range(2):
                    hh = 2 * hp + s
                    ins = act.activation(self.prob[:, i, hh, :], bank[:, s * MEM:(s + 1) * MEM], ACT.Exp,
                                         bias=self.neg[:, 4 * i + hh:4 * i + hh + 1],
                                         accum_out=self.sum[:, 4 * i + hh:4 * i + hh + 1])
                ins.then_inc(k.A.free, 1)
        for n in range(2):
            for j in range(NM):
                bank, full = k.A.empty()
                act.wait_ge(k.A.full, full)
                act.activation(self.v[:, j, n * 512:(n + 1) * 512], bank,
                               ACT.Copy).then_inc(k.A.free, 1)
        for t in range(KD):
            bank, full = k.A.empty()
            act.wait_ge(k.A.full, full)
            act.activation(self.oT[:, t, :], bank, ACT.Copy).then_inc(k.A.free, 1)

    def dve(self, dve):
        k = self.k
        self.norm.dve(dve)
        first = self.a0 + 12
        for i in range(NT):
            for hp in range(2):
                n = first + 2 * i + hp
                dve.wait_ge(k.A.full, n + 1)
                dve.tensor_reduce(self.neg[:, 4 * i + 2 * hp:4 * i + 2 * hp + 2],
                                  k.A.banks[n % 4].rearrange("p (a t) -> p a t", a=2), AX.X, ALU.max,
                                  negate=True).then_inc(self.mx, 1)
            if i:
                self.normalise(dve, i - 1)
        self.normalise(dve, NT - 1)
        for hh in range(XH):
            for j in range(NM):
                bank, full = k.R.empty()
                dve.wait_ge(k.R.full, full)
                if hh >= 2:
                    dve.wait_ge(k.A.full, first + 12 + 2 * (hh - 2) + 2)
                dve.tensor_copy(self.pT[:, hh % 2, j, :], bank).then_inc(k.R.free, 1)
        add_rows(k, dve)

    def normalise(self, dve, i):
        k = self.k
        dve.wait_ge(k.A.free, k.A.stored(self.a0 + 12 + 2 * i + 2))
        k.dlink(dve.reciprocal(self.inv[:, 4 * i:4 * i + 4], self.sum[:, 4 * i:4 * i + 4]))
        for hp in range(2):
            dve.tensor_tensor(self.prob[:, i, 2 * hp:2 * hp + 2, :], self.prob[:, i, 2 * hp:2 * hp + 2, :],
                              spread(self.inv[:, 4 * i + 2 * hp:4 * i + 2 * hp + 2], MEM),
                              ALU.mult).then_inc(self.pr, 1)

    A_JOBS, R_JOBS, W_BLOCKS = 4 + 4 + 8 + 8 + 8, 2 * NT + 8 + 8, 8


def load_weights(k, sp, blocks):
    for src in blocks:
        slot, full, free = k.W.load()
        sp.wait_ge(k.W.free, free)
        if k.handed_back:
            sp.wait_ge(*k.handed_back.pop(0))
        sp.dma_start(slot.rearrange("p (k n) -> p k n", k=src.shape[1]), src).then_inc(full, 16)


def own_ring(k, name, w0, places):
    slots = [k.W6.slots[(w0 + at) % WSLOTS] for at in places]
    return Weights(slots, [k.sem(f"{name}_weights_full{j}") for j in range(len(slots))], k.sem(f"{name}_weights_free"))


def load_own_ring(k, sp, name, w0, places, blocks, place0_free):
    own = own_ring(k, name, w0, places)
    for n, src in enumerate(blocks):
        slot, full, free = own.load()
        if n < len(places):
            sp.wait_ge(k.W6.free, w0 + places[n] + 1)
        else:
            sp.wait_ge(own.free, free)
        sp.dma_start(slot.rearrange("p (k n) -> p k n", k=src.shape[1]), src).then_inc(full, 16)
    last = {places[n % len(places)]: n for n in range(own.loaded)}
    k.handed_back = [place0_free] + [(own.free, last[at] + 1 + len(places)) for at in range(1, WSLOTS)]


def project_rows(k, pe, tiles, between=None):
    blocks = [k.W.take() for _ in range(len(tiles) // 4)]
    for _, full, got in blocks:
        pe.wait_ge(full, got)
    for i in range(NT):
        for n in range(2):
            bank, free = k.R.fill()
            pe.wait_ge(k.R.free, free)
            for c, t in enumerate(tiles):
                w = blocks[c // 4][0].rearrange("p (k n) -> p k n", k=4)
                mm = pe.matmul(bank, t[:, i * P:(i + 1) * P], w[:, c % 4, n * 512:(n + 1) * 512], start=c == 0,
                               stop=c == len(tiles) - 1)
                if c == 0:
                    k.W.first(mm)
            mm.then_inc(k.R.full, 1)
        if between and i == NT // 2 - 1:
            between(pe)
    k.W.owed += len(blocks)


def add_rows(k, dve, between=None):
    for i in range(NT):
        for n in range(2):
            bank, full = k.R.empty()
            dve.wait_ge(k.R.full, full)
            hs = k.h[:, i, n * 512:(n + 1) * 512]
            dve.tensor_tensor(hs, hs, bank, ALU.add).then_inc(k.R.free, 1)
        if between and i == NT // 2 - 1:
            between(dve)


class PairSignals:

    def __init__(self, k, name):
        s = lambda what: k.sem(f"{name}_{what}")
        self.chosen = s("chosen")
        self.gated = s("gated")
        self.x_full = s("x_full")
        self.x_stored = s("x_stored")
        self.turn_full = s("turn_full")
        self.turn_stored = s("turn_stored")
        self.hT_full = s("hT_full")
        self.hT_stored = s("hT_stored")
        self.g_full = s("gate_full")
        self.u_full = s("up_full")
        self.silu = s("silu")
        self.hid = s("hid")
        self.y_full = s("y_full")
        self.y_stored = s("y_stored")
        self.sc_full = s("sc_full")
        self.sc_added = s("sc_added")


class Moe:

    DVE_STEPS = 1

    def __init__(self, k, l):
        self.k, self.l = k, l
        self.uT = k.at(0, 4096, k=KD)
        self.xn = k.at(4096, 4096, i=NT)
        self.norm = Norm(k, lambda i: k.h[:, i, :], NT, k.s(f"g_ffn{l}"), self.uT, keep=self.xn)
        at = SPLIT0
        self.parts = []
        for _ in range(3):
            self.parts.append(k.arena[:, at:at + NT * D // 2].bitcast(BF16).rearrange("p (i d) -> p i d", i=NT))
            at += NT * D // 2
        self.S = k.arena[:, 8192:8448].bitcast(BF16).rearrange("p (i s) -> p i s", i=NT)
        self.SG = k.at(8704, 512, i=NT)
        self.xsT = k.at(9216, 1024, k=KD)
        self.turned = k.at(10240, 512, i=NT)
        self.y = k.at(10752, 1024)
        self.hidden_rows = k.at(11776, 512)
        self.hT = k.at(12288, 512, m=4)
        self.rank = k.at(12800, NPASS * NT * NE, b=NPASS, i=NT)
        self.gates = k.at(13824, NT * NE, i=NT)
        self.member = k.at(13952, NT * NE, i=NT)
        self.tmp = 14080
        self.routed, self.routed0 = k.reserve("moe_routed", 1)
        self.passes, self.passes0 = k.reserve("moe_passes", 1)
        self.rexp, self.rexp0 = k.reserve("moe_exp_in", 2)
        self.rexpd, self.rexpd0 = k.reserve("moe_exp_out", 2)
        self.part, self.part0 = k.reserve("moe_parts", 3 * NT)
        self.rest, self.rest0 = k.reserve("moe_rests", 2 * NT)
        self.main = PairSignals(k, "pair")
        self.more = PairSignals(k, f"more{l}")
        self.more_done = k.sem(f"more{l}_done")
        self.more_w = k.sem(f"more{l}_weights_full")
        self.npass = k.npass

    A_JOBS, R_JOBS, W_BLOCKS = 0, 2 * NT + 2, 6 * PAIRS

    def pair_blocks(self, pair):
        d, l = self.k.dram, self.l
        for w in ("moe_w_gate", "moe_w_up"):
            for e in range(2):
                yield d[w][l][bass.ds(2 * pair + e, 1)].rearrange("e (k p) n -> p (e k) n", p=P)
        for e in range(2):
            yield d["moe_w_down"][l][bass.ds(2 * pair + e, 1)].rearrange("e (k p) n -> p (e k) n", p=P)

    def sp(self, sp):
        k = self.k
        n0 = k.W.loaded
        with sp.Fori(0, PAIRS) as pair:
            for j, src in enumerate(self.pair_blocks(pair)):
                slot = k.W.slots[(n0 + j) % WSLOTS]
                sp.wait_ge(k.W.free, 6 * pair + (n0 + j + 1))
                sp.dma_start(slot.rearrange("p (k n) -> p k n", k=src.shape[1]), src).then_inc(
                    k.W.full[(n0 + j) % WSLOTS], 16)
        k.W.loaded += 6 * PAIRS
        self.w0 = n0

        def again(g, pair):
            sp.wait_ge(self.more.sc_added, 8 * g + 2)
            for j, src in enumerate(self.pair_blocks(pair)):
                slot = k.W.slots[(n0 + j) % WSLOTS]
                sp.dma_start(slot.rearrange("p (k n) -> p k n", k=src.shape[1]), src).then_inc(self.more_w, 16)

        self.further(sp, again, lambda: sp.wait_ge(self.main.sc_added, self.l * 8 * PAIRS + 8 * PAIRS + 2),
                     lambda: sp.wait_ge(self.more_done, 1))

    def further(self, eng, body, before=None, after=None):
        eng.wait_ge(self.passes, self.passes0 + 1)
        n = eng.value_load(self.npass[0:1, self.l:self.l + 1], min_val=1, max_val=NPASS)
        with eng.If(n > 1):
            if before:
                before()
            with eng.Fori(1, n) as b:
                with eng.Fori(0, PAIRS) as pair:
                    g = eng.snap(b * PAIRS + pair - PAIRS, min_val=0, max_val=PAIRS * NPASS)
                    body(g, pair)
            if after:
                after()

    def choose(self, dve, sg, g, b, pair, alone=False):
        k = self.k
        if not alone:
            dve.wait_ge(sg.x_full, 2 * g)
            dve.wait_ge(sg.gated, g)
        slots = self.S.rearrange("p i (e s) -> p i e s", e=2)
        iota = k.c("iota").unsqueeze(1).unsqueeze(1).broadcast_to([P, NT, 2, CAP])
        rank = self.rank[:, b, :, :] if isinstance(b, int) else self.rank[:, bass.ds(b, 1), :, :].rearrange(
            "p b i e -> p (b i) e")
        rank = spread(rank[:, :, bass.ds(2 * pair, 2)], CAP)
        dve.tensor_tensor(slots, iota, rank, ALU.is_equal).then_inc(sg.chosen, 1)

    def weigh(self, dve, sg, g, pair, alone=False):
        if not alone:
            dve.wait_ge(sg.turn_full, g)
        dve.wait_ge(sg.chosen, g + 1)
        dve.tensor_tensor(self.SG.rearrange("p i (e s) -> p i e s", e=2),
                          self.S.rearrange("p i (e s) -> p i e s", e=2),
                          spread(self.gates[:, :, bass.ds(2 * pair, 2)], CAP), ALU.mult).then_inc(sg.gated, 1)

    def gather(self, pe, sg, g):
        k = self.k
        pe.wait_ge(sg.chosen, g + 1)
        for half in range(2):
            bank = k.banks[half]
            for a in range(4):
                c = 4 * half + a
                for i in range(NT):
                    for j, part in enumerate(self.parts):
                        mm = pe.matmul(bank[:, a * P:(a + 1) * P], part[:, i, c * P:(c + 1) * P], self.S[:, i, :],
                                       start=i == j == 0, stop=i == NT - 1 and j == 2)
            mm.then_inc(sg.x_full, 1)

    def turn(self, pe, sg, g):
        k = self.k
        pe.wait_ge(sg.gated, g + 1)
        pe.wait_ge(sg.hid, g + 1)
        for i in range(NT):
            mm = pe.transpose(k.banks[2][:, i * P:(i + 1) * P], self.SG[:, i, :], k.c("ident"))
            if i == 0:
                self.freed(mm)
        mm.then_inc(sg.turn_full, 1)

    def turn_hidden(self, pe, sg, g):
        k = self.k
        pe.wait_ge(sg.hid, g + 1)
        for m in range(4):
            mm = pe.transpose(k.banks[3][:, m * P:(m + 1) * P], self.hidden_rows[:, m * P:(m + 1) * P],
                              k.c("ident"))
        mm.then_inc(sg.hT_full, 1)

    def gate_up(self, pe, sg, g, wait, w, alone=False, free_first=False):
        k = self.k
        pe.wait_ge(sg.x_stored, 2 * g + 2)
        for u in range(2):
            if not alone:
                pe.wait_ge(*((sg.turn_stored, g), (sg.hT_stored, g))[u])
            wait(2 * u)
            wait(2 * u + 1)
            bank = k.banks[2 + u]
            for c in range(KD):
                for e in range(2):
                    wt = w[2 * u + e].rearrange("p (k n) -> p k n", k=KD)
                    mm = pe.matmul(bank[e * CAP:(e + 1) * CAP, :], self.xsT[:, c, e * CAP:(e + 1) * CAP],
                                   wt[:, c, :], start=c == 0, stop=c == KD - 1)
                    if c == 0 and e == 0 and (u == 1 or free_first):
                        self.freed(mm)
            mm.then_inc((sg.g_full, sg.u_full)[u], 1)

    def down(self, pe, sg, g, wait, w, alone=False):
        k = self.k
        pe.wait_ge(sg.hT_stored, g + 1)
        for n in range(2):
            if not alone:
                pe.wait_ge(sg.y_stored, 2 * g + n - 1)
            if n == 0:
                wait(4)
                wait(5)
            for m in range(4):
                for e in range(2):
                    wt = w[4 + e].rearrange("p (k n) -> p k n", k=4)
                    mm = pe.matmul(k.banks[4 + n][e * CAP:(e + 1) * CAP, :], self.hT[:, m, e * CAP:(e + 1) * CAP],
                                   wt[:, m, n * 512:(n + 1) * 512], start=m == 0, stop=m == 3)
            mm.then_inc(sg.y_full, 1)

    def scatter(self, pe, sg, g):
        k = self.k
        pe.wait_ge(sg.turn_stored, g + 1)
        pe.wait_ge(sg.y_stored, 2 * g + 2)
        for j in range(8):
            i, n = j // 2, j % 2
            pe.wait_ge(sg.sc_added, 8 * g + j + 1)
            pe.matmul(k.banks[6 + n], self.turned[:, i, :], self.y[:, n * 512:(n + 1) * 512], start=True,
                      stop=True).then_inc(sg.sc_full, 1)

    def store_gathered(self, dve, sg, g):
        k = self.k
        for half in range(2):
            dve.wait_ge(sg.x_full, 2 * g + half + 1)
            dve.tensor_tensor(self.xsT[:, 4 * half:4 * half + 4, :],
                              k.banks[half].rearrange("p (a t) -> p a t", a=4),
                              spread(k.s(f"g_ffn{self.l}")[:, 4 * half:4 * half + 4], P),
                              ALU.mult).then_inc(sg.x_stored, 1)

    def hidden(self, dve, sg, g):
        dve.wait_ge(sg.u_full, g + 1)
        dve.wait_ge(sg.silu, g + 1)
        dve.tensor_tensor(self.hidden_rows, self.hidden_rows, self.k.banks[3], ALU.mult).then_inc(sg.hid, 1)

    def add_scattered(self, dve, sg, g):
        k = self.k
        for j in range(8):
            i, n = j // 2, j % 2
            dve.wait_ge(sg.sc_full, 8 * g + j + 1)
            if j == 0:
                dve.wait_ge(sg.sc_added, 8 * g + 2)
            hs = k.h[:, i, n * 512:(n + 1) * 512]
            dve.tensor_tensor(hs, hs, k.banks[6 + n], ALU.add).then_inc(sg.sc_added, 1)

    def silu(self, act, sg, g, alone=False):
        act.wait_ge(sg.g_full, g + 1)
        if not alone:
            act.wait_ge(sg.hT_full, g)
        act.activation(self.hidden_rows, self.k.banks[2], ACT.Silu).then_inc(sg.silu, 1)

    def store_turned(self, act, sg, g, alone=False):
        act.wait_ge(sg.turn_full, g + 1)
        if not alone:
            act.wait_ge(sg.sc_full, 8 * g)
        act.activation(self.turned, self.k.banks[2].rearrange("p (i t) -> p i t", i=NT),
                       ACT.Copy).then_inc(sg.turn_stored, 1)

    def store_hidden(self, act, sg, g, alone=False):
        act.wait_ge(sg.hT_full, g + 1)
        if not alone:
            act.wait_ge(sg.y_full, 2 * g)
        act.activation(self.hT, self.k.banks[3].rearrange("p (m s) -> p m s", m=4),
                       ACT.Copy).then_inc(sg.hT_stored, 1)

    def store_down(self, act, sg, g):
        for n in range(2):
            act.wait_ge(sg.y_full, 2 * g + n + 1)
            act.activation(self.y[:, n * 512:(n + 1) * 512], self.k.banks[4 + n],
                           ACT.Copy).then_inc(sg.y_stored, 1)

    def each(self, eng, body):
        g0 = self.l * PAIRS
        body(0, g0, True, False)
        with eng.Fori(1, PAIRS - 1) as pair:
            body(pair, pair + g0, False, False)
        body(PAIRS - 1, g0 + PAIRS - 1, False, True)

    def pe(self, pe):
        k, sg = self.k, self.main
        self.norm.pe(pe)
        bank, free = k.R.fill()
        pe.wait_ge(k.R.free, free)
        pe.wait_ge(k.R.free, k.R.stored(k.R.filled - 1))
        wr = k.s(f"w_route{self.l}").rearrange("p (k n) -> p k n", k=KD)
        for i in range(NT):
            for c in range(KD):
                mm = pe.matmul(bank[:, i * 36:(i + 1) * 36], self.uT[:, c, i * P:(i + 1) * P], wr[:, c, :],
                               start=c == 0, stop=c == KD - 1)
        mm.then_inc(k.R.full, 1)
        bank, free = k.R.fill()
        pe.wait_ge(k.R.free, free)
        pe.wait_ge(self.routed, self.routed0 + 1)
        for i in range(NT + 1):
            for j in range(min(i + 1, NT)):
                mm = pe.matmul(bank[:, i * NE:(i + 1) * NE], k.c("supper") if j == i else k.c("ones"),
                               self.member[:, j, :], start=j == 0, stop=j == min(i, NT - 1))
        mm.then_inc(k.R.full, 1)
        pe.wait_ge(k.A.free, k.A.all())
        pe.wait_ge(k.R.free, k.R.all())
        n0 = k.W.taken
        w = [k.W.slots[(n0 + j) % WSLOTS] for j in range(6)]

        def wait_main(pair):
            def wait(j):
                s = (n0 + j) % WSLOTS
                pe.wait_ge(k.W.full[s], 16 * pair + 16 * ((n0 + j) // WSLOTS + 1))
            return wait

        self.freed = lambda mm: mm.then_inc(k.W.free, 2)
        assert k.W.owed == 0
        pe.wait_ge(self.part, self.part0 + 3 * NT)
        self.gather(pe, sg, self.l * PAIRS)

        def body(pair, g, first, last):
            wait = wait_main(pair)
            alone = first and self.l == 0
            self.gate_up(pe, sg, g, wait, w, alone, free_first=not first)
            if not first:
                self.scatter(pe, sg, g - 1)
            self.turn(pe, sg, g)
            self.turn_hidden(pe, sg, g)
            if not last:
                self.gather(pe, sg, g + 1)
            self.down(pe, sg, g, wait, w, alone)

        self.each(pe, body)
        self.scatter(pe, sg, self.l * PAIRS + PAIRS - 1)
        k.W.taken += 6 * PAIRS
        k.W.owed += 2

        def again(g, pair):
            sm = self.more
            self.freed = lambda mm: None
            wait = lambda j: pe.wait_ge(self.more_w, 96 * g + 96)
            self.gather(pe, sm, g)
            self.gate_up(pe, sm, g, wait, w, alone=True)
            self.turn(pe, sm, g)
            self.turn_hidden(pe, sm, g)
            self.down(pe, sm, g, wait, w, alone=True)
            self.scatter(pe, sm, g)

        self.further(pe, again)

    def act(self, act):
        k, sg = self.k, self.main
        self.norm.act(act)
        t = self.route_tiles()
        for j in range(3):
            for i in range(NT):
                if j == 0:
                    act.wait_ge(self.norm.hn, self.norm.hn0 + i + 1)
                else:
                    act.wait_ge(self.rest, self.rest0 + NT * (j - 1) + i + 1)
                act.activation(self.parts[j][:, i, :], self.xn[:, i, :], ACT.Copy).then_inc(self.part, 1)
        act.wait_ge(self.rexp, self.rexp0 + 1)
        act.activation(t["gexp"], t["gdiff"], ACT.Exp).then_inc(self.rexpd, 1)
        act.wait_ge(self.rexp, self.rexp0 + 2)
        act.activation(t["eexp"], t["ediff"], ACT.Exp).then_inc(self.rexpd, 1)

        def body(pair, g, first, last):
            alone = first and self.l == 0
            self.silu(act, sg, g, alone)
            self.store_turned(act, sg, g, alone)
            self.store_hidden(act, sg, g, alone)
            self.store_down(act, sg, g)

        self.each(act, body)

        def again(g, pair):
            sm = self.more
            self.silu(act, sm, g, alone=True)
            self.store_turned(act, sm, g, alone=True)
            self.store_hidden(act, sm, g, alone=True)
            self.store_down(act, sm, g)

        self.further(act, again)

    def route_tiles(self):
        k, at, out = self.k, self.tmp, {}

        def tile(name, *shape):
            nonlocal at
            n = int(np.prod(shape))
            v = k.arena[:, at:at + n]
            at += n
            letters = "abcd"[:len(shape)]
            out[name] = v.rearrange(f"p ({' '.join(letters)}) -> p {' '.join(letters)}",
                                    **dict(zip(letters, shape))) if len(shape) > 1 else v

        tile("logits", NT, NG + NE)
        tile("gmax", NT)
        tile("gdiff", NT, NG)
        tile("gexp", NT, NG)
        tile("gsum", NT)
        tile("gw", NT)
        tile("geq", NT, NG)
        tile("gtop", NT)
        tile("group", NT, NG)
        tile("spreadl", NT, NG, EPG)
        tile("el", NT, EPG)
        tile("m1", NT)
        tile("m2", NT)
        tile("eq", NT, EPG)
        tile("top", NT)
        tile("one1", NT, EPG)
        tile("one2", NT, EPG)
        tile("el2", NT, EPG)
        tile("ediff", NT)
        tile("eexp", NT)
        tile("den", NT)
        tile("gate1", NT)
        tile("gate2", NT)
        tile("g8", NT, EPG)
        tile("m8", NT, EPG)
        tile("cmax", 1)
        tile("over", NPASS - 1)
        tile("np", 1)
        assert at <= SPLIT0
        return out

    def first_of(self, link, dve, x, top, eq, cand, onehot, n):
        k = self.k
        prio = k.c("prio")[:, 0:n].unsqueeze(1).broadcast_to([P, NT, n])
        link(dve.tensor_tensor(eq, x, spread(top, n), ALU.is_equal))
        link(dve.tensor_tensor(eq, eq, prio, ALU.mult))
        link(dve.tensor_reduce(cand, eq, AX.X, ALU.max))
        link(dve.tensor_tensor(onehot, eq, spread(cand, n), ALU.is_equal))

    def route(self, dve):
        k, t, link = self.k, self.route_tiles(), self.k.dlink
        logits = t["logits"]
        bank, full = k.R.empty()
        dve.wait_ge(k.R.full, full)
        bias = k.s(f"b_route{self.l}").unsqueeze(1).broadcast_to([P, NT, NG + NE])
        dve.tensor_tensor(logits, bank[:, 0:NT * (NG + NE)].rearrange("p (a b) -> p a b", a=NT), bias,
                          ALU.add).then_inc(k.R.free, 1)
        dve.wait_ge(k.R.free, k.R.stored(k.R.emptied))
        groups, experts = logits[:, :, 0:NG], logits[:, :, NG:NG + NE]
        link(dve.tensor_reduce(t["gmax"], groups, AX.X, ALU.max))
        dve.tensor_tensor(t["gdiff"], groups, spread(t["gmax"], NG), ALU.subtract).then_inc(self.rexp, 1)
        self.first_of(link, dve, groups, t["gmax"], t["geq"], t["gtop"], t["group"], NG)
        link(dve.tensor_tensor(t["spreadl"], experts.rearrange("p a (g e) -> p a g e", g=NG),
                               spread(t["group"], EPG), ALU.mult))
        link(dve.tensor_reduce(t["el"], t["spreadl"].rearrange("p a g e -> p a e g"), AX.X, ALU.add))
        link(dve.tensor_reduce(t["m1"], t["el"], AX.X, ALU.max))
        self.first_of(link, dve, t["el"], t["m1"], t["eq"], t["top"], t["one1"], EPG)
        link(dve.scalar_tensor_tensor(t["el2"], t["one1"], -3.0e38, t["el"], ALU.mult, ALU.add))
        link(dve.tensor_reduce(t["m2"], t["el2"], AX.X, ALU.max))
        self.first_of(link, dve, t["el2"], t["m2"], t["eq"], t["top"], t["one2"], EPG)
        dve.tensor_tensor(t["ediff"], t["m2"], t["m1"], ALU.subtract).then_inc(self.rexp, 1)
        dve.wait_ge(self.rexpd, self.rexpd0 + 2)
        link(dve.tensor_reduce(t["gsum"], t["gexp"], AX.X, ALU.add))
        link(dve.tensor_scalar(t["den"], t["eexp"], 1.0, None, ALU.add))
        link(dve.tensor_tensor(t["den"], t["den"], t["gsum"], ALU.mult))
        link(dve.reciprocal(t["gate1"], t["den"]))
        link(dve.tensor_tensor(t["gate2"], t["gate1"], t["eexp"], ALU.mult))
        link(dve.tensor_tensor(t["g8"], t["one1"], spread(t["gate1"], EPG), ALU.mult))
        link(dve.tensor_tensor(t["m8"], t["one2"], spread(t["gate2"], EPG), ALU.mult))
        link(dve.tensor_tensor(t["g8"], t["g8"], t["m8"], ALU.add))
        link(dve.tensor_tensor(t["m8"], t["one1"], t["one2"], ALU.add))

        def by_group(dst, v):
            ins = None
            for g in range(NG):
                ins = dve.tensor_tensor(dst[:, :, g * EPG:(g + 1) * EPG], v,
                                        t["group"][:, :, g:g + 1].broadcast_to([P, NT, EPG]), ALU.mult)
                if g < NG - 1:
                    ins.then_inc(k.dlink.sem, 1)
                    k.dlink.n += 1
            return ins

        link(by_group(self.gates, t["g8"]))
        link(by_group(self.member, t["m8"]))
        dve.sem_inc(self.routed, 1)
        bank, full = k.R.empty()
        dve.wait_ge(k.R.full, full)
        ranks = bank[:, 0:NT * NE].rearrange("p (a e) -> p a e", a=NT)
        link(dve.scalar_tensor_tensor(self.rank[:, 0, :, :], ranks, 1.0, self.member, ALU.add, ALU.mult))
        link(dve.tensor_reduce(t["cmax"], bank[:, NT * NE:(NT + 1) * NE], AX.X, ALU.max))
        link(dve.tensor_scalar(self.rank[:, 0, :, :], self.rank[:, 0, :, :], -1.0, None, ALU.add))
        for b in range(1, NPASS):
            dve.tensor_scalar(self.rank[:, b, :, :], self.rank[:, 0, :, :], -float(CAP * b), None,
                              ALU.add).then_inc(k.dlink.sem, 1)
            k.dlink.n += 1
        link(dve.tensor_tensor(t["over"], k.c("limits"), t["cmax"].broadcast_to([P, NPASS - 1]), ALU.is_lt))
        link(dve.tensor_reduce(t["np"], t["over"], AX.X, ALU.add))
        dve.tensor_scalar(self.npass[:, self.l:self.l + 1], t["np"], 1.0, None, ALU.add).then_inc(self.passes, 1)
        dve.sem_inc(k.R.free, 1)

    def dve(self, dve):
        k, sg = self.k, self.main
        self.norm.dve(dve)
        self.route(dve)
        g0 = self.l * PAIRS
        self.choose(dve, sg, g0, 0, 0, alone=True)
        self.weigh(dve, sg, g0, 0, alone=True)
        self.store_gathered(dve, sg, g0)

        def body(pair, g, first, last):
            if not last:
                self.choose(dve, sg, g + 1, 0, pair + 1)
            self.hidden(dve, sg, g)
            if not first:
                self.add_scattered(dve, sg, g - 1)
            if not last:
                self.weigh(dve, sg, g + 1, pair + 1)
                self.store_gathered(dve, sg, g + 1)

        self.each(dve, body)
        self.add_scattered(dve, sg, g0 + PAIRS - 1)

        def again(g, pair):
            sm = self.more
            b = dve.snap((g - pair) // PAIRS + 1, min_val=1, max_val=NPASS - 1)
            self.choose(dve, sm, g, b, pair, alone=True)
            self.weigh(dve, sm, g, pair, alone=True)
            self.store_gathered(dve, sm, g)
            self.hidden(dve, sm, g)
            self.add_scattered(dve, sm, g)

        self.further(dve, again, after=lambda: dve.drain().then_inc(self.more_done, 1))

    def pool(self, pool):
        k = self.k
        for j in range(2):
            for i in range(NT):
                pool.wait_ge(self.part, self.part0 + NT * j + i + 1)
                if j == 0:
                    pool.wait_ge(k.R.full, self.r0 + 2 * i + 2)
                x = self.xn[:, i, :]
                pool.tensor_tensor(x, x, self.parts[j][:, i, :], ALU.subtract).then_inc(self.rest, 1)


class Store:

    A_JOBS = R_JOBS = W_BLOCKS = 0

    def __init__(self, k):
        self.k = k
        self.sq, self.ms, self.rt = k.sem("final_sums"), k.sem("final_means"), k.sem("final_roots")
        self.rows, self.out, self.gain = k.sem("final_rows"), k.sem("out_stored"), k.sem("final_gain")
        self.g = k.at(4096, D)

    def pool(self, pool):
        k = self.k
        pool.dma_start(self.g, k.dram["final_gain"]).then_inc(self.gain, 16)

    def sp(self, sp):
        k = self.k
        for i in range(NT):
            sp.wait_ge(self.rows, i + 1)
            sp.dma_start(k.dram["out"][0][i * P:(i + 1) * P, :], k.at(8192, NT * D, i=NT)[:, i, :]).then_inc(self.out, 16)
        sp.wait_ge(self.out, 16 * NT)

    def act(self, act):
        k = self.k
        for i in range(NT):
            if i:
                act.wait_ge(self.sq, i)
            act.activation(k.at(0, D), k.h[:, i, :], ACT.Square, accum_out=k.stat[:, i:i + 1]).then_inc(self.sq, 1)
        act.wait_ge(self.ms, 1)
        act.activation(k.stat[:, 8:12], k.stat[:, 4:8], ACT.Sqrt).then_inc(self.rt, 1)

    def dve(self, dve):
        k = self.k
        dve.wait_ge(self.sq, NT)
        dve.tensor_scalar(k.stat[:, 4:8], k.stat[:, 0:4], 1.0 / D, EPS, ALU.mult, ALU.add).then_inc(self.ms, 1)
        dve.wait_ge(self.rt, 1)
        k.dlink(dve.reciprocal(k.stat[:, 12:16], k.stat[:, 8:12]))
        dve.wait_ge(self.gain, 16)
        for i in range(NT):
            dve.scalar_tensor_tensor(k.at(8192, NT * D, i=NT)[:, i, :], k.h[:, i, :], k.stat[:, 12 + i:13 + i],
                                     self.g, ALU.mult, ALU.mult).then_inc(self.rows, 1)

    def pe(self, pe):
        pass



class Even:

    W_BLOCKS = 0
    PLACES = (5, 1, 2, 3, 4)
    A_JOBS = 4 + 12 + NT * 6
    R_JOBS = 8 + 8 + 10 + 1 + 1 + (3 * NT + 2 * (NT - 1) + 2 * (NT - 1)) + 8 + 8 + MemoryRows.R_JOBS

    def __init__(self, k):
        self.k = k
        self.uT = k.at(0, 4096, k=KD)
        self.mixT = k.at(4096, 6144, k=MIXT)
        self.norm = Norm(k, lambda i: k.h[:, i, :], NT, k.s("g_mix0"), self.uT)
        self.memory = MemoryRows(k)
        self.xs = k.at(10240, 4096, i=NT)
        self.bc = k.at(14336, 2048, k=4)
        self.btok = k.at(16384, 1024, i=NT, g=SSM_G)
        self.cg = k.at(17408, 1024, b=2)
        self.pad3 = k.at(18432, 2 * 514, b=2)
        self.acc3 = k.at(19460, 1024, b=2)
        self.xpad = k.at(6144, 2 * 516, b=2)
        self.acc = k.at(7176, 1024, b=2)
        self.sil = k.at(8200, 1024, b=2)
        self.state = k.at(17408, 1024, g=SSM_G)
        self.xdt = k.at(18432, 1024)
        self.xde = k.at(19456, 1024)
        self.G = k.at(6144, 1024, b=2)
        self.E = k.at(7168, 1024, b=2)
        self.cb = k.at(8192, 256, g=SSM_G)
        self.off = [k.at(8448, 512), k.at(20480, 512)]
        small = lambda j: k.at(9344 + 64 * j, 64, i=NT)
        (self.dt, self.adt, self.cum, self.ecum, self.tot, self.etot, self.toend, self.dte, self.t0,
         self.t1) = [small(j) for j in range(10)]
        self.ea = k.at(9984, 16)
        self.gsum = k.at(10000, 8)
        s = lambda n: k.sem(f"ssd_{n}")
        self.pads, self.conv, self.silu = s("pads"), s("convolved"), s("silu")
        self.dte_in, self.dte_out, self.dt_ready = s("softplus_in"), s("softplus_out"), s("decay_ready")
        self.dt_first = s("exponents_ready")
        self.cexp = s("cum_exp")
        self.g_ready, self.w_ready, self.x_ready = s("segments_in"), s("weights_ready"), s("x_scaled")
        self.gated, self.sums, self.roots, self.normed = s("gated"), s("sums"), s("roots"), s("normed")
        self.state_ready = s("state_ready")
        self.sq_free, self.z_ready = s("means"), s("z_ready")

    def loads(self):
        d = self.k.dram
        for c in (1, 2, 0, 5, 6, 7, 3, 4):
            yield d["ev_w_in"][0][:, c * 512:(c + 1) * 512].rearrange("(k p) n -> p k n", p=P)
        for j in range(3):
            yield d["ev_w_out"][0][j * 512:(j + 1) * 512, :].rearrange("(k p) n -> p k n", p=P)

    def sp(self, sp):
        load_own_ring(self.k, sp, "even", self.w0, self.PLACES, self.loads(), (self.sums, 2 * NT))

    def z(self, i):
        return self.k.W6.slots[self.w0 % WSLOTS][:, i * D:(i + 1) * D]

    def segment_turn(self, n):
        return self.a0 + 16 + 6 * (n // 4) + (0, 1, 3, 4)[n % 4]

    def pool(self, pool):
        k = self.k
        pool.wait_ge(self.dt_ready, 1)
        pool.wait_ge(self.silu, 12)
        pool.wait_ge(k.R.free, k.R.stored(self.chunk_r(0)))
        upper = k.c("upper").unsqueeze(1).broadcast_to([P, 4, P])
        for i in range(NT):
            if i:
                pool.wait_ge(k.R.full, self.chunk_r(i))
            xs = self.xs[:, i, :].rearrange("p (h d) -> p h d", h=SSM_H)

            def segment(hb):
                n = 4 * i + hb
                if n >= 2:
                    pool.wait_ge(k.A.full, self.segment_turn(n - 2) + 1)
                pool.tensor_tensor(self.G[:, n % 2, :].rearrange("p (h t) -> p h t", h=4), upper,
                                   spread(self.adt[:, i, 4 * hb:4 * hb + 4], P), ALU.mult).then_inc(self.g_ready, 1)

            segment(0)
            segment(1)
            pool.tensor_tensor(self.xdt.rearrange("p (h d) -> p h d", h=SSM_H), xs, spread(self.dt[:, i, :], SSM_P),
                               ALU.mult).then_inc(self.x_ready, 1)
            pool.tensor_tensor(self.xde.rearrange("p (h d) -> p h d", h=SSM_H), xs, spread(self.dte[:, i, :], SSM_P),
                               ALU.mult).then_inc(self.x_ready, 1)
            pool.wait_ge(self.x_ready, 3 * i + 2)
            pool.tensor_tensor(xs, xs, spread(k.s("d_skip"), SSM_P), ALU.mult).then_inc(self.x_ready, 1)
            segment(2)
            segment(3)
        self.memory.load(pool, k.R.free, k.R.stored(self.r0 + self.R_JOBS - 8 - MemoryRows.R_JOBS))

    def chunk_r(self, i):
        return self.r0 + 8 + 8 + 10 + 2 + 3 * i + 2 * max(i - 1, 0) + 2 * min(i, NT - 1)

    def pe(self, pe):
        k = self.k
        self.norm.pe(pe)
        k.W = own_ring(k, "even", self.w0, self.PLACES)
        pe.sem_inc(k.W.free, len(self.PLACES))
        pe.wait_ge(k.R.free, k.R.all())

        def project(ring, w, m):
            bank, free = ring.fill()
            pe.wait_ge(ring.free, free)
            for c in range(KD):
                mm = pe.matmul(bank, w[:, c, m * P:(m + 1) * P], self.uT[:, c, :], start=c == 0, stop=c == KD - 1)
                k.W.first(mm)
            mm.then_inc(ring.full, 1)

        def block():
            w, full, got = k.W.take()
            pe.wait_ge(full, got)
            return w.rearrange("p (k n) -> p k n", k=KD)

        w3 = []
        for m in range(4):
            for j, ring in enumerate((k.A, k.R, k.R)):
                if m == 0:
                    w3.append(block())
                project(ring, w3[j], m)
        k.W.owed += 3

        def turned(m):
            pe.wait_ge(self.silu, m + 1)
            bank, free = k.R.fill()
            pe.wait_ge(k.R.free, free)
            src = self.sil[:, m % 2, :] if m < 8 else self.bc[:, m - 8, :]
            for i in range(NT):
                mm = pe.transpose(bank[:, i * P:(i + 1) * P], src[:, i * P:(i + 1) * P], k.c("ident"))
            mm.then_inc(k.R.full, 1)

        bank, free = k.R.fill()
        pe.wait_ge(k.R.free, free)
        wdt = k.s("w_dt").rearrange("p (k n) -> p k n", k=KD)
        for i in range(NT):
            for c in range(KD):
                mm = pe.matmul(bank[:, i * SSM_H:(i + 1) * SSM_H], self.uT[:, c, i * P:(i + 1) * P], wdt[:, c, :],
                               start=c == 0, stop=c == KD - 1)
        mm.then_inc(k.R.full, 1)
        for m in range(12):
            if m % 4 == 0:
                w = block()
            project(k.A, w, m % 4)
            if m == 1:
                bank, free = k.R.fill()
                pe.wait_ge(k.R.free, free)
                pe.wait_ge(self.dt_first, 1)
                adt = self.adt.rearrange("p i h -> p (i h)")
                pe.matmul(bank[:, 0:64], k.c("upper"), adt, start=True, stop=True)
                pe.matmul(bank[:, 64:128], k.c("ones"), adt, start=True, stop=True).then_inc(k.R.full, 1)
            if m % 4 == 3:
                k.W.owed += 1
            if 2 <= m:
                turned(m - 2)
        wz = [block(), block()]

        def z_rows(i, n):
            bank, free = k.A.fill()
            pe.wait_ge(k.A.free, free)
            for c in range(KD):
                mm = pe.matmul(bank, self.uT[:, c, i * P:(i + 1) * P], wz[n][:, c, :], start=c == 0,
                               stop=c == KD - 1)
                k.W.first(mm)
            mm.then_inc(k.A.full, 1)

        for i in range(NT):
            tok = slice(i * P, (i + 1) * P)
            bank, free = k.R.fill()
            pe.wait_ge(k.R.free, free)
            pe.wait_ge(self.silu, 12)
            for g in range(SSM_G):
                mm = pe.matmul(bank[:, g * P:(g + 1) * P], self.bc[:, g, tok], self.bc[:, 2 + g, tok], start=True,
                               stop=True)
            mm.then_inc(k.R.full, 1)

            def segment(hb):
                n = 4 * i + hb
                bank, free = k.A.fill()
                pe.wait_ge(k.A.free, free)
                pe.wait_ge(self.g_ready, n + 1)
                pe.matmul(bank, k.c("slower"), self.G[:, n % 2, :], start=True, stop=True).then_inc(k.A.full, 1)

            def diagonal(bank, hb):
                n = 4 * i + hb
                pe.wait_ge(self.w_ready, n + 1)
                for j in range(4):
                    h = 4 * hb + j
                    mm = pe.matmul(bank[:, (h % 8) * SSM_P:(h % 8 + 1) * SSM_P],
                                   self.E[:, n % 2, j * P:(j + 1) * P], self.xdt[:, h * SSM_P:(h + 1) * SSM_P],
                                   start=True, stop=True)
                return mm

            segment(0)
            segment(1)
            if i:
                pe.wait_ge(self.state_ready, 2 * i)
                for g in range(SSM_G):
                    bank, free = k.R.fill()
                    pe.wait_ge(k.R.free, free)
                    pe.matmul(bank, self.bc[:, 2 + g, tok], self.state[:, g, :], start=True,
                              stop=True).then_inc(k.R.full, 1)
            z_rows(i, 0)
            pe.wait_ge(self.x_ready, 3 * i + 2)
            bank, free = k.R.fill()
            pe.wait_ge(k.R.free, free)
            diagonal(bank, 0)
            segment(2)
            mm = diagonal(bank, 1)
            mm.then_inc(k.R.full, 1)
            segment(3)
            z_rows(i, 1)
            bank, free = k.R.fill()
            pe.wait_ge(k.R.free, free)
            diagonal(bank, 2)
            mm = diagonal(bank, 3)
            mm.then_inc(k.R.full, 1)
            if i < NT - 1:
                for g in range(SSM_G):
                    bank, free = k.R.fill()
                    pe.wait_ge(k.R.free, free)
                    pe.matmul(bank, self.btok[:, i, g, :], self.xde[:, g * 512:(g + 1) * 512], start=True,
                              stop=True).then_inc(k.R.full, 1)
        k.W.owed += 2
        for i in range(NT):
            pe.wait_ge(self.normed, i + 1)
            for half in range(2):
                bank, free = k.R.fill()
                pe.wait_ge(k.R.free, free)
                for a in range(4):
                    c = 4 * half + a
                    mm = pe.transpose(bank[:, a * P:(a + 1) * P], self.xs[:, i, c * P:(c + 1) * P], k.c("ident"))
                    k.W.first(mm)
                mm.then_inc(k.R.full, 1)
        pe.wait_ge(k.R.free, k.R.all())
        project_rows(k, pe, [self.mixT[:, c, :] for c in range(MIXT)], self.memory.norm.pe)
        pe.drain().then_inc(k.W.free, k.W.owed)
        k.W = k.W6

    def act(self, act):
        k = self.k
        self.norm.act(act)
        act.wait_ge(k.sem("constants_loaded"), 32)
        for m in range(4):
            bank, full = k.A.empty()
            act.wait_ge(k.A.full, full)
            if m >= 2:
                act.wait_ge(k.R.free, k.R.stored(self.r0 + 8 + 2 * (m - 2) + 1))
            act.activation(self.cg[:, m % 2, :], bank, ACT.Copy).then_inc(k.A.free, 1)
        w, b = k.s("ssm_conv"), k.s("ssm_convb")

        def silu(m):
            act.wait_ge(self.conv, m + 1)
            if 2 <= m < 10:
                act.wait_ge(k.R.full, self.r0 + 18 + m - 2 + 1)
            dst = self.sil[:, m % 2, :] if m < 8 else self.bc[:, m - 8, :]
            act.activation(dst, self.acc[:, m % 2, :], ACT.Silu).then_inc(self.silu, 1)

        act.activation(self.ea, k.s("a_log"), ACT.Exp).then_inc(self.dte_out, 1)
        act.wait_ge(self.dte_in, 1)
        softplus_tail(act, self.t0, self.dt, self.dte_out, 1)
        act.wait_ge(self.pads, 2)
        for m in range(12):
            if m == 3:
                act.wait_ge(self.cexp, 1)
                act.activation(self.ecum, self.cum, ACT.Exp).then_inc(self.dte_out, 1)
                act.activation(self.etot, self.tot, ACT.Exp).then_inc(self.dte_out, 1)
                act.wait_ge(self.cexp, 2)
                act.activation(self.toend, self.t1, ACT.Exp).then_inc(self.dte_out, 1)
            bank, full = k.A.empty()
            act.wait_ge(k.A.full, full)
            if m >= 2:
                act.wait_ge(self.silu, m - 1)
            act.activation(self.xpad[:, m % 2, 3:3 + SEQ], bank, ACT.Copy)
            act.activation(self.acc[:, m % 2, :], bank, ACT.Identity, bias=b[:, m:m + 1],
                           scale=w[:, 4 * m + 3:4 * m + 4]).then_inc(k.A.free, 1)
            if m:
                silu(m - 1)
        silu(11)

        def z_rows(i, n):
            bank, full = k.A.empty()
            act.wait_ge(k.A.full, full)
            act.activation(self.z(i)[:, n * 512:(n + 1) * 512], bank, ACT.Copy).then_inc(k.A.free, 1)

        def gate(i):
            act.wait_ge(k.A.free, k.A.stored(k.A.emptied))
            act.activation(self.z(i), self.z(i), ACT.Silu).then_inc(self.z_ready, 1)

        for i in range(NT):
            if i == NT - 1:
                for j in range(i):
                    gate(j)
            for hb in range(4):
                bank, full = k.A.empty()
                act.wait_ge(k.A.full, full)
                act.activation(self.E[:, hb % 2, :], bank, ACT.Exp).then_inc(k.A.free, 1)
                if hb % 2:
                    z_rows(i, hb // 2)
        gate(NT - 1)
        for i in range(NT):
            self.square(act, i)
        act.wait_ge(self.sq_free, 1)
        act.activation(k.stat[:, 24:32], k.stat[:, 16:24], ACT.Sqrt).then_inc(self.roots, 1)
        self.memory.norm.act(act)

    def square(self, act, i):
        k = self.k
        act.wait_ge(self.gated, i + 1)
        for g in range(SSM_G):
            act.activation(self.z(i)[:, g * 512:(g + 1) * 512], self.xs[:, i, g * 512:(g + 1) * 512], ACT.Square,
                           accum_out=self.gsum[:, 2 * i + g:2 * i + g + 1]).then_inc(self.sums, 1)

    def dve(self, dve):
        k = self.k
        link = k.dlink
        self.norm.dve(dve)
        w = k.s("sc_conv")
        dve.memset(self.pad3[:, :, 0:2], 0.0).then_inc(self.pads, 1)
        dve.memset(self.xpad[:, :, 0:3], 0.0).then_inc(self.pads, 1)
        dve.wait_ge(self.pads, 2)
        for m in range(4):
            b = m % 2
            bank, full = k.R.empty()
            dve.wait_ge(k.R.full, full)
            dve.wait_ge(k.A.free, k.A.stored(self.a0 + m + 1))
            dve.tensor_tensor(self.pad3[:, b, 2:2 + SEQ], self.cg[:, b, :], bank, ALU.mult).then_inc(k.R.free, 1)
            dve.wait_ge(k.R.free, k.R.stored(k.R.emptied))
            link(dve.tensor_scalar(self.acc3[:, b, :], self.pad3[:, b, 0:SEQ], w[:, 3 * m:3 * m + 1], None, ALU.mult))
            for j in (1, 2):
                link(dve.scalar_tensor_tensor(self.acc3[:, b, :], self.pad3[:, b, j:j + SEQ],
                                              w[:, 3 * m + j:3 * m + j + 1], self.acc3[:, b, :], ALU.mult, ALU.add))
            bank, full = k.R.empty()
            dve.wait_ge(k.R.full, full)
            dve.tensor_tensor(self.mixT[:, m, :], self.acc3[:, b, :], bank, ALU.mult).then_inc(k.R.free, 1)
        w = k.s("ssm_conv")

        def store(m):
            bank, full = k.R.empty()
            dve.wait_ge(k.R.full, full)
            dst = self.xs[:, :, m * P:(m + 1) * P] if m < 8 else self.btok[:, :, m - 8, :]
            dve.tensor_copy(dst, bank.rearrange("p (i f) -> p i f", i=NT)).then_inc(k.R.free, 1)

        bank, full = k.R.empty()
        dve.wait_ge(k.R.full, full)
        bias = k.s("dt_bias").unsqueeze(1).broadcast_to([P, NT, SSM_H])
        dve.tensor_tensor(self.dt, bank[:, 0:64].rearrange("p (i h) -> p i h", i=NT), bias,
                          ALU.add).then_inc(k.R.free, 1)
        dve.wait_ge(k.R.free, k.R.stored(k.R.emptied))
        dve.sem_inc(self.dte_in, 1)
        dve.wait_ge(self.dte_out, 4)
        link(dve.scalar_tensor_tensor(self.dt, self.dt, 0.0, self.t0, ALU.max, ALU.add))
        ea = self.ea.unsqueeze(1).broadcast_to([P, NT, SSM_H])
        dve.scalar_tensor_tensor(self.adt, self.dt, -1.0, ea, ALU.mult, ALU.mult).then_inc(self.dt_first, 1)
        for m in range(12):
            dve.wait_ge(k.A.free, k.A.stored(self.a0 + 4 + m + 1))
            for j in range(3):
                ins = dve.scalar_tensor_tensor(self.acc[:, m % 2, :], self.xpad[:, m % 2, j:j + SEQ],
                                               w[:, 4 * m + j:4 * m + j + 1], self.acc[:, m % 2, :], ALU.mult, ALU.add)
                if j < 2:
                    link(ins)
                else:
                    ins.then_inc(self.conv, 1)
            if m == 1:
                bank, full = k.R.empty()
                dve.wait_ge(k.R.full, full)
                link(dve.tensor_copy(self.cum, bank[:, 0:64].rearrange("p (i h) -> p i h", i=NT)))
                dve.tensor_copy(self.tot, bank[:, 64:128].rearrange("p (i h) -> p i h", i=NT)).then_inc(k.R.free, 1)
                dve.wait_ge(k.R.free, k.R.stored(k.R.emptied))
                link(dve.tensor_tensor(self.t1, self.tot, self.cum, ALU.subtract))
                dve.sem_inc(self.cexp, 2)
            if m == 4:
                dve.wait_ge(self.dte_out, 7)
                dve.tensor_tensor(self.dte, self.dt, self.toend, ALU.mult).then_inc(self.dt_ready, 1)
            if m >= 2:
                store(m - 2)
        upper = k.c("upper").unsqueeze(1).broadcast_to([P, SSM_G, P])

        def gate(i):
            dve.wait_ge(self.z_ready, i + 1)
            dve.tensor_tensor(self.xs[:, i, :], self.xs[:, i, :], self.z(i), ALU.mult).then_inc(self.gated, 1)

        for i in range(NT):
            if i == NT - 1:
                for j in range(i):
                    gate(j)
            bank, full = k.R.empty()
            dve.wait_ge(k.R.full, full)
            dve.tensor_tensor(self.cb, bank[:, 0:256].rearrange("p (g t) -> p g t", g=2), upper,
                              ALU.mult).then_inc(k.R.free, 1)
            dve.wait_ge(k.R.free, k.R.stored(k.R.emptied))

            def weigh(hb):
                n = 4 * i + hb
                dve.wait_ge(k.A.free, k.A.stored(self.segment_turn(n) + 1))
                e = self.E[:, n % 2, :].rearrange("p (h t) -> p h t", h=4)
                cb = self.cb[:, hb // 2, :].unsqueeze(1).broadcast_to([P, 4, P])
                dve.tensor_tensor(e, e, cb, ALU.mult).then_inc(self.w_ready, 1)

            weigh(0)
            weigh(1)
            if i:
                for g in range(SSM_G):
                    bank, full = k.R.empty()
                    dve.wait_ge(k.R.full, full)
                    dve.tensor_tensor(self.off[g].rearrange("p (h d) -> p h d", h=8),
                                      bank.rearrange("p (h d) -> p h d", h=8),
                                      spread(self.ecum[:, i, 8 * g:8 * g + 8], SSM_P), ALU.mult).then_inc(k.R.free, 1)
                dve.wait_ge(k.R.free, k.R.stored(k.R.emptied))
            weigh(2)
            weigh(3)
            dve.wait_ge(self.x_ready, 3 * i + 3)
            for g in range(SSM_G):
                xs = self.xs[:, i, g * 512:(g + 1) * 512]
                if i:
                    link(dve.tensor_tensor(xs, xs, self.off[g], ALU.add))
                bank, full = k.R.empty()
                dve.wait_ge(k.R.full, full)
                dve.tensor_tensor(xs, xs, bank, ALU.add).then_inc(k.R.free, 1)
            if i < NT - 1:
                for g in range(SSM_G):
                    st = self.state[:, g, :]
                    if i:
                        s3 = st.rearrange("p (h d) -> p h d", h=8)
                        link(dve.tensor_tensor(s3, s3, spread(self.etot[:, i, 8 * g:8 * g + 8], SSM_P), ALU.mult))
                    bank, full = k.R.empty()
                    dve.wait_ge(k.R.full, full)
                    if i:
                        dve.tensor_tensor(st, st, bank, ALU.add).then_inc(k.R.free, 1)
                    else:
                        dve.tensor_copy(st, bank).then_inc(k.R.free, 1)
                dve.wait_ge(k.R.free, k.R.stored(k.R.emptied))
                dve.sem_inc(self.state_ready, 2)
        dve.wait_ge(k.R.free, k.R.stored(k.R.emptied))
        gate(NT - 1)
        dve.wait_ge(self.sums, 2 * NT)
        dve.tensor_scalar(k.stat[:, 16:24], self.gsum, SSM_G / SSM_INNER, EPS, ALU.mult,
                          ALU.add).then_inc(self.sq_free, 1)
        dve.wait_ge(self.roots, 1)
        link(dve.reciprocal(k.stat[:, 32:40], k.stat[:, 24:32]))
        for i in range(NT):
            y = self.xs[:, i, :].rearrange("p (g d) -> p g d", g=2)
            dve.tensor_tensor(y, y, spread(k.stat[:, 32 + 2 * i:34 + 2 * i], 512), ALU.mult).then_inc(self.normed, 1)
        for i in range(NT):
            for half in range(2):
                bank, full = k.R.empty()
                dve.wait_ge(k.R.full, full)
                dve.tensor_tensor(self.mixT[:, 4 + 4 * half:8 + 4 * half, i * P:(i + 1) * P],
                                  bank.rearrange("p (a t) -> p a t", a=4),
                                  spread(k.s("ssm_norm")[:, 4 * half:4 * half + 4], P), ALU.mult).then_inc(k.R.free, 1)
        add_rows(k, dve, self.memory.norm.dve)


def softplus_tail(act, x, src, done, base):
    act.activation(x, src, ACT.Abs).then_inc(done, 1)
    act.wait_ge(done, base + 1)
    act.activation(x, x, ACT.Exp, scale=-1.0).then_inc(done, 1)
    act.wait_ge(done, base + 2)
    act.activation(x, x, ACT.Ln, bias=1.0).then_inc(done, 1)



def over_heads(m, n=4):
    return m.unsqueeze(1).broadcast_to([P, n, m.shape[1]])


def in_order(setup, level, scan, gate=lambda i: None):
    for part in range(4):
        setup(0, part)
    for c in range(NT):
        for l in range(1, LEVELS):
            level(c, l, 0)
            if c and l == 1:
                scan(c - 1, 0)
            level(c, l, 1)
            if c and l < 3:
                scan(c - 1, l)
            if c < NT - 1 and l > 2:
                setup(c + 1, l - 3)
    scan(NT - 1, 0)
    gate(0)
    for part in (1, 2):
        scan(NT - 1, part)
    for i in range(1, NT):
        gate(i)


def half_turns():
    a = [("column", t) for t in range(12)] + [("turned back", t) for t in range(8)]
    r = [("turned", t) for t in range(12)]

    def setup(c, part):
        if part == 0:
            a.extend([("decay", c), ("growth", c)])
        elif part == 1:
            r.extend([("kk", c), ("qk", c)])
        elif part == 2:
            a.extend([("L'", c), ("qk'", c)])
        else:
            a.append(("T0'", c))

    def level(c, l, step):
        for two in range(2):
            if step == 0:
                a.append(("LT", c, l, two))
            else:
                r.extend([("T", c, l, two), ("T'", c, l, two)] if l < LEVELS - 1 else [("T'", c, l, two)])

    def scan(c, part):
        if part == 0 and c:
            r.append(("kS", c))
        elif part == 1:
            a.append(("new", c))
        elif part == 2:
            r.extend([("o", c), ("S", c)] if c < NT - 1 else [("o", c)])

    in_order(setup, level, scan, lambda i: a.append(("gate", i)))
    r.extend(("gated", i) for i in range(NT))
    return a, r


class Odd:

    A_TURNS, R_TURNS = half_turns()
    A_HALF, R_HALF = len(A_TURNS), len(R_TURNS)
    W_BLOCKS = 0
    PLACES = (1, 3, 4, 5, 2)
    A_JOBS = 2 * A_HALF + 12 + 8 * 5
    R_JOBS = 8 + 2 + 2 * R_HALF + 32 + 8 + MemoryRows.R_JOBS

    def __init__(self, k):
        self.k = k
        self.uT = k.at(0, 4096, k=KD)
        self.mixT = k.at(4096, 6144, k=MIXT)
        self.norm = Norm(k, lambda i: k.h[:, i, :], NT, k.s("g_mix1"), self.uT)
        self.memory = MemoryRows(k)
        self.qT = k.at(10240, 2048, h=4)
        self.kT = k.at(12288, 2048, h=4)
        self.ktok = k.at(14336, 2048, i=NT)
        self.vtok = k.at(16384, 2048, i=NT)
        self.qtok = k.at(6144, 2048, i=NT)
        self.xpad = k.at(18432, 2 * 516, b=2)
        self.acc = k.at(19464, 1024, b=2)
        self.sil = k.at(8192, 1024, b=2)
        self.sqr = k.at(9216, 1024, b=2)
        self.b = [k.at(8192 + 512 * j, 512, h=4) for j in range(4)] + [k.at(18432 + 512 * j, 512, h=4) for j in range(4)]
        self.state = k.at(20480, 512, h=4)
        per = lambda j: k.decays[:, 32 * j:32 * j + 32].rearrange("p (i h) -> p i h", i=NT)
        self.g, self.beta, self.egl, self.etot = per(0), per(1), per(2), per(3)
        tmp = lambda j: k.at(20496 + 32 * j, 32, i=NT)
        self.araw, self.braw, self.t0, self.cum, self.ebeta, self.den = [tmp(j) for j in range(6)]
        self.ea = k.at(20496 + 32 * 6, GH)
        self.sq = k.at(10240, 2048, m=4)
        self.sk = k.at(12288, 2048, m=4)
        self.sv = k.at(14336, 2048, i=NT)
        s = lambda n: k.sem(f"gdn_{n}")
        self.pads, self.conv, self.silu = s("pads"), s("convolved"), s("silu")
        self.gin, self.gout, self.gready, self.cin = s("gates_in"), s("gates_out"), s("decays_ready"), s("cum_in")
        self.squares, self.ssum, self.means, self.roots, self.recip, self.qscaled, self.kscaled = (
            s("squares"), s("square_sums"), s("means"), s("roots"), s("reciprocals"), s("q_scaled"), s("k_scaled"))
        self.seg, self.edec, self.dmask, self.tinit, self.lmask, self.kd, self.rhs, self.done = (
            s("segments_in"), s("decayed_qk"), s("decay_masked"), s("inverse_begun"), s("level_masked"), s("k_decayed"),
            s("rhs_ready"), s("chunk_done"))
        self.gatedz = s("gated")
        t = lambda n: k.sem(f"stick_{n}")
        self.sa, self.se, self.ssp, self.sw, self.swm = (
            t("sizes"), t("softplus"), t("softplus_masked"), t("weights"), t("weights_masked"))

    def loads(self):
        w = self.k.dram["od_w_in"][0]
        cols = []
        for hf in range(2):
            cols += [512 * hf, 1024 + 512 * hf, 2048 + 512 * hf, 3072 + 512 * hf]
        base = 4 * GH * GDK + 2 * GH
        cols += [base, base + 512, base + 1024]
        for c in cols:
            yield w[:, c:c + 512].rearrange("(k p) n -> p k n", p=P)
        for j in range(3):
            yield self.k.dram["od_w_out"][0][j * 512:(j + 1) * 512, :].rearrange("(k p) n -> p k n", p=P)

    def sp(self, sp):
        load_own_ring(self.k, sp, "odd", self.w0, self.PLACES, self.loads(),
                      (self.k.A.free, self.k.A.stored(self.a0 + self.A_JOBS)))

    def A(self, hf, *key):
        return self.a0 + hf * self.A_HALF + self.A_TURNS.index(key)

    def R(self, hf, *key):
        return self.r0 + 10 + hf * self.R_HALF + self.R_TURNS.index(key)

    def stored_a(self, hf, *key):
        return self.k.A.stored(self.A(hf, *key) + 1)

    def stored_r(self, hf, *key):
        return self.k.R.stored(self.R(hf, *key) + 1)

    def buffers(self, c):
        if c % 2 == 0:
            return self.b
        slot = self.k.W6.slots[self.w0 % WSLOTS].rearrange("p (j h t) -> p j h t", j=8, h=4)
        return [slot[:, j, :, :] for j in range(8)]

    def stick_buffers(self):
        k = self.k
        slot = k.W6.slots[self.w0 % WSLOTS]
        return [k.at(16384, 1280), slot[:, 0:1280]], [k.at(17664, 1280), k.at(18944, 1280), slot[:, 1280:2560]]

    def pe(self, pe):
        k = self.k
        self.norm.pe(pe)
        k.W = own_ring(k, "odd", self.w0, self.PLACES)
        pe.sem_inc(k.W.free, len(self.PLACES))
        pe.wait_ge(k.R.free, k.R.all())
        bank, free = k.R.fill()
        pe.wait_ge(k.R.free, free)
        wab = k.s("w_ab").rearrange("p (k n) -> p k n", k=KD)
        for i in range(NT):
            for c in range(KD):
                mm = pe.matmul(bank[:, i * 16:(i + 1) * 16], self.uT[:, c, i * P:(i + 1) * P], wab[:, c, :],
                               start=c == 0, stop=c == KD - 1)
        mm.then_inc(k.R.full, 1)
        for hf in range(2):
            self.pe_project(pe, hf)
            w = self.block(pe)
            in_order(*(lambda c, *part, f=f: f(pe, hf, c, *part) for f in (self.pe_setup, self.pe_level, self.pe_scan)),
                     lambda i: self.rows(pe, w, i))
            self.pe_gate(pe, hf)
        self.pe_stick(pe)
        project_rows(k, pe, [self.mixT[:, c, :] for c in range(MIXT)], self.memory.norm.pe)
        pe.drain().then_inc(k.W.free, k.W.owed)
        k.W = k.W6

    def block(self, pe):
        w, full, got = self.k.W.take()
        pe.wait_ge(full, got)
        return w.rearrange("p (k n) -> p k n", k=KD)

    def columns(self, pe, w, m):
        k = self.k
        bank, free = k.A.fill()
        pe.wait_ge(k.A.free, free)
        for c in range(KD):
            mm = pe.matmul(bank, w[:, c, m * P:(m + 1) * P], self.uT[:, c, :], start=c == 0, stop=c == KD - 1)
            k.W.first(mm)
        mm.then_inc(k.A.full, 1)

    def rows(self, pe, w, i):
        k = self.k
        bank, free = k.A.fill()
        pe.wait_ge(k.A.free, free)
        for c in range(KD):
            mm = pe.matmul(bank, self.uT[:, c, i * P:(i + 1) * P], w[:, c, :], start=c == 0, stop=c == KD - 1)
            k.W.first(mm)
        mm.then_inc(k.A.full, 1)

    def four(self, pe, ring, f, turn=None, heads=range(4)):
        assert turn is None or turn == ring.filled
        bank, free = ring.fill()
        pe.wait_ge(ring.free, free)
        for h in heads:
            mm = f(bank[:, h * P:(h + 1) * P], h)
        mm.then_inc(ring.full, 1)

    def pe_project(self, pe, hf):
        k = self.k

        def turned(t):
            pe.wait_ge(self.silu, 12 * hf + t + 1)
            self.four(pe, k.R, lambda out, i: pe.transpose(out, self.sil[:, t % 2, i * P:(i + 1) * P], k.c("ident")))

        for t in range(12):
            if t % 4 == 0:
                w = self.block(pe)
            self.columns(pe, w, t % 4)
            if (hf, t) == (0, 1):
                bank, free = k.R.fill()
                pe.wait_ge(k.R.free, free)
                pe.wait_ge(self.cin, 1)
                g = self.g.rearrange("p i h -> p (i h)")
                pe.matmul(bank[:, 0:32], k.c("upper"), g, start=True, stop=True)
                pe.matmul(bank[:, 32:64], k.c("ones"), g, start=True, stop=True).then_inc(k.R.full, 1)
            if t % 4 == 3:
                k.W.owed += 1
            if t >= 2:
                turned(t - 2)
        turned(10)
        turned(11)
        for x, scaled in ((self.qtok, self.qscaled), (self.ktok, self.kscaled)):
            pe.wait_ge(scaled, 4 * hf + 4)
            for h in range(4):
                self.four(pe, k.A, lambda out, i: pe.transpose(out, x[:, i, h * P:(h + 1) * P], k.c("ident")))

    def pe_setup(self, pe, hf, c, part):
        k, n, b = self.k, 4 * hf + c, self.buffers(c)
        tok = slice(c * P, (c + 1) * P)
        if part == 0:
            for key, lhs, rhs in (("decay", "upper", b[1]), ("growth", "ones", b[0])):
                assert k.A.filled == self.A(hf, key, c)
                bank, free = k.A.fill()
                pe.wait_ge(k.A.free, free)
                pe.wait_ge(self.seg, 2 * n + 2)
                pe.matmul(bank, k.c(lhs), rhs.rearrange("p h t -> p (h t)"), start=True, stop=True).then_inc(k.A.full, 1)
        elif part == 1:
            if c == 0:
                pe.wait_ge(k.A.free, self.stored_a(hf, "turned back", 7))
            self.four(pe, k.R, lambda out, h: pe.matmul(out, self.kT[:, h, tok], self.kT[:, h, tok], start=True,
                                                        stop=True), self.R(hf, "kk", c))
            self.four(pe, k.R, lambda out, h: pe.matmul(out, self.qT[:, h, tok], self.kT[:, h, tok], start=True,
                                                        stop=True), self.R(hf, "qk", c))
        elif part == 2:
            pe.wait_ge(k.R.free, self.stored_r(hf, "qk", c))
            self.four(pe, k.A, lambda out, h: pe.transpose(out, b[0][:, h, :], k.c("ident")), self.A(hf, "L'", c))
            self.four(pe, k.A, lambda out, h: pe.transpose(out, b[2][:, h, :], k.c("ident")), self.A(hf, "qk'", c))
        else:
            pe.wait_ge(self.tinit, n + 1)
            self.four(pe, k.A, lambda out, h: pe.transpose(out, b[6][:, h, :], k.c("ident")), self.A(hf, "T0'", c))

    def pe_level(self, pe, hf, c, l, step):
        k, n, b = self.k, 4 * hf + c, self.buffers(c)
        product = lambda x, y: lambda out, h: pe.matmul(out, x[:, h, :], y[:, h, :], start=True, stop=True)
        for two in range(2):
            heads = range(2 * two, 2 * two + 2)
            if step == 0:
                pe.wait_ge(self.lmask, 6 * n + l)
                if l > 1:
                    pe.wait_ge(k.R.free, self.stored_r(hf, "T", c, l - 1, two))
                self.four(pe, k.A, product(b[2], b[6]), self.A(hf, "LT", c, l, two), heads)
                continue
            if l > 1:
                pe.wait_ge(k.R.free, self.stored_r(hf, "T'", c, l - 1, two))
            pe.wait_ge(k.A.free, self.stored_a(hf, "LT", c, l, two))
            if l < LEVELS - 1:
                self.four(pe, k.R, product(b[7], b[0]), self.R(hf, "T", c, l, two), heads)
            self.four(pe, k.R, product(b[0], b[7]), self.R(hf, "T'", c, l, two), heads)

    def pe_scan(self, pe, hf, c, part):
        k, n, b, state = self.k, 4 * hf + c, self.buffers(c), self.state
        if part == 0:
            if c:
                pe.wait_ge(self.edec, 2 * n + 2)
                pe.wait_ge(self.done, n)
                self.four(pe, k.R, lambda out, h: pe.matmul(out, b[5][:, h, :], state[:, h, :], start=True, stop=True),
                          self.R(hf, "kS", c))
        elif part == 1:
            pe.wait_ge(k.R.free, self.stored_r(hf, "T'", c, LEVELS - 1, 1))
            pe.wait_ge(self.rhs, n + 1)
            self.four(pe, k.A, lambda out, h: pe.matmul(out, b[7][:, h, :], b[6][:, h, :], start=True, stop=True),
                      self.A(hf, "new", c))
        else:
            pe.wait_ge(k.A.free, self.stored_a(hf, "new", c))

            def out_rows(out, h):
                if c:
                    pe.matmul(out, b[4][:, h, :], state[:, h, :], start=True, stop=False)
                return pe.matmul(out, b[3][:, h, :], b[0][:, h, :], start=c == 0, stop=True)

            self.four(pe, k.R, out_rows, self.R(hf, "o", c))
            if c < NT - 1:
                pe.wait_ge(self.kd, n + 1 - hf)
                self.four(pe, k.R, lambda out, h: pe.matmul(out, b[1][:, h, :], b[0][:, h, :], start=True, stop=True),
                          self.R(hf, "S", c))

    def pe_gate(self, pe, hf):
        k = self.k
        k.W.owed += 1
        for i in range(NT):
            pe.wait_ge(self.gatedz, 4 * hf + i + 1)
            bank, free = k.R.fill()
            pe.wait_ge(k.R.free, free)
            for j in range(4):
                mm = pe.transpose(bank[:, j * P:(j + 1) * P], self.vtok[:, i, j * P:(j + 1) * P], k.c("ident"))
                k.W.first(mm)
            mm.then_inc(k.R.full, 1)

    def width(self, kt):
        return SEQ - kt * P

    def span(self, x, kt):
        at = sum(self.width(j) for j in range(kt))
        return x[:, at:at + self.width(kt)]

    def pe_stick(self, pe):
        k = self.k
        pe.wait_ge(k.R.free, k.R.all())
        for _ in range(2):
            w = self.block(pe)
            for m in range(4):
                self.columns(pe, w, m)
            k.W.owed += 1
        w = self.block(pe)
        for i in range(NT):
            self.rows(pe, w, i)
        k.W.owed += 1
        pe.wait_ge(k.A.free, k.A.all())

        sps, lgs = self.stick_buffers()

        def logits(hh):
            m, at = hh // 2, SBD * (hh % 2)
            for kt in reversed(range(NT)):
                bank, free = k.A.fill()
                pe.wait_ge(k.A.free, free)
                pe.matmul(bank[:, 0:self.width(kt)], self.sk[at:at + SBD, m, kt * P:(kt + 1) * P],
                          self.sq[at:at + SBD, m, kt * P:SEQ], start=True, stop=True).then_inc(k.A.full, 1)

        def between(hh):
            for j, kt in enumerate(reversed(range(NT))):
                pe.wait_ge(self.ssp, 4 * hh + j + 1)
                bank, free = k.R.fill()
                pe.wait_ge(k.R.free, free)
                for later in range(kt, NT):
                    mm = pe.matmul(bank[:, (later - kt) * P:self.width(kt)],
                                   k.c("lower") if later == kt else k.c("ones"), self.span(sps[hh % 2], later),
                                   start=later == kt, stop=later == NT - 1)
                mm.then_inc(k.R.full, 1)

        def values(hh):
            pe.wait_ge(self.swm, 4 * hh + 4)
            at = SBD * (hh % 2)
            bank, free = k.A.fill()
            pe.wait_ge(k.A.free, free)
            for kt in range(NT):
                mm = pe.matmul(bank[at:at + SBD, kt * P:SEQ], self.sv[:, kt, hh * SBD:(hh + 1) * SBD],
                               self.span(lgs[hh % 3], kt), start=kt == 0, stop=kt == NT - 1)
            mm.then_inc(k.A.full, 1)

        logits(0)
        for hh in range(SBH):
            if hh < SBH - 1:
                logits(hh + 1)
            between(hh)
            if hh:
                values(hh - 1)
        values(SBH - 1)
        pe.wait_ge(k.A.free, k.A.all())
        pe.wait_ge(k.R.free, k.R.all())

    def act(self, act):
        k = self.k
        self.norm.act(act)
        act.activation(self.ea, k.s("gdn_alog"), ACT.Exp).then_inc(self.gout, 1)
        act.wait_ge(self.gin, 1)
        softplus_tail(act, self.t0, self.araw, self.gout, 1)
        act.activation(self.ebeta, self.braw, ACT.Exp, scale=-1.0).then_inc(self.gout, 1)
        for hf in range(2):
            self.act_project(act, hf)
            in_order(*(lambda c, *part, f=f: f(act, hf, c, *part)
                       for f in (self.act_setup, self.act_level, self.act_scan)),
                     lambda i: self.act_gate(act, hf, i))
        self.act_stick(act)
        self.memory.norm.act(act)

    def act_project(self, act, hf):
        k = self.k
        w = k.s("gdn_conv")
        act.wait_ge(self.pads, hf + 1)

        def silu(t):
            n = 12 * hf + t
            act.wait_ge(self.conv, n + 1)
            if t >= 2:
                act.wait_ge(k.R.full, self.R(hf, "turned", t - 2) + 1)
            act.activation(self.sil[:, t % 2, :], self.acc[:, t % 2, :], ACT.Silu).then_inc(self.silu, 1)

        for t in range(12):
            if (hf, t) == (0, 3):
                act.wait_ge(self.gin, 2)
                act.activation(self.egl, self.egl, ACT.Exp).then_inc(self.gout, 1)
                act.activation(self.etot, self.etot, ACT.Exp).then_inc(self.gout, 1)
            if t == 11:
                act.wait_ge(self.means, 2 * hf + 1)
                act.activation(k.stat[:, 16:48], k.stat[:, 16:48], ACT.Sqrt).then_inc(self.roots, 1)
            bank, full = k.A.empty()
            act.wait_ge(k.A.full, full)
            if t >= 2:
                act.wait_ge(self.silu, 12 * hf + t - 1)
            tile = 8 * (t // 4) + 4 * hf + t % 4
            act.activation(self.xpad[:, t % 2, 3:3 + SEQ], bank, ACT.Copy)
            act.activation(self.acc[:, t % 2, :], bank, ACT.Copy,
                           scale=w[:, 4 * tile + 3:4 * tile + 4]).then_inc(k.A.free, 1)
            if t:
                silu(t - 1)
        silu(11)
        for x in (self.qT, self.kT):
            for h in range(4):
                bank, full = k.A.empty()
                act.wait_ge(k.A.full, full)
                act.activation(x[:, h, :], bank, ACT.Copy).then_inc(k.A.free, 1)

    def act_store(self, act, dst, func=ACT.Copy):
        k = self.k
        bank, full = k.A.empty()
        act.wait_ge(k.A.full, full)
        act.activation(dst, bank.rearrange("p (h t) -> p h t", h=4), func).then_inc(k.A.free, 1)

    def act_setup(self, act, hf, c, part):
        n, b = 4 * hf + c, self.buffers(c)
        if part == 0:
            if hf or c > 1:
                act.wait_ge(self.done, max(n - 1, 4 * hf))
            self.act_store(act, b[2], ACT.Exp)
            self.act_store(act, b[3], ACT.Exp)
        elif part == 2:
            self.act_store(act, b[1])
            act.wait_ge(self.edec, 2 * n + 2)
            self.act_store(act, b[3])
        elif part == 3:
            self.act_store(act, b[7])

    def act_level(self, act, hf, c, l, step):
        if step == 0:
            for two in range(2):
                bank, full = self.k.A.empty()
                act.wait_ge(self.k.A.full, full)
                heads = slice(2 * two, 2 * two + 2)
                act.activation(self.buffers(c)[0][:, heads, :], bank.rearrange("p (h t) -> p h t", h=4)[:, heads, :],
                               ACT.Copy).then_inc(self.k.A.free, 1)

    def act_scan(self, act, hf, c, part):
        if part == 1:
            self.act_store(act, self.buffers(c)[0])

    def act_gate(self, act, hf, i):
        k = self.k
        bank, full = k.A.empty()
        act.wait_ge(k.A.full, full)
        if i == 0:
            act.wait_ge(self.done, 4 * hf + 3)
        act.activation(self.b[4 + i], bank.rearrange("p (h t) -> p h t", h=4), ACT.Silu).then_inc(k.A.free, 1)
        if i == 1:
            act.wait_ge(self.means, 2 * hf + 2)
            act.activation(k.stat[:, 16:32], k.stat[:, 16:32], ACT.Sqrt).then_inc(self.roots, 1)

    def act_stick(self, act):
        k = self.k
        for x, scale in ((self.sq, SBD ** -0.5), (self.sk, 1.0)):
            for m in range(4):
                bank, full = k.A.empty()
                act.wait_ge(k.A.full, full)
                act.activation(x[:, m, :], bank, ACT.Copy, scale=scale).then_inc(k.A.free, 1)
        for i in range(NT):
            bank, full = k.A.empty()
            act.wait_ge(k.A.full, full)
            act.activation(self.sv[:, i, :], bank, ACT.Copy).then_inc(k.A.free, 1)

        def store_values(hh):
            at = SBD * (hh % 2)
            bank, full = k.A.empty()
            act.wait_ge(k.A.full, full)
            act.activation(self.mixT[at:at + SBD, 8 + hh // 2, :], bank[at:at + SBD, :], ACT.Copy).then_inc(k.A.free, 1)

        r0 = self.r0 + 10 + 2 * self.R_HALF
        sps, lgs = self.stick_buffers()

        def softplus(hh):
            for kt in reversed(range(NT)):
                bank, full = k.A.empty()
                act.wait_ge(k.A.full, full)
                act.activation(self.span(lgs[hh % 3], kt), bank[:, 0:self.width(kt)], ACT.Copy).then_inc(k.A.free, 1)
            for j, kt in enumerate(reversed(range(NT))):
                act.wait_ge(self.sa, 4 * hh + j + 1)
                sp = self.span(sps[hh % 2], kt)
                act.activation(sp, sp, ACT.Exp, scale=-1.0).then_inc(self.se, 1)
            for j, kt in enumerate(reversed(range(NT))):
                act.wait_ge(self.se, 8 * hh + j + 1)
                sp = self.span(sps[hh % 2], kt)
                act.activation(sp, sp, ACT.Ln, bias=1.0).then_inc(self.se, 1)

        softplus(0)
        for hh in range(SBH):
            if hh < SBH - 1:
                softplus(hh + 1)
            for j, kt in enumerate(reversed(range(NT))):
                act.wait_ge(k.R.free, k.R.stored(r0 + 4 * hh + j + 1))
                lt = self.span(lgs[hh % 3], kt)
                act.activation(lt, lt, ACT.Exp).then_inc(self.sw, 1)
            if hh:
                store_values(hh - 1)
        store_values(SBH - 1)

    def dve(self, dve):
        k, link = self.k, self.k.dlink
        self.norm.dve(dve)
        bank, full = k.R.empty()
        dve.wait_ge(k.R.full, full)
        raw = bank[:, 0:64].rearrange("p (i n) -> p i n", i=NT)
        bias = k.s("gdn_dtb").unsqueeze(1).broadcast_to([P, NT, GH])
        link(dve.tensor_tensor(self.araw, raw[:, :, 0:GH], bias, ALU.add))
        dve.tensor_copy(self.braw, raw[:, :, GH:2 * GH]).then_inc(k.R.free, 1)
        dve.wait_ge(k.R.free, k.R.stored(k.R.emptied))
        dve.sem_inc(self.gin, 1)
        dve.wait_ge(self.gout, 5)
        link(dve.scalar_tensor_tensor(self.t0, self.araw, 0.0, self.t0, ALU.max, ALU.add))
        ea = self.ea.unsqueeze(1).broadcast_to([P, NT, GH])
        dve.scalar_tensor_tensor(self.g, self.t0, -1.0, ea, ALU.mult, ALU.mult).then_inc(self.cin, 1)
        link(dve.tensor_scalar(self.den, self.ebeta, 1.0, None, ALU.add))
        link(dve.reciprocal(self.beta, self.den))
        for hf in range(2):
            self.dve_project(dve, hf)
            in_order(*(lambda c, *part, f=f: f(dve, hf, c, *part)
                       for f in (self.dve_setup, self.dve_level, self.dve_scan)))
            self.dve_gate(dve, hf)
        self.dve_stick(dve)
        add_rows(k, dve, self.memory.norm.dve)

    def dve_project(self, dve, hf):
        k, link = self.k, self.k.dlink
        w = k.s("gdn_conv")
        dve.memset(self.xpad[:, :, 0:3], 0.0).then_inc(self.pads, 1)
        dve.wait_ge(self.pads, hf + 1)

        def store(t):
            bank, full = k.R.empty()
            dve.wait_ge(k.R.full, full)
            dst = (self.qtok, self.ktok, self.vtok)[t // 4]
            dve.tensor_copy(dst[:, :, (t % 4) * P:(t % 4 + 1) * P],
                            bank.rearrange("p (i f) -> p i f", i=NT)).then_inc(k.R.free, 1)

        for t in range(12):
            dve.wait_ge(k.A.free, self.stored_a(hf, "column", t))
            tile = 8 * (t // 4) + 4 * hf + t % 4
            for j in range(3):
                ins = dve.scalar_tensor_tensor(self.acc[:, t % 2, :], self.xpad[:, t % 2, j:j + SEQ],
                                               w[:, 4 * tile + j:4 * tile + j + 1], self.acc[:, t % 2, :], ALU.mult,
                                               ALU.add)
                if j < 2:
                    link(ins)
                else:
                    ins.then_inc(self.conv, 1)
            if (hf, t) == (0, 1):
                bank, full = k.R.empty()
                dve.wait_ge(k.R.full, full)
                link(dve.tensor_copy(self.cum, bank[:, 0:32].rearrange("p (i h) -> p i h", i=NT)))
                dve.tensor_copy(self.etot, bank[:, 32:64].rearrange("p (i h) -> p i h", i=NT)).then_inc(k.R.free, 1)
                dve.wait_ge(k.R.free, k.R.stored(k.R.emptied))
                dve.tensor_tensor(self.egl, self.etot, self.cum, ALU.subtract).then_inc(self.gin, 1)
            if (hf, t) == (0, 4):
                dve.wait_ge(self.gout, 7)
                dve.sem_inc(self.gready, 1)
            if t >= 2:
                store(t - 2)
            for n in {6: (0, 1), 7: (2, 3), 10: (4, 5, 6, 7)}.get(t, ()):
                self.reduce_square(dve, 12 * hf + n, k.stat[:, 16 + 4 * n:20 + 4 * n])
            if t == 10:
                dve.wait_ge(self.ssum, 12 * hf + 8)
                dve.tensor_scalar(k.stat[:, 16:48], k.stat[:, 16:48], EPS, None, ALU.add).then_inc(self.means, 1)
                dve.wait_ge(self.roots, 2 * hf + 1)
                link(dve.reciprocal(k.stat[:, 16:48], k.stat[:, 16:48]))
                dve.tensor_scalar(k.stat[:, 16:32], k.stat[:, 16:32], GDK ** -0.5, None,
                                  ALU.mult).then_inc(self.recip, 1)
        store(10)
        store(11)
        for i in range(NT):
            xi = self.ktok[:, i, :].rearrange("p (h d) -> p h d", h=4)
            dve.tensor_tensor(xi, xi, spread(k.stat[:, 32 + 4 * i:36 + 4 * i], P), ALU.mult).then_inc(self.kscaled, 1)

    def reduce_square(self, dve, n, dst):
        dve.wait_ge(self.squares, n + 1)
        dve.tensor_reduce(dst, self.sqr[:, n % 2, :].rearrange("p (h d) -> p h d", h=4), AX.X,
                          ALU.add).then_inc(self.ssum, 1)

    def dve_setup(self, dve, hf, c, part):
        k, n, b, link = self.k, 4 * hf + c, self.buffers(c), self.k.dlink
        tok = slice(c * P, (c + 1) * P)
        if part == 1:
            dve.wait_ge(k.A.free, self.stored_a(hf, "growth", c))
            dve.tensor_tensor(b[4], self.qT[:, :, tok], b[3], ALU.mult).then_inc(self.edec, 1)
            dve.tensor_tensor(b[5], self.kT[:, :, tok], b[3], ALU.mult).then_inc(self.edec, 1)
            bank, full = k.R.empty()
            dve.wait_ge(k.R.full, full)
            dve.wait_ge(self.dmask, 2 * n + 2)
            dve.scalar_tensor_tensor(b[0].rearrange("p h t -> p (h t)"), bank, -1.0,
                                     b[0].rearrange("p h t -> p (h t)"), ALU.mult, ALU.mult).then_inc(k.R.free, 1)
            bank, full = k.R.empty()
            dve.wait_ge(k.R.full, full)
            dve.tensor_tensor(b[2], bank.rearrange("p (h t) -> p h t", h=4), b[2], ALU.mult).then_inc(k.R.free, 1)
        elif part == 2:
            dve.wait_ge(k.R.free, self.stored_r(hf, "kk", c))
            link(dve.tensor_tensor(b[6], b[0], over_heads(k.c("below0")), ALU.mult))
            dve.tensor_tensor(b[6], b[6], over_heads(k.c("ident")), ALU.add).then_inc(self.tinit, 1)

    def dve_level(self, dve, hf, c, l, step):
        k, b = self.k, self.buffers(c)
        if step == 1:
            for two in range(2):
                heads = slice(2 * two, 2 * two + 2)
                for t in (b[6], b[7]) if l < LEVELS - 1 else (b[7],):
                    bank, full = k.R.empty()
                    dve.wait_ge(k.R.full, full)
                    dve.tensor_tensor(t[:, heads, :], t[:, heads, :],
                                      bank.rearrange("p (h t) -> p h t", h=4)[:, heads, :],
                                      ALU.add).then_inc(k.R.free, 1)

    def dve_scan(self, dve, hf, c, part):
        k, n, b, link, state = self.k, 4 * hf + c, self.buffers(c), self.k.dlink, self.state
        four = lambda bank: bank.rearrange("p (h t) -> p h t", h=4)
        heads = slice(4 * hf, 4 * hf + 4)
        if part == 0:
            v = self.vtok[:, c, :].rearrange("p (h d) -> p h d", h=4)
            dve.wait_ge(k.A.full, self.A(hf, "LT", c, LEVELS - 1, 1) + 1)
            if c:
                bank, full = k.R.empty()
                dve.wait_ge(k.R.full, full)
                dve.tensor_tensor(b[6], v, four(bank), ALU.subtract).then_inc(k.R.free, 1)
                dve.wait_ge(k.R.free, self.stored_r(hf, "kS", c))
                v = b[6]
            dve.tensor_tensor(b[6], v, spread(self.beta[:, c, heads], P), ALU.mult).then_inc(self.rhs, 1)
        elif part == 2:
            bank, full = k.R.empty()
            dve.wait_ge(k.R.full, full)
            dve.tensor_copy(self.vtok[:, c, :], bank).then_inc(k.R.free, 1)
            if c < NT - 1:
                if c:
                    link(dve.tensor_tensor(state, state, spread(self.etot[:, c, heads], P), ALU.mult))
                bank, full = k.R.empty()
                dve.wait_ge(k.R.full, full)
                if c:
                    dve.tensor_tensor(state, state, four(bank), ALU.add).then_inc(k.R.free, 1)
                else:
                    dve.tensor_copy(state, four(bank)).then_inc(k.R.free, 1)
            dve.wait_ge(k.R.free, k.R.stored(k.R.emptied))
            dve.sem_inc(self.done, 1)

    def dve_gate(self, dve, hf):
        k, link = self.k, self.k.dlink
        for i in range(NT):
            self.reduce_square(dve, 12 * hf + 8 + i, k.stat[:, 16 + 4 * i:20 + 4 * i])
        dve.wait_ge(self.ssum, 12 * hf + 12)
        dve.tensor_scalar(k.stat[:, 16:32], k.stat[:, 16:32], 1.0 / GDK, EPS, ALU.mult, ALU.add).then_inc(self.means, 1)
        dve.wait_ge(self.roots, 2 * hf + 2)
        dve.reciprocal(k.stat[:, 16:32], k.stat[:, 16:32]).then_inc(self.recip, 1)
        for i in range(NT):
            bank, full = k.R.empty()
            dve.wait_ge(k.R.full, full)
            dve.tensor_scalar(self.mixT[:, 4 * hf:4 * hf + 4, i * P:(i + 1) * P],
                              bank.rearrange("p (h t) -> p h t", h=4), k.s("gdn_norm"), None,
                              ALU.mult).then_inc(k.R.free, 1)

    def dve_stick(self, dve):
        k, link = self.k, self.k.dlink
        mask = k.c("supper")
        sps, lgs = self.stick_buffers()
        a0 = self.a0 + 2 * self.A_HALF + 12

        def sizes(hh):
            for j, kt in enumerate(reversed(range(NT))):
                dve.wait_ge(k.A.free, k.A.stored(a0 + 4 * hh + max(hh - 2, 0) + j + 1))
                sp, lt = self.span(sps[hh % 2], kt), self.span(lgs[hh % 3], kt)
                dve.scalar_tensor_tensor(sp, lt, -1.0, lt, ALU.mult, ALU.max).then_inc(self.sa, 1)

        def softplus(hh):
            for j, kt in enumerate(reversed(range(NT))):
                dve.wait_ge(self.se, 8 * hh + 4 + j + 1)
                sp, lt = self.span(sps[hh % 2], kt), self.span(lgs[hh % 3], kt)
                link(dve.scalar_tensor_tensor(sp, lt, 0.0, sp, ALU.max, ALU.add))
                dve.tensor_tensor(sp[:, 0:P], sp[:, 0:P], mask, ALU.mult).then_inc(self.ssp, 1)

        sizes(0)
        softplus(0)
        for hh in range(SBH):
            if hh < SBH - 1:
                sizes(hh + 1)
            for kt in reversed(range(NT)):
                lt = self.span(lgs[hh % 3], kt)
                bank, full = k.R.empty()
                dve.wait_ge(k.R.full, full)
                dve.tensor_tensor(lt, lt, bank[:, 0:self.width(kt)], ALU.subtract).then_inc(k.R.free, 1)
            if hh < SBH - 1:
                softplus(hh + 1)
            for j, kt in enumerate(reversed(range(NT))):
                dve.wait_ge(self.sw, 4 * hh + j + 1)
                lt = self.span(lgs[hh % 3], kt)
                dve.scalar_tensor_tensor(lt[:, 0:P], lt[:, 0:P], 1.0, mask, ALU.min, ALU.mult).then_inc(self.swm, 1)

    def pool(self, pool):
        k = self.k
        for hf in range(2):
            for kind, x in enumerate((self.qtok, self.ktok)):
                for i in range(NT):
                    n = 12 * hf + 4 * kind + i
                    if i == 0:
                        pool.wait_ge(k.R.free, self.stored_r(hf, "turned", 4 * kind + 3))
                    self.square(pool, n, x[:, i, :])
            pool.wait_ge(self.recip, 2 * hf + 1)
            for i in range(NT):
                xi = self.qtok[:, i, :].rearrange("p (h d) -> p h d", h=4)
                pool.tensor_tensor(xi, xi, spread(k.stat[:, 16 + 4 * i:20 + 4 * i], P), ALU.mult).then_inc(self.qscaled, 1)
            pool.wait_ge(self.gready, 1)
            in_order(*(lambda c, *part, f=f: f(pool, hf, c, *part)
                       for f in (self.pool_setup, self.pool_level, self.pool_scan)))
            pool.wait_ge(self.done, 4 * hf + 4)
            for i in range(NT):
                self.square(pool, 12 * hf + 8 + i, self.vtok[:, i, :])
            pool.wait_ge(self.recip, 2 * hf + 2)
            for i in range(NT):
                o = self.vtok[:, i, :].rearrange("p (h d) -> p h d", h=4)
                k.plink(pool.tensor_tensor(o, o, spread(k.stat[:, 16 + 4 * i:20 + 4 * i], P), ALU.mult))
                pool.wait_ge(k.A.free, self.stored_a(hf, "gate", i))
                pool.tensor_tensor(o, o, self.b[4 + i], ALU.mult).then_inc(self.gatedz, 1)
        self.memory.load(pool, k.A.free, k.A.stored(self.a0 + self.A_JOBS))

    def square(self, pool, n, x):
        if n >= 2:
            pool.wait_ge(self.ssum, n - 1)
        pool.tensor_tensor(self.sqr[:, n % 2, :], x, x, ALU.mult).then_inc(self.squares, 1)

    def pool_setup(self, pool, hf, c, part):
        k, n, b = self.k, 4 * hf + c, self.buffers(c)
        heads = slice(4 * hf, 4 * hf + 4)
        if part == 0:
            if c == 0:
                pool.wait_ge(self.ssum, 12 * hf + 8)
                pool.wait_ge(self.silu, 12 * hf + 12)
                pool.wait_ge(k.R.full, self.R(hf, "turned", 11) + 1)
            if hf or c > 1:
                pool.wait_ge(self.done, max(n - 1, 4 * hf))
            g = spread(self.g[:, c, heads], P)
            pool.tensor_tensor(b[0], over_heads(k.c("upper")), g, ALU.mult).then_inc(self.seg, 1)
            pool.tensor_tensor(b[1], over_heads(k.c("slower")), g, ALU.mult).then_inc(self.seg, 1)
            k.plink(pool.tensor_tensor(b[7], over_heads(k.c("slower")), spread(self.beta[:, c, heads], P), ALU.mult))
        elif part == 1:
            pool.wait_ge(k.A.free, self.stored_a(hf, "growth", c))
            pool.tensor_tensor(b[0], b[2], b[7], ALU.mult).then_inc(self.dmask, 1)
            pool.tensor_tensor(b[2], b[2], over_heads(k.c("lower")), ALU.mult).then_inc(self.dmask, 1)

    def pool_level(self, pool, hf, c, l, step):
        k, b = self.k, self.buffers(c)
        if step == 0:
            if l == 1:
                pool.wait_ge(k.A.free, self.stored_a(hf, "qk'", c))
            else:
                pool.wait_ge(k.A.full, self.A(hf, "LT", c, l - 1, 1) + 1)
            m = k.c("belowT")[:, (l - 1) * P:l * P]
            pool.tensor_tensor(b[2], b[1], over_heads(m), ALU.mult).then_inc(self.lmask, 1)

    def pool_scan(self, pool, hf, c, part):
        n, b = 4 * hf + c, self.buffers(c)
        if part == 0 and c < NT - 1:
            pool.wait_ge(self.lmask, 6 * n + 6)
            kt = self.ktok[:, c, :].rearrange("p (h d) -> p h d", h=4)
            pool.tensor_tensor(b[1], kt, spread(self.egl[:, c, slice(4 * hf, 4 * hf + 4)], P),
                               ALU.mult).then_inc(self.kd, 1)


def stages(k, which):
    out = []
    for name in which:
        if name == "xa0" or name == "xa1":
            st = CrossAttention(k, int(name[-1]))
        elif name == "moe0" or name == "moe1":
            st = Moe(k, int(name[-1]))
        elif name == "even":
            st = Even(k)
        elif name == "odd":
            st = Odd(k)
        else:
            st = Store(k)
        out.append(st)
    return out


STAGES = ("even", "xa0", "moe0", "odd", "xa1", "moe1", "store")


def build_program(nc, dram, consts, small, which=STAGES):
    with ExitStack() as ctx:
        k = Core(nc, ctx, dram, consts, small)
        k.stat = ctx.enter_context(nc.sbuf_tensor("stat", [P, 64], F32))[:, :]
        k.npass = ctx.enter_context(nc.sbuf_tensor("npass", [P, 2], I32))[:, :]
        k.decays = ctx.enter_context(nc.sbuf_tensor("decays", [P, 128], F32))[:, :]
        k.dlink = k.alink = k.plink = None
        plan = stages(k, which)
        a = r = w = 0
        for st in plan:
            st.a0, st.r0, st.w0 = a, r, w
            a, r, w = a + st.A_JOBS, r + st.R_JOBS, w + st.W_BLOCKS
        rows, ready = k.sem("x_loaded"), k.sem("constants_loaded")
        dchain, achain, pchain = k.sem("dve_chain"), k.sem("act_chain"), k.sem("pool_chain")
        block = ctx.enter_context(nc.Block())

        def between(eng, n):
            eng.drain().then_inc(k.stage_ends, 1)
            eng.wait_ge(k.stage_ends, 4 * n)

        @block.sync
        def _(sp):
            sp.dma_start(k.h, dram["x"][0].rearrange("(i p) d -> p i d", p=P)).then_inc(rows, 16)
            sp.dma_start(k.smallbuf[:, :], dram["small"]).then_inc(ready, 16)
            sp.dma_start(k.constbuf[:, :], dram["consts"]).then_inc(ready, 16)
            for st in plan:
                st.sp(sp)

        @block.gpsimd
        def _(pool):
            k.plink = Links(pool, pchain)
            pool.wait_ge(ready, 32)
            for n, st in enumerate(plan):
                if n:
                    between(pool, n)
                st.pool(pool)

        @block.tensor
        def _(pe):
            pe.sem_inc(k.W.free, WSLOTS)
            pe.wait_ge(ready, 32)
            for n, st in enumerate(plan):
                assert k.W.taken == st.w0, (n, k.W.taken, st.w0)
                if n:
                    between(pe, n)
                assert (k.A.filled, k.R.filled) == (st.a0, st.r0), (n, k.A.filled, st.a0, k.R.filled, st.r0)
                st.pe(pe)

        @block.scalar
        def _(act):
            k.alink = Links(act, achain)
            act.sem_inc(k.A.free, len(k.A.banks))
            act.wait_ge(rows, 16)
            for n, st in enumerate(plan):
                if n:
                    between(act, n)
                assert k.A.emptied == st.a0, (n, k.A.emptied, st.a0)
                st.act(act)
                if isinstance(st, (Even, Odd, CrossAttention)) and isinstance(plan[n + 1], (CrossAttention, Moe)):
                    end = st.r0 + st.R_JOBS
                    memory = 0 if isinstance(st, CrossAttention) else MemoryRows.R_JOBS
                    plan[n + 1].norm.early(act, lambda i: k.R.stored(end - 6 + 2 * i - (memory if i < 2 else 0)))

        @block.vector
        def _(dve):
            k.dlink = Links(dve, dchain)
            dve.sem_inc(k.R.free, len(k.R.banks))
            for name in ("pair", "more0", "more1"):
                if f"{name}_sc_added" in k.sems:
                    dve.sem_inc(k.sem(f"{name}_sc_added"), 2)
            dve.wait_ge(rows, 16)
            dve.wait_ge(ready, 32)
            for n, st in enumerate(plan):
                if n:
                    between(dve, n)
                assert k.R.emptied == st.r0, (n, k.R.emptied, st.r0)
                st.dve(dve)


WHICH = STAGES
BIG = ("x", "mem", "xa_wq", "xa_wk", "xa_wv", "xa_wo", "moe_w_gate", "moe_w_up", "moe_w_down", "ev_w_in",
       "ev_w_out", "od_w_in", "od_w_out")


def kernel(**inputs):
    import concourse.bacc as bacc
    from concourse.bass_utils import run_bass_kernel_spmd as run

    nc = bacc.Bacc("TRN2", target_bir_lowering=False, num_devices=1)
    consts, small = constant_columns(), small_columns(inputs)
    arrays = {name: np.ascontiguousarray(inputs[name]) for name in BIG}
    arrays["consts"], arrays["small"] = consts[0], small[0]
    arrays["final_gain"] = np.ascontiguousarray(on_every_row(inputs["final_norm"]))
    dram = {name: nc.dram_tensor(f"in_{name}", a.shape, mybir.dt.from_np(a.dtype), kind="ExternalInput").ap()
            for name, a in arrays.items()}
    dram["out"] = nc.dram_tensor("out", (1, SEQ, D), F32, kind="ExternalOutput").ap()
    build_program(nc, dram, consts, small, WHICH)
    r = run(nc, [{f"in_{name}": a for name, a in arrays.items()}], core_ids=[0])
    return r.results[0]["out"]
```
